# Optimizing a Trainium2 kernel written in Bass

```python
import jax, jax.numpy as jnp
from jax import lax
import numpy as np

D_MODEL = 1024
BATCH = 1
SEQ = 1024
DEPTH = 2

N_MIXERS = 2
NSA_HEADS = 16
NSA_KV_GROUPS = 4
NSA_HEAD_DIM = D_MODEL // NSA_HEADS
NSA_HPG = NSA_HEADS // NSA_KV_GROUPS
NSA_KV_W = NSA_KV_GROUPS * NSA_HEAD_DIM
N_BRANCH = 3
CMP_LEN = 32
CMP_STRIDE = 16
CMP_HIDDEN = NSA_HEAD_DIM
SLC_LEN = 64
SLC_TOPN = 8
WINDOW = 512
Q_BLOCK = 128
FORCE_SCORE = 1.0e4
NEG_BIG = -1.0e30
NSA_SPLITS = [NSA_HEADS * NSA_HEAD_DIM + k * NSA_KV_W for k in range(0, 7)]
NSA_IN_W = NSA_HEADS * NSA_HEAD_DIM + 6 * NSA_KV_W + N_BRANCH * NSA_HEADS
SG_WIDTH = 2 * D_MODEL
SG_GROUPS = 16
SG_GROUP_W = SG_WIDTH // SG_GROUPS
SG_CHUNK = 128
FFN_HIDDEN = 2816
CONV_W = 3
EPS = 1e-6
N_NSA_LAYERS = (DEPTH + 1) // 2
N_SG_LAYERS = DEPTH // 2

kernel_name = "nsa_gmlp_interleaved_convffn_trunk"

def rmsnorm(x, g):
    xf = x.astype(jnp.float32)
    y = xf * lax.rsqrt(jnp.mean(xf * xf, axis=-1, keepdims=True) + EPS)
    return (y * g.astype(jnp.float32)).astype(x.dtype)

def layernorm(x, g, b):
    xf = x.astype(jnp.float32)
    mu = jnp.mean(xf, axis=-1, keepdims=True)
    var = jnp.mean(jnp.square(xf - mu), axis=-1, keepdims=True)
    y = (xf - mu) * lax.rsqrt(var + EPS)
    return (y * g.astype(jnp.float32) + b.astype(jnp.float32)).astype(x.dtype)

def masked_softmax(s, mask):
    s = jnp.where(mask, s.astype(jnp.float32), NEG_BIG)
    m = jnp.max(s, axis=-1, keepdims=True)
    e = jnp.where(mask, jnp.exp(s - m), 0.0)
    den = jnp.sum(e, axis=-1, keepdims=True)
    return e / jnp.maximum(den, 1e-30)

def compress_blocks(k, pe, w1, w2):
    T = k.shape[1]
    n_cmp = (T - CMP_LEN) // CMP_STRIDE + 1
    idx = np.arange(n_cmp)[:, None] * CMP_STRIDE + np.arange(CMP_LEN)[None, :]
    kb = k[:, idx] + pe[None, None, :, None, :]
    kb = jnp.transpose(kb, (0, 1, 3, 2, 4)).reshape(k.shape[0], n_cmp, NSA_KV_GROUPS, CMP_LEN * NSA_HEAD_DIM)
    h = jax.nn.gelu(jnp.einsum('bngf,fh->bngh', kb, w1))
    return jnp.einsum('bngh,hd->bngd', h, w2)

def cmp_to_slc_weights(n_cmp, n_slc):
    cs = np.arange(n_cmp)[:, None] * CMP_STRIDE
    ss = np.arange(n_slc)[None, :] * SLC_LEN
    ov = np.clip(np.minimum(cs + CMP_LEN, ss + SLC_LEN) - np.maximum(cs, ss), 0, None)
    return jnp.asarray(ov.astype(np.float32) / np.float32(CMP_LEN))

def nsa_mixer(x, w_in, cmp_pe, cmp_w1, cmp_w2, w_out):
    B, T, _ = x.shape
    G, HPG, DH = NSA_KV_GROUPS, NSA_HPG, NSA_HEAD_DIM
    scale = DH ** -0.5
    proj = x @ w_in
    q, kc, vc, ks, vs, kw, vw, gl = jnp.split(proj, NSA_SPLITS, axis=-1)
    q = q.reshape(B, T, G, HPG, DH)
    kc, vc, ks, vs, kw, vw = [a.reshape(B, T, G, DH) for a in (kc, vc, ks, vs, kw, vw)]
    gates = jax.nn.sigmoid(gl.astype(jnp.float32)).reshape(B, T, G, HPG, N_BRANCH)
    t = jnp.arange(T)

    kcmp = compress_blocks(kc, cmp_pe[0], cmp_w1[0], cmp_w2[0])
    vcmp = compress_blocks(vc, cmp_pe[1], cmp_w1[1], cmp_w2[1])
    n_cmp = kcmp.shape[1]
    cmp_end = jnp.arange(n_cmp) * CMP_STRIDE + CMP_LEN - 1
    cmp_mask = cmp_end[None, :] <= t[:, None]
    s_cmp = jnp.einsum('btghd,bngd->bghtn', q, kcmp) * scale
    p_cmp = masked_softmax(s_cmp, cmp_mask)
    o_cmp = jnp.einsum('bghtn,bngd->btghd', p_cmp.astype(vcmp.dtype), vcmp)

    n_slc = T // SLC_LEN
    imp = jnp.einsum('bghtn,nj->bgtj', p_cmp, cmp_to_slc_weights(n_cmp, n_slc))
    j = jnp.arange(n_slc)[None, :]
    blk = (t // SLC_LEN)[:, None]
    valid = j <= blk
    forced = (j == 0) | (j == blk) | (j == blk - 1)
    score = jnp.where(valid, imp + jnp.where(forced, FORCE_SCORE, 0.0), -FORCE_SCORE)
    n_sel = min(SLC_TOPN, n_slc)
    _, sel = lax.top_k(score, n_sel)

    ks_blocks = jnp.transpose(ks.reshape(B, n_slc, SLC_LEN, G, DH), (0, 3, 1, 2, 4))
    vs_blocks = jnp.transpose(vs.reshape(B, n_slc, SLC_LEN, G, DH), (0, 3, 1, 2, 4))
    kw_pad = jnp.pad(kw, ((0, 0), (WINDOW, 0), (0, 0), (0, 0)))
    vw_pad = jnp.pad(vw, ((0, 0), (WINDOW, 0), (0, 0), (0, 0)))
    gather = jax.vmap(jax.vmap(lambda blocks, ix: blocks[ix]))

    def block_fn(qb):
        s0 = qb * Q_BLOCK
        tq = s0 + jnp.arange(Q_BLOCK)
        qblk = lax.dynamic_slice_in_dim(q, s0, Q_BLOCK, axis=1)
        sel_b = lax.dynamic_slice_in_dim(sel, s0, Q_BLOCK, axis=2)
        kg = gather(ks_blocks, sel_b).reshape(B, G, Q_BLOCK, n_sel * SLC_LEN, DH)
        vg = gather(vs_blocks, sel_b).reshape(B, G, Q_BLOCK, n_sel * SLC_LEN, DH)
        kpos = (sel_b[..., None] * SLC_LEN + jnp.arange(SLC_LEN)).reshape(B, G, Q_BLOCK, n_sel * SLC_LEN)
        smask = (kpos <= tq[None, None, :, None])[:, :, None]
        s_s = jnp.einsum('bqghd,bgqkd->bghqk', qblk, kg) * scale
        p_s = masked_softmax(s_s, smask).astype(vg.dtype)
        o_s = jnp.einsum('bghqk,bgqkd->bqghd', p_s, vg)
        kwin = lax.dynamic_slice_in_dim(kw_pad, s0, WINDOW + Q_BLOCK, axis=1)
        vwin = lax.dynamic_slice_in_dim(vw_pad, s0, WINDOW + Q_BLOCK, axis=1)
        wpos = s0 - WINDOW + jnp.arange(WINDOW + Q_BLOCK)
        wmask = (wpos[None, :] <= tq[:, None]) & (wpos[None, :] > tq[:, None] - WINDOW) & (wpos[None, :] >= 0)
        s_w = jnp.einsum('bqghd,bkgd->bghqk', qblk, kwin) * scale
        p_w = masked_softmax(s_w, wmask).astype(vwin.dtype)
        o_w = jnp.einsum('bghqk,bkgd->bqghd', p_w, vwin)
        return o_s, o_w

    o_slc, o_win = lax.map(block_fn, jnp.arange(T // Q_BLOCK))
    o_slc = jnp.moveaxis(o_slc, 0, 1).reshape(B, T, G, HPG, DH)
    o_win = jnp.moveaxis(o_win, 0, 1).reshape(B, T, G, HPG, DH)

    o = (gates[..., 0:1] * o_cmp + gates[..., 1:2] * o_slc + gates[..., 2:3] * o_win).astype(x.dtype)
    return o.reshape(B, T, NSA_HEADS * DH) @ w_out

def sg_mixer(x, w_in, ln_g, ln_b, w_sp, b_sp, w_out):
    B, T, _ = x.shape
    z = jax.nn.gelu(x @ w_in)
    u, v = jnp.split(z, 2, axis=-1)
    v = layernorm(v, ln_g, ln_b)
    nc = T // SG_CHUNK
    v = v.reshape(B, nc, SG_CHUNK, SG_GROUPS, SG_GROUP_W)
    causal = jnp.tril(jnp.ones((SG_CHUNK, SG_CHUNK), dtype=bool))
    w = jnp.where(causal[None], w_sp, 0.0).astype(v.dtype)
    mixed = jnp.einsum('gts,bnsgf->bntgf', w, v) + b_sp.T[None, None, :, :, None]
    return (u * mixed.reshape(B, T, SG_WIDTH)) @ w_out

def conv_ffn(x, w_up, conv_w, conv_b, w_down):
    h = x @ w_up
    C = h.shape[-1]
    h = lax.conv_general_dilated(
        h, conv_w.reshape(CONV_W, 1, C).astype(h.dtype), window_strides=(1,),
        padding=[(CONV_W - 1, 0)], dimension_numbers=('NWC', 'WIO', 'NWC'),
        feature_group_count=C) + conv_b
    g, val = jnp.split(h, 2, axis=-1)
    return (jax.nn.silu(g) * val) @ w_down

def setup_inputs(seed: int = 0) -> dict:
    key = jax.random.key(seed)
    ks = jax.random.split(key, 18)
    nrm = jax.random.normal
    f32 = jnp.float32
    D, E, F, DH = D_MODEL, SG_WIDTH, FFN_HIDDEN, NSA_HEAD_DIM
    return {
        "x": nrm(ks[0], (BATCH, SEQ, D), f32),
        "norm_gains": 1.0 + 0.02 * nrm(ks[1], (DEPTH, 4, D), f32),
        "nsa_w_in": nrm(ks[2], (N_NSA_LAYERS, D, NSA_IN_W), f32) * D ** -0.5,
        "nsa_cmp_pe": 0.1 * nrm(ks[3], (N_NSA_LAYERS, 2, CMP_LEN, DH), f32),
        "nsa_cmp_w1": nrm(ks[4], (N_NSA_LAYERS, 2, CMP_LEN * DH, CMP_HIDDEN), f32) * (CMP_LEN * DH) ** -0.5,
        "nsa_cmp_w2": nrm(ks[5], (N_NSA_LAYERS, 2, CMP_HIDDEN, DH), f32) * CMP_HIDDEN ** -0.5,
        "nsa_w_out": nrm(ks[6], (N_NSA_LAYERS, NSA_HEADS * DH, D), f32) * (NSA_HEADS * DH) ** -0.5,
        "sg_w_in": nrm(ks[7], (N_SG_LAYERS, D, 2 * E), f32) * D ** -0.5,
        "sg_ln_g": 1.0 + 0.02 * nrm(ks[8], (N_SG_LAYERS, E), f32),
        "sg_ln_b": 0.02 * nrm(ks[9], (N_SG_LAYERS, E), f32),
        "sg_w_sp": nrm(ks[10], (N_SG_LAYERS, SG_GROUPS, SG_CHUNK, SG_CHUNK), f32) * SG_CHUNK ** -0.5,
        "sg_b_sp": 1.0 + 0.02 * nrm(ks[11], (N_SG_LAYERS, SG_GROUPS, SG_CHUNK), f32),
        "sg_w_out": nrm(ks[12], (N_SG_LAYERS, E, D), f32) * E ** -0.5,
        "ffn_w_up": nrm(ks[13], (DEPTH, D, 2 * F), f32) * D ** -0.5,
        "ffn_conv_w": nrm(ks[14], (DEPTH, CONV_W, 2 * F), f32) * CONV_W ** -0.5,
        "ffn_conv_b": 0.02 * nrm(ks[15], (DEPTH, 2 * F), f32),
        "ffn_w_down": nrm(ks[16], (DEPTH, F, D), f32) * F ** -0.5,
    }

def reference(x, norm_gains, nsa_w_in, nsa_cmp_pe, nsa_cmp_w1, nsa_cmp_w2, nsa_w_out,
              sg_w_in, sg_ln_g, sg_ln_b, sg_w_sp, sg_b_sp, sg_w_out,
              ffn_w_up, ffn_conv_w, ffn_conv_b, ffn_w_down):
    for i in range(DEPTH):
        g = norm_gains[i]
        slot = i // N_MIXERS
        h = rmsnorm(x, g[0])
        if i % N_MIXERS == 0:
            m = nsa_mixer(h, nsa_w_in[slot], nsa_cmp_pe[slot], nsa_cmp_w1[slot],
                          nsa_cmp_w2[slot], nsa_w_out[slot])
        else:
            m = sg_mixer(h, sg_w_in[slot], sg_ln_g[slot], sg_ln_b[slot],
                         sg_w_sp[slot], sg_b_sp[slot], sg_w_out[slot])
        x = x + rmsnorm(m, g[1])
        h = rmsnorm(x, g[2])
        x = x + rmsnorm(conv_ffn(h, ffn_w_up[i], ffn_conv_w[i], ffn_conv_b[i], ffn_w_down[i]), g[3])
    return x


_drawn_inputs = setup_inputs


def setup_inputs(seed=0):
    import zlib

    import numpy as np

    out = dict(_drawn_inputs(seed))
    spreads = {}
    factors = {}
    for name, (base, spread) in spreads.items():
        noise = np.random.default_rng([zlib.crc32(name.encode()), seed]).standard_normal(out[name].shape)
        drawn = base * np.exp(spread * noise) if base else spread * noise
        out[name] = __import__('jax').numpy.asarray(drawn.astype(out[name].dtype))
    for name, factor in factors.items():
        out[name] = (out[name] * factor).astype(out[name].dtype)
    return out
```

```python
from contextlib import ExitStack

import concourse.bass as bass
from concourse import mybir

ALU = mybir.AluOpType
ACT = mybir.ActivationFunctionType
AX = mybir.AxisListType
F32 = mybir.dt.float32
F32R = mybir.dt.float32r
BF16 = mybir.dt.bfloat16

P = 128
D = 1024
T = 1024
NT = T // P
KD = D // P
HALF = 512
EPS = 1e-6
HEADS, GROUPS, DH = 16, 4, 64
HPG = HEADS // GROUPS
SCALE = DH ** -0.5
CMP_LEN, CMP_STRIDE = 32, 16
NCMP = (T - CMP_LEN) // CMP_STRIDE + 1
SLC_LEN, TOPN, WINDOW = 64, 8, 512
NSLC = T // SLC_LEN
FORCE, NEG = 1.0e4, -1.0e30
GATES = 3 * HEADS
KVW = GROUPS * DH
F = 2816
KF = F // P
E = 2 * D
KE = E // P
FM_TILES = (HEADS * DH + 4 * KVW) // P
BASE = 16640

CONST_AT, H_AT, Y_AT, WORK = 0, 4, 68, 100
GMLP_AT = 182


class Chip:

    def __init__(self, nc, ctx):
        self.nc, self.tensors, self.in_stage = nc, {}, []
        self.banks = ctx.enter_context(nc.psum_tensor("banks", [P, 8, HALF], F32))
        self.ident = self.at("ident", CONST_AT, [P, P])
        self.ident_bf = self.at("ident_bf", CONST_AT + 0.5, [P, P], BF16)
        self.causal = self.at("causal", CONST_AT + 0.75, [P, P], BF16)
        self.too_old = self.at("too_old", CONST_AT + 1.0, [P, P], BF16)
        self.eps = self.at("eps", CONST_AT + 1.25, [P, 1])
        self.gates = self.at("gates", CONST_AT + 1.5, [P, NT, GATES])
        self.hT = [self.at(n, H_AT + 32 * j, [P, KD, T], F32R) for j, n in enumerate(("hT_hi", "hT_lo"))]
        self.y = self.at("y", Y_AT, [P, NT, D])
        self.w_spT = self.at("w_spT", GMLP_AT, [P, KE, P])
        self.sg_bias = self.at("sg_bias", GMLP_AT + 8, [P, KE, P])

    def semaphore(self, name):
        self.in_stage.append(self.nc.alloc_semaphore(name=name))
        return self.in_stage[-1]

    def end_stage(self):
        self.nc.clear_and_free_semaphores(self.in_stage)
        self.nc.all_engine_barrier()
        self.in_stage = []

    def at(self, name, kb, shape, dt=F32):
        if name not in self.tensors:
            self.tensors[name] = self.nc.alloc_sbuf_tensor_at(name, shape, dt, offset=BASE + int(kb * 1024))
        return self.tensors[name]


def pair(ap):
    return ap.rearrange("p a c -> p (a c)")


def constants_stage(nc, chip, ctx):
    filled, cut = (chip.semaphore(f"const_{n}") for n in ("filled", "cut"))
    block = ctx.enter_context(nc.Block())

    @block.gpsimd
    def _(pool):
        nc.gpsimd.memset(chip.eps[:], EPS)
        for m in (chip.ident, chip.ident_bf, chip.causal, chip.too_old):
            nc.gpsimd.memset(m[:], 0.0).then_inc(filled, 1)
        pool.wait_ge(filled, 4)
        for m in (chip.ident, chip.ident_bf):
            nc.gpsimd.affine_select(out=m[:], in_=m[:], compare_op=ALU.not_equal, fill=1.0, base=0,
                                    pattern=[[-1, P]], channel_multiplier=1).then_inc(cut, 1)
        nc.gpsimd.affine_select(out=chip.causal[:], in_=chip.causal[:], compare_op=ALU.is_ge, fill=NEG, base=0,
                                pattern=[[-1, P]], channel_multiplier=1).then_inc(cut, 1)
        nc.gpsimd.affine_select(out=chip.too_old[:], in_=chip.too_old[:], compare_op=ALU.is_gt, fill=NEG, base=0,
                                pattern=[[1, P]], channel_multiplier=-1).then_inc(cut, 1)
        pool.wait_ge(cut, 4)


def norm_stage(nc, chip, ctx, tag, x_in, x_out=None, post_gain=None, pre_gain=None):
    sem = lambda n: chip.semaphore(f"{tag}_{n}")
    x_loaded, gains_loaded, x_stored = sem("x_loaded"), sem("gains_loaded"), sem("x_stored")
    y_squared, y_root, y_inverse, y_normed = sem("y_squared"), sem("y_root"), sem("y_inverse"), sem("y_normed")
    x_new, x_squared, x_root, x_inverse = sem("x_new"), sem("x_squared"), sem("x_root"), sem("x_inverse")
    x_normed, turned, hi_done, lo_done = sem("x_normed"), sem("turned"), sem("hi_done"), sem("lo_done")
    y, (hT_hi, hT_lo), banks = chip.y, chip.hT, chip.banks
    x = chip.at("norm_x", WORK, [P, NT, D])
    g_post = chip.at("norm_g_post", WORK + 32, [P, D])
    g_pre = chip.at("norm_g_pre", WORK + 36, [P, D])
    junk = chip.at("norm_junk", WORK + 40, [P, D])
    stats = chip.at("norm_stats", WORK + 44, [P, 6, NT])
    y_sum, y_rms, y_inv, x_sum, x_rms, x_inv = (stats[:, j, :] for j in range(6))
    gains = 16 * ((post_gain is not None) + (pre_gain is not None))
    block = ctx.enter_context(nc.Block())

    @block.sync
    def _(sp):
        sp.dma_start(x[:], x_in.rearrange("(n p) d -> p n d", p=P)).then_inc(x_loaded, 16)
        if post_gain is not None:
            sp.dma_start(g_post[:], post_gain.broadcast_to([P, D])).then_inc(gains_loaded, 16)
        if pre_gain is not None:
            sp.dma_start(g_pre[:], pre_gain.broadcast_to([P, D])).then_inc(gains_loaded, 16)
        if x_out is not None:
            for n in range(NT):
                sp.wait_ge(x_new, n + 1)
                sp.dma_start(x_out[n * P:(n + 1) * P, :], x[:, n, :]).then_inc(x_stored, 16)
            sp.wait_ge(x_stored, 16 * NT)

    @block.scalar
    def _(act):
        if post_gain is not None:
            for n in range(NT):
                nc.scalar.activation(junk[:], y[:, n, :], ACT.Square, accum_out=y_sum[:, n:n + 1]).then_inc(y_squared, 1)
                act.wait_ge(y_squared, n + 1)
            nc.scalar.activation(y_rms, y_sum, ACT.Sqrt, bias=chip.eps[:, 0:1], scale=1.0 / D).then_inc(y_root, 1)
        if pre_gain is not None:
            act.wait_ge(x_loaded, 16)
            for n in range(NT):
                if post_gain is not None:
                    act.wait_ge(x_new, n + 1)
                nc.scalar.activation(junk[:], x[:, n, :], ACT.Square, accum_out=x_sum[:, n:n + 1]).then_inc(x_squared, 1)
                act.wait_ge(x_squared, n + 1)
            nc.scalar.activation(x_rms, x_sum, ACT.Sqrt, bias=chip.eps[:, 0:1], scale=1.0 / D).then_inc(x_root, 1)
            for n in range(NT):
                act.wait_ge(turned, n + 1)
                b = 2 * (n % 2)
                nc.scalar.activation(hT_hi[:, :, n * P:(n + 1) * P],
                                     banks[:, b:b + 2, :].rearrange("p a (k t) -> p (a k) t", t=P),
                                     ACT.Copy).then_inc(hi_done, 1)

    @block.gpsimd
    def _(pool):
        if post_gain is not None:
            pool.wait_ge(x_loaded, 16)
            for n in range(NT):
                pool.wait_ge(y_normed, n + 1)
                nc.gpsimd.tensor_tensor(x[:, n, :], x[:, n, :], y[:, n, :], ALU.add).then_inc(x_new, 1)

    @block.vector
    def _(dve):
        dve.wait_ge(gains_loaded, gains)
        if post_gain is not None:
            dve.wait_ge(y_root, 1)
            nc.vector.reciprocal(y_inv, y_rms).then_inc(y_inverse, 1)
            dve.wait_ge(y_inverse, 1)
            for n in range(NT):
                nc.vector.scalar_tensor_tensor(out=y[:, n, :], in0=y[:, n, :], scalar=y_inv[:, n:n + 1], in1=g_post[:],
                                               op0=ALU.mult, op1=ALU.mult).then_inc(y_normed, 1)
        if pre_gain is None:
            return
        dve.wait_ge(x_root, 1)
        nc.vector.reciprocal(x_inv, x_rms).then_inc(x_inverse, 1)
        dve.wait_ge(x_inverse, 1)

        def low_part(n):
            dve.wait_ge(hi_done, n + 1)
            b = 2 * (n % 2)
            nc.vector.tensor_tensor(hT_lo[:, :, n * P:(n + 1) * P],
                                    banks[:, b:b + 2, :].rearrange("p a (k t) -> p (a k) t", t=P),
                                    hT_hi[:, :, n * P:(n + 1) * P].bitcast(F32), ALU.subtract).then_inc(lo_done, 1)

        for n in range(NT):
            nc.vector.scalar_tensor_tensor(out=y[:, n, :], in0=x[:, n, :], scalar=x_inv[:, n:n + 1], in1=g_pre[:],
                                           op0=ALU.mult, op1=ALU.mult).then_inc(x_normed, 1)
            if n >= 1:
                low_part(n - 1)
        low_part(NT - 1)

    @block.tensor
    def _(pe):
        if pre_gain is None:
            return
        for n in range(NT):
            pe.wait_ge(x_normed, n + 1)
            if n >= 2:
                pe.wait_ge(lo_done, n - 1)
            for k in range(KD):
                last = nc.tensor.transpose(banks[:, 2 * (n % 2) + k // 4, (k % 4) * P:(k % 4 + 1) * P],
                                           y[:, n, k * P:(k + 1) * P], chip.ident[:])
            last.then_inc(turned, 1)


def feature_major_product(nc, chip, first_bank, w_hi, w_lo):
    hT_hi, hT_lo = chip.hT
    for k in range(KD):
        for j, (w, h) in enumerate(((w_hi, hT_hi), (w_hi, hT_lo), (w_lo, hT_hi))):
            for half in range(2):
                last = nc.tensor.matmul(chip.banks[:, first_bank + half, :], w[:, k, :],
                                        h[:, k, half * HALF:(half + 1) * HALF],
                                        start=(k == 0 and j == 0), stop=(k == KD - 1 and j == 2))
    return last


def ffn_stage(nc, chip, ctx, tag, w_up, w_down, conv):
    sem = lambda n: chip.semaphore(f"{tag}_{n}")
    ROUNDS = KF // 2
    up_loaded = [sem(f"up_loaded_{c}") for c in "ab"]
    down_loaded, conv_loaded = sem("down_loaded"), sem("conv_loaded")
    up_w_hi, up_w_ready = sem("up_w_hi"), sem("up_w_ready")
    down_w_hi, down_w_ready = sem("down_w_hi"), sem("down_w_ready")
    up_done = [sem(f"up_done_{c}") for c in "gv"]
    centre = [sem(f"centre_{c}") for c in "gv"]
    cur_ready = sem("cur_ready")
    conv_step, gated_ready, prod_ready = sem("conv_step"), sem("gated_ready"), sem("prod_ready")
    conv_done = [sem(f"conv_done_{c}") for c in "gv"]
    prod_hi, prod_split = sem("prod_hi"), sem("prod_split")
    down_done, y_free = sem("down_done"), sem("y_free")

    raw_up = [chip.at(f"ffn_raw_up{c}", WORK + 8 * j, [P, 2, KD, P]) for j, c in enumerate("ab")]
    raw_down = chip.at(f"ffn_raw_down", WORK + 16, [P, 2, D])
    up_hi = [chip.at(f"ffn_up_hi{c}", WORK + 24 + 16 * j, [P, 2, KD, P], F32R) for j, c in enumerate("ab")]
    up_lo = [chip.at(f"ffn_up_lo{c}", WORK + 32 + 16 * j, [P, 2, KD, P], F32R) for j, c in enumerate("ab")]
    down_hi = chip.at(f"ffn_down_hi", WORK + 56, [P, 2, D], F32R)
    down_lo = chip.at(f"ffn_down_lo", WORK + 64, [P, 2, D], F32R)
    p_hi = [chip.at(f"ffn_p_hi{c}", WORK + 72 + 8 * j, [P, T], F32R) for j, c in enumerate("ab")]
    p_lo = [chip.at(f"ffn_p_lo{c}", WORK + 76 + 8 * j, [P, T], F32R) for j, c in enumerate("ab")]
    cg = [chip.at(f"ffn_conv_{c}", WORK + 88 + 4 * j, [P, T]) for j, c in enumerate("gv")]
    prod = chip.at(f"ffn_prod", WORK + 96, [P, T])
    cw = chip.at(f"ffn_cw", WORK + 100, [P, KF, 2, 4])
    cur = [chip.at(f"ffn_cur{j}", WORK + 101 + 0.125 * j, [P, 2, 4]) for j in range(2)]
    banks, y = chip.banks, chip.y
    up_bank = [banks[:, 0:2, :], banks[:, 2:4, :]]
    block = ctx.enter_context(nc.Block())

    @block.sync
    def _(sp):
        def load_up(c, n, wait=None):
            if wait is not None:
                sp.wait_ge(up_w_ready, wait)
            sp.dma_start(raw_up[c][:], w_up[n].rearrange("p (s k c) -> p s k c", s=2, k=KD)).then_inc(up_loaded[c], 16)

        def load_down(i, wait=None):
            if wait is not None:
                sp.wait_ge(down_w_ready, wait)
            sp.dma_start(raw_down[:], w_down[i].rearrange("p (s n) -> p s n", s=2)).then_inc(down_loaded, 16)

        load_up(0, 0)
        sp.dma_start(cw[:], conv).then_inc(conv_loaded, 16)
        load_up(1, 1)
        load_down(0)
        with sp.Fori(0, ROUNDS - 1) as i:
            load_up(0, i * 2 + 2, wait=i * 2 + 1)
            load_up(1, i * 2 + 3, wait=i * 2 + 2)
            load_down(i + 1, wait=i + 1)

    @block.scalar
    def _(act):
        def split_up(c, n, wait=None):
            act.wait_ge(up_loaded[c], (n - c) * 8 + 16)
            if wait is not None:
                act.wait_ge(up_done[1], wait)
            nc.scalar.activation(up_hi[c][:], raw_up[c][:], ACT.Copy).then_inc(up_w_hi, 1)

        def split_down(i, wait=None):
            act.wait_ge(down_loaded, i * 16 + 16)
            if wait is not None:
                act.wait_ge(down_done, wait)
            nc.scalar.activation(down_hi[:], raw_down[:], ACT.Copy).then_inc(down_w_hi, 1)

        def convolved(c, n):
            for s in range(2):
                act.wait_ge(up_done[s], n + 1)
                if s == 1:
                    act.wait_ge(prod_ready, n)
                act.wait_ge(cur_ready, n + 1)
                nc.scalar.activation(cg[s][:], pair(up_bank[s]), ACT.Identity, bias=cur[c][:, s, 3:4],
                                     scale=cur[c][:, s, 2:3]).then_inc(centre[s], 1)
            act.wait_ge(conv_done[0], n + 1)
            act.wait_ge(prod_split, n)
            nc.scalar.activation(prod[:], cg[0][:], ACT.Silu).then_inc(gated_ready, 1)

        def product_hi(c, n, wait=None):
            act.wait_ge(prod_ready, n + 1)
            if wait is not None:
                act.wait_ge(down_done, wait)
            nc.scalar.activation(p_hi[c][:], prod[:], ACT.Copy).then_inc(prod_hi, 1)

        split_up(0, 0)
        split_up(1, 1)
        convolved(0, 0)
        product_hi(0, 0)
        split_down(0)
        with act.Fori(0, ROUNDS - 1) as i:
            split_up(0, i * 2 + 2, wait=i * 2 + 1)
            convolved(1, i * 2 + 1)
            product_hi(1, i * 2 + 1)
            split_up(1, i * 2 + 3, wait=i * 2 + 2)
            convolved(0, i * 2 + 2)
            product_hi(0, i * 2 + 2, wait=i * NT + NT)
            split_down(i + 1, wait=i * NT + NT)
        convolved(1, KF - 1)
        product_hi(1, KF - 1)


    @block.gpsimd
    def _(pool):
        def up_low(c, n):
            pool.wait_ge(up_w_hi, n + 1)
            nc.gpsimd.tensor_tensor(up_lo[c][:], raw_up[c][:], up_hi[c][:].bitcast(F32), ALU.subtract).then_inc(up_w_ready, 1)

        def down_low(i):
            pool.wait_ge(down_w_hi, i + 1)
            nc.gpsimd.tensor_tensor(down_lo[:], raw_down[:], down_hi[:].bitcast(F32), ALU.subtract).then_inc(down_w_ready, 1)

        def product_low(c, n):
            pool.wait_ge(prod_hi, n + 1)
            nc.gpsimd.tensor_tensor(p_lo[c][:], prod[:], p_hi[c][:].bitcast(F32), ALU.subtract).then_inc(prod_split, 1)

        up_low(0, 0)
        up_low(1, 1)
        product_low(0, 0)
        down_low(0)
        with pool.Fori(0, ROUNDS - 1) as i:
            up_low(0, i * 2 + 2)
            product_low(1, i * 2 + 1)
            up_low(1, i * 2 + 3)
            product_low(0, i * 2 + 2)
            down_low(i + 1)
        product_low(1, KF - 1)

    @block.vector
    def _(dve):
        def fetch_taps(c, n):
            nc.vector.tensor_copy(cur[c][:], cw[:, bass.ds(n, 1), :, :].rearrange("p a s j -> p (a s) j")).then_inc(cur_ready, 1)

        def convolve(c, n):
            dve.wait_ge(cur_ready, n + 1)
            for s in range(2):
                dve.wait_ge(centre[s], n + 1)
                h = pair(up_bank[s])
                nc.vector.scalar_tensor_tensor(out=cg[s][:, 1:T], in0=h[:, 0:T - 1], scalar=cur[c][:, s, 1:2],
                                               in1=cg[s][:, 1:T], op0=ALU.mult, op1=ALU.add).then_inc(conv_step, 1)
                dve.wait_ge(conv_step, n * 2 + (s + 1))
                nc.vector.scalar_tensor_tensor(out=cg[s][:, 2:T], in0=h[:, 0:T - 2], scalar=cur[c][:, s, 0:1],
                                               in1=cg[s][:, 2:T], op0=ALU.mult, op1=ALU.add).then_inc(conv_done[s], 1)
            dve.wait_ge(gated_ready, n + 1)
            dve.wait_ge(conv_done[1], n + 1)
            nc.vector.tensor_tensor(prod[:], prod[:], cg[1][:], ALU.mult).then_inc(prod_ready, 1)

        def add_down(i):
            for t in range(NT):
                dve.wait_ge(down_done, i * NT + (t + 1))
                b = 4 + 2 * (t % 2)
                nc.vector.tensor_tensor(y[:, t, :], y[:, t, :], pair(banks[:, b:b + 2, :]), ALU.add).then_inc(y_free, 1)

        dve.wait_ge(conv_loaded, 16)
        nc.vector.memset(y[:], 0.0).then_inc(y_free, 2)
        dve.wait_ge(y_free, 2)
        fetch_taps(0, 0)
        fetch_taps(1, 1)
        convolve(0, 0)
        with dve.Fori(0, ROUNDS - 1) as i:
            fetch_taps(0, i * 2 + 2)
            convolve(1, i * 2 + 1)
            fetch_taps(1, i * 2 + 3)
            convolve(0, i * 2 + 2)
            dve.wait_ge(y_free, i * NT + 2)
            add_down(i)
        convolve(1, KF - 1)
        dve.wait_ge(y_free, (ROUNDS - 1) * NT + 2)
        add_down(ROUNDS - 1)

    @block.tensor
    def _(pe):
        def up(c, n):
            pe.wait_ge(up_w_ready, n + 1)
            for s in range(2):
                pe.wait_ge(conv_done[s], n)
                feature_major_product(nc, chip, 2 * s, up_hi[c][:, s], up_lo[c][:, s]).then_inc(up_done[s], 1)

        up(0, 0)
        with pe.Fori(0, ROUNDS - 1) as i:
            up(1, i * 2 + 1)
            up(0, i * 2 + 2)
            down_product(nc, chip, pe, i, p_hi, p_lo, down_hi, down_lo, prod_split, down_w_ready, y_free, down_done)
        up(1, KF - 1)
        down_product(nc, chip, pe, ROUNDS - 1, p_hi, p_lo, down_hi, down_lo, prod_split, down_w_ready, y_free, down_done)


def down_product(nc, chip, pe, i, p_hi, p_lo, w_hi, w_lo, prod_split, w_ready, y_free, down_done):
    pe.wait_ge(w_ready, i + 1)
    pe.wait_ge(prod_split, i * 2 + 2)
    for t in range(NT):
        pe.wait_ge(y_free, i * NT + (t + 1))
        b = 4 + 2 * (t % 2)
        for c in range(2):
            for j, (p, w) in enumerate(((p_hi, w_hi), (p_hi, w_lo), (p_lo, w_hi))):
                for half in range(2):
                    last = nc.tensor.matmul(chip.banks[:, b + half, :], p[c][:, t * P:(t + 1) * P],
                                            w[:, c, half * HALF:(half + 1) * HALF],
                                            start=(c == 0 and j == 0), stop=(c == 1 and j == 2))
        last.then_inc(down_done, 1)


def gmlp_bias_stage(nc, chip, ctx, w_sp, b_sp, ln_b):
    sem = lambda n: chip.semaphore(f"bias_{n}")
    loaded, masked, ones_set, summed, sums_kept, spread, kept = (
        sem(n) for n in ("loaded", "masked", "ones_set", "summed", "sums_kept", "spread", "kept"))
    ones = chip.at("bias_ones", WORK, [P, P])
    rows = chip.at("bias_rows", WORK + 1, [1, 3, E])
    w_spT, bias = chip.w_spT, chip.sg_bias
    ln_row, sp_row, sum_row = (rows[0:1, j, :] for j in range(3))
    block = ctx.enter_context(nc.Block())

    @block.sync
    def _(sp):
        sp.dma_start(w_spT[:], w_sp.rearrange("s (g t) -> s g t", g=KE)).then_inc(loaded, 16)
        sp.dma_start(ln_row, ln_b).then_inc(loaded, 16)
        sp.dma_start(sp_row, b_sp).then_inc(loaded, 16)

    @block.gpsimd
    def _(pool):
        nc.gpsimd.memset(ones[:], 1.0).then_inc(ones_set, 1)
        pool.wait_ge(loaded, 48)
        nc.gpsimd.affine_select(out=w_spT[:], in_=w_spT[:], compare_op=ALU.is_ge, fill=0.0, base=0,
                                pattern=[[0, KE], [1, P]], channel_multiplier=-1).then_inc(masked, 1)

    @block.tensor
    def _(pe):
        pe.wait_ge(ones_set, 1)
        pe.wait_ge(masked, 1)
        for b in range(4):
            last = nc.tensor.matmul(chip.banks[0:1, b, :], ones[:, 0:1],
                                    w_spT[:, 4 * b:4 * b + 4, :].rearrange("s g t -> s (g t)"), start=True, stop=True)
        last.then_inc(summed, 1)
        pe.wait_ge(sums_kept, 1)
        for g in range(KE):
            at = chip.banks[:, 4 + g // 4, (g % 4) * P:(g % 4 + 1) * P]
            cols = slice(g * P, (g + 1) * P)
            nc.tensor.matmul(at, ln_row[:, cols], sum_row[:, cols], start=True, stop=False)
            last = nc.tensor.matmul(at, ones[0:1, :], sp_row[:, cols], start=False, stop=True)
        last.then_inc(spread, 1)

    @block.vector
    def _(dve):
        dve.wait_ge(summed, 1)
        nc.vector.tensor_copy(sum_row, pair(chip.banks[0:1, 0:4, :])).then_inc(sums_kept, 1)
        dve.wait_ge(spread, 1)
        nc.vector.tensor_copy(bias[:].rearrange("p g t -> p (g t)"), pair(chip.banks[:, 4:8, :])).then_inc(kept, 1)


def gmlp_v_stage(nc, chip, ctx, w_v, v_out):
    sem = lambda n: chip.semaphore(f"v_{n}")
    CHUNKS, PIECES, KP = E // HALF, 4, 2
    raw_loaded = [sem(f"raw_loaded{b}") for b in range(2)]
    w_hi_done, w_ready, v_done, gelu_done = sem("w_hi_done"), sem("w_ready"), sem("v_done"), sem("gelu_done")
    counted, averaged, root_done, inverse_done = sem("counted"), sem("averaged"), sem("root_done"), sem("inverse_done")
    v_normed, v_stored = sem("v_normed"), sem("v_stored")
    v = chip.at("v", Y_AT, [P, NT, E])
    w_hi = chip.at("v_w_hi", Y_AT + 64, [P, 2, KD, HALF], F32R)
    w_lo = chip.at("v_w_lo", Y_AT + 96, [P, 2, KD, HALF], F32R)
    raw = [chip.at(f"v_raw{b}", Y_AT + 128 + 4 * b, [P, KP, HALF]) for b in range(2)]
    stats = chip.at("v_stats", Y_AT + 136, [P, NT, CHUNKS, 6])
    mean_var = chip.at("v_mean_var", Y_AT + 137, [P, NT, 2])
    dev = chip.at("v_dev", Y_AT + 137.25, [P, NT])
    inv = chip.at("v_inv", Y_AT + 137.5, [P, NT])
    hT_hi, hT_lo = chip.hT
    block = ctx.enter_context(nc.Block())

    @block.sync
    def _(sp):
        for q in range(2):
            sp.dma_start(raw[q][:], w_v[q].rearrange("p (k n) -> p k n", k=KP)).then_inc(raw_loaded[q], 16)
        with sp.Fori(0, CHUNKS * PIECES // 2 - 1) as i:
            for q in range(2):
                sp.wait_ge(w_ready, i * 2 + (q + 1))
                sp.dma_start(raw[q][:], w_v[i * 2 + (q + 2)].rearrange("p (k n) -> p k n", k=KP)).then_inc(raw_loaded[q], 16)
        for t in range(NT):
            sp.wait_ge(v_normed, t + 1)
            sp.dma_start(v_out[t * P:(t + 1) * P, :], v[:, t, :]).then_inc(v_stored, 16)
        sp.wait_ge(v_stored, 16 * NT)

    @block.scalar
    def _(act):
        def split(c, wait=None):
            if wait is not None:
                act.wait_ge(v_done, wait)
            for q in range(PIECES):
                act.wait_ge(raw_loaded[q % 2], c * 32 + (q // 2 + 1) * 16)
                nc.scalar.activation(w_hi[:, bass.ds(c % 2, 1), KP * q:KP * (q + 1), :].rearrange("p a k n -> p (a k) n"),
                                     raw[q % 2][:], ACT.Copy).then_inc(w_hi_done, 1)

        def gelu(c):
            for t in range(NT):
                act.wait_ge(v_done, c * NT + (t + 2))
                nc.scalar.activation(v[:, t, bass.ds(c * HALF, HALF)], chip.banks[:, t, :],
                                     ACT.Gelu_apprx_tanh).then_inc(gelu_done, 1)

        act.sem_inc(gelu_done, 1)
        split(0)
        with act.Fori(0, CHUNKS - 1) as c:
            split(c + 1, wait=c * NT + 1)
            gelu(c)
        gelu(CHUNKS - 1)
        act.wait_ge(averaged, NT)
        nc.scalar.activation(dev[:], mean_var[:, :, 1], ACT.Sqrt, bias=chip.eps[:, 0:1]).then_inc(root_done, 1)

    @block.gpsimd
    def _(pool):
        with pool.Fori(0, CHUNKS) as c:
            for q in range(PIECES):
                pool.wait_ge(w_hi_done, c * PIECES + (q + 1))
                at = lambda w: w[:, bass.ds(c % 2, 1), KP * q:KP * (q + 1), :].rearrange("p a k n -> p (a k) n")
                nc.gpsimd.tensor_tensor(at(w_lo), raw[q % 2][:], at(w_hi).bitcast(F32), ALU.subtract).then_inc(w_ready, 1)

    @block.vector
    def _(dve):
        with dve.Fori(0, CHUNKS) as c:
            for t in range(NT):
                dve.wait_ge(gelu_done, c * NT + (t + 2))
                nc.vector.bn_stats(stats[:, t, bass.ds(c, 1), :].rearrange("p a s -> p (a s)"),
                                   v[:, t, bass.ds(c * HALF, HALF)]).then_inc(counted, 1)
        dve.wait_ge(counted, CHUNKS * NT)
        for t in range(NT):
            nc.vector.bn_aggr(mean_var[:, t, :], stats[:, t]).then_inc(averaged, 1)
        dve.wait_ge(root_done, 1)
        nc.vector.reciprocal(inv[:], dev[:]).then_inc(inverse_done, 1)
        dve.wait_ge(inverse_done, 1)
        for t in range(NT):
            nc.vector.tensor_scalar(v[:, t, :], v[:, t, :], mean_var[:, t, 0:1], inv[:, t:t + 1],
                                    ALU.subtract, ALU.mult).then_inc(v_normed, 1)

    @block.tensor
    def _(pe):
        pe.sem_inc(v_done, 1)
        with pe.Fori(0, CHUNKS) as c:
            pe.wait_ge(w_ready, c * PIECES + PIECES)
            half = c % 2
            for t in range(NT):
                pe.wait_ge(gelu_done, c * NT + 1)
                for k in range(KD):
                    for j, (h, w) in enumerate(((hT_hi, w_hi), (hT_hi, w_lo), (hT_lo, w_hi))):
                        last = nc.tensor.matmul(chip.banks[:, t, :], h[:, k, t * P:(t + 1) * P],
                                                w[:, bass.ds(half, 1), k, :].rearrange("p a n -> p (a n)"),
                                                start=(k == 0 and j == 0), stop=(k == KD - 1 and j == 2))
                last.then_inc(v_done, 1)


def gmlp_stage(nc, chip, ctx, w_u, w_down, v_in, ln_g):
    sem = lambda n: chip.semaphore(f"sg_{n}")
    ROUNDS = KE // 2
    up_loaded, v_loaded = ([sem(f"{n}_{c}") for c in "ab"] for n in ("up_loaded", "v_loaded"))
    down_loaded, gain_loaded = sem("down_loaded"), sem("gain_loaded")
    up_w_hi, up_w_ready, down_w_hi, down_w_ready = sem("up_w_hi"), sem("up_w_ready"), sem("down_w_hi"), sem("down_w_ready")
    u_done, mix_done, gelu_done, cur_ready, mix_biased = (
        sem("u_done"), sem("mix_done"), sem("gelu_done"), sem("cur_ready"), sem("mix_biased"))
    prod_ready, prod_hi, prod_split = sem("prod_ready"), sem("prod_hi"), sem("prod_split")
    down_done, y_free = sem("down_done"), sem("y_free")

    raw_up = [chip.at(f"sg_raw_up{c}", WORK + 4 * j, [P, KD, P]) for j, c in enumerate("ab")]
    raw_down = chip.at("sg_raw_down", WORK + 8, [P, 2, D])
    up_hi = [chip.at(f"sg_up_hi{c}", WORK + 16 + 8 * j, [P, KD, P], F32R) for j, c in enumerate("ab")]
    up_lo = [chip.at(f"sg_up_lo{c}", WORK + 20 + 8 * j, [P, KD, P], F32R) for j, c in enumerate("ab")]
    down_hi = chip.at("sg_down_hi", WORK + 32, [P, 2, D], F32R)
    down_lo = chip.at("sg_down_lo", WORK + 40, [P, 2, D], F32R)
    p_hi = [chip.at(f"sg_p_hi{c}", WORK + 48 + 8 * j, [P, T], F32R) for j, c in enumerate("ab")]
    p_lo = [chip.at(f"sg_p_lo{c}", WORK + 52 + 8 * j, [P, T], F32R) for j, c in enumerate("ab")]
    u = chip.at("sg_u", WORK + 64, [P, T])
    prod = chip.at("sg_prod", WORK + 68, [P, T])
    vg = [chip.at(f"sg_v{c}", WORK + 72 + 4 * j, [P, NT, P]) for j, c in enumerate("ab")]
    gain = chip.at("sg_gain", WORK + 80, [P, KE])
    cur = [chip.at(f"sg_cur{j}", WORK + 80.5 + 0.125 * j, [P, 1]) for j in range(2)]
    w_spT, bias, banks, y = chip.w_spT, chip.sg_bias, chip.banks, chip.y
    block = ctx.enter_context(nc.Block())

    @block.sync
    def _(sp):
        def load_up(c, n, wait=None):
            if wait is not None:
                sp.wait_ge(up_w_ready, wait)
            sp.dma_start(raw_up[c][:], w_u[n].rearrange("p (k c) -> p k c", k=KD)).then_inc(up_loaded[c], 16)
            if wait is not None:
                sp.wait_ge(mix_done, wait)
            sp.dma_start(vg[c][:], v_in[:, bass.ds(n * P, P)].rearrange("(n p) f -> p n f", p=P)).then_inc(v_loaded[c], 16)

        def load_down(i, wait=None):
            if wait is not None:
                sp.wait_ge(down_w_ready, wait)
            sp.dma_start(raw_down[:], w_down[i].rearrange("p (s n) -> p s n", s=2)).then_inc(down_loaded, 16)

        load_up(0, 0)
        sp.dma_start(gain[:], ln_g).then_inc(gain_loaded, 16)
        load_up(1, 1)
        load_down(0)
        with sp.Fori(0, ROUNDS - 1) as i:
            load_up(0, i * 2 + 2, wait=i * 2 + 1)
            load_up(1, i * 2 + 3, wait=i * 2 + 2)
            load_down(i + 1, wait=i + 1)

    @block.scalar
    def _(act):
        def split_up(c, n, wait=None):
            act.wait_ge(up_loaded[c], (n - c) * 8 + 16)
            if wait is not None:
                act.wait_ge(u_done, wait)
            nc.scalar.activation(up_hi[c][:], raw_up[c][:], ACT.Copy).then_inc(up_w_hi, 1)

        def split_down(i, wait=None):
            act.wait_ge(down_loaded, i * 16 + 16)
            if wait is not None:
                act.wait_ge(down_done, wait)
            nc.scalar.activation(down_hi[:], raw_down[:], ACT.Copy).then_inc(down_w_hi, 1)

        def gelu(n):
            act.wait_ge(u_done, n + 1)
            act.wait_ge(prod_ready, n)
            nc.scalar.activation(u[:], pair(banks[:, 0:2, :]), ACT.Gelu_apprx_tanh).then_inc(gelu_done, 1)

        def product_hi(c, n, wait=None):
            act.wait_ge(prod_ready, n + 1)
            if wait is not None:
                act.wait_ge(down_done, wait)
            nc.scalar.activation(p_hi[c][:], prod[:], ACT.Copy).then_inc(prod_hi, 1)

        split_up(0, 0)
        split_up(1, 1)
        gelu(0)
        product_hi(0, 0)
        split_down(0)
        with act.Fori(0, ROUNDS - 1) as i:
            split_up(0, i * 2 + 2, wait=i * 2 + 1)
            gelu(i * 2 + 1)
            product_hi(1, i * 2 + 1)
            split_up(1, i * 2 + 3, wait=i * 2 + 2)
            gelu(i * 2 + 2)
            product_hi(0, i * 2 + 2, wait=i * NT + NT)
            split_down(i + 1, wait=i * NT + NT)
        gelu(KE - 1)
        product_hi(1, KE - 1)

    @block.gpsimd
    def _(pool):
        def up_low(c, n):
            pool.wait_ge(up_w_hi, n + 1)
            nc.gpsimd.tensor_tensor(up_lo[c][:], raw_up[c][:], up_hi[c][:].bitcast(F32), ALU.subtract).then_inc(up_w_ready, 1)

        def down_low(i):
            pool.wait_ge(down_w_hi, i + 1)
            nc.gpsimd.tensor_tensor(down_lo[:], raw_down[:], down_hi[:].bitcast(F32), ALU.subtract).then_inc(down_w_ready, 1)

        def product_low(c, n):
            pool.wait_ge(prod_hi, n + 1)
            nc.gpsimd.tensor_tensor(p_lo[c][:], prod[:], p_hi[c][:].bitcast(F32), ALU.subtract).then_inc(prod_split, 1)

        up_low(0, 0)
        up_low(1, 1)
        product_low(0, 0)
        down_low(0)
        with pool.Fori(0, ROUNDS - 1) as i:
            up_low(0, i * 2 + 2)
            product_low(1, i * 2 + 1)
            up_low(1, i * 2 + 3)
            product_low(0, i * 2 + 2)
            down_low(i + 1)
        product_low(1, KE - 1)

    @block.vector
    def _(dve):
        def fetch_gain(c, n):
            nc.vector.tensor_copy(cur[c][:], gain[:, bass.ds(n, 1)]).then_inc(cur_ready, 1)

        def combine(c, n):
            dve.wait_ge(cur_ready, n + 1)
            dve.wait_ge(mix_done, n + 1)
            dve.wait_ge(prod_split, n)
            nc.vector.scalar_tensor_tensor(
                out=prod[:].rearrange("p (n t) -> p n t", t=P),
                in0=pair(banks[:, 2:4, :]).rearrange("p (n t) -> p n t", t=P), scalar=cur[c][:, 0:1],
                in1=bias[:, bass.ds(n, 1), :].broadcast_to([P, NT, P]),
                op0=ALU.mult, op1=ALU.add).then_inc(mix_biased, 1)
            dve.wait_ge(mix_biased, n + 1)
            dve.wait_ge(gelu_done, n + 1)
            nc.vector.tensor_tensor(prod[:], prod[:], u[:], ALU.mult).then_inc(prod_ready, 1)

        def add_down(i):
            for t in range(NT):
                dve.wait_ge(down_done, i * NT + (t + 1))
                b = 4 + 2 * (t % 2)
                nc.vector.tensor_tensor(y[:, t, :], y[:, t, :], pair(banks[:, b:b + 2, :]), ALU.add).then_inc(y_free, 1)

        dve.wait_ge(gain_loaded, 16)
        nc.vector.memset(y[:], 0.0).then_inc(y_free, 2)
        dve.wait_ge(y_free, 2)
        fetch_gain(0, 0)
        fetch_gain(1, 1)
        combine(0, 0)
        with dve.Fori(0, ROUNDS - 1) as i:
            fetch_gain(0, i * 2 + 2)
            combine(1, i * 2 + 1)
            fetch_gain(1, i * 2 + 3)
            combine(0, i * 2 + 2)
            dve.wait_ge(y_free, i * NT + 2)
            add_down(i)
        combine(1, KE - 1)
        dve.wait_ge(y_free, (ROUNDS - 1) * NT + 2)
        add_down(ROUNDS - 1)

    @block.tensor
    def _(pe):
        def up(c, n):
            pe.wait_ge(up_w_ready, n + 1)
            pe.wait_ge(gelu_done, n)
            feature_major_product(nc, chip, 0, up_hi[c], up_lo[c]).then_inc(u_done, 1)
            pe.wait_ge(v_loaded[c], (n - c) * 8 + 16)
            pe.wait_ge(mix_biased, n)
            for s in range(NT):
                last = nc.tensor.matmul(banks[:, 2 + s // 4, (s % 4) * P:(s % 4 + 1) * P], vg[c][:, s, :],
                                        w_spT[:, bass.ds(n, 1), :].rearrange("s a t -> s (a t)"), start=True, stop=True)
            last.then_inc(mix_done, 1)

        up(0, 0)
        with pe.Fori(0, ROUNDS - 1) as i:
            up(1, i * 2 + 1)
            up(0, i * 2 + 2)
            down_product(nc, chip, pe, i, p_hi, p_lo, down_hi, down_lo, prod_split, down_w_ready, y_free, down_done)
        up(1, KE - 1)
        down_product(nc, chip, pe, ROUNDS - 1, p_hi, p_lo, down_hi, down_lo, prod_split, down_w_ready, y_free, down_done)


FT_AT, KT_AT, V_AT, SEL_AT, ONEHOT_AT, VC_AT = 68, 116, 148, 164, 166, 174
SLC, WIN = 0, 1


class NsaState:

    def __init__(self, chip):
        self.fT = chip.at("fT", FT_AT, [P, 12, T])
        self.kT = chip.at("kT", KT_AT, [P, 2, GROUPS, T])
        self.v = chip.at("v_tok", V_AT, [P, NT, 2 * KVW])
        self.selT = chip.at("selT", SEL_AT, [GROUPS * NSLC, T], BF16)
        self.onehot = chip.at("onehot", ONEHOT_AT, [GROUPS * NSLC, GROUPS, T], BF16)
        self.vc = chip.at("vc_split", VC_AT, [NCMP, GROUPS, P], F32R)


def nsa_projection_stage(nc, chip, ctx, nsa, w_fm):
    sem = lambda n: chip.semaphore(f"proj_{n}")
    loaded = [sem(f"loaded_{c}") for c in "ab"]
    w_hi_done, w_ready, product_done, kept = sem("w_hi_done"), sem("w_ready"), sem("product_done"), sem("kept")
    at = 164
    raw = [chip.at(f"proj_raw_{c}", at + 4 * j, [P, KD, P]) for j, c in enumerate("ab")]
    w_hi = [chip.at(f"proj_hi_{c}", at + 8 + 8 * j, [P, KD, P], F32R) for j, c in enumerate("ab")]
    w_lo = [chip.at(f"proj_lo_{c}", at + 12 + 8 * j, [P, KD, P], F32R) for j, c in enumerate("ab")]
    ROUNDS, PLAIN = FM_TILES // 2, 12 // 2
    block = ctx.enter_context(nc.Block())

    @block.sync
    def _(sp):
        def load(c, n):
            sp.dma_start(raw[c][:], w_fm[n].rearrange("p (k c) -> p k c", k=KD)).then_inc(loaded[c], 16)
        load(0, 0)
        load(1, 1)
        with sp.Fori(0, ROUNDS - 1) as i:
            for c in range(2):
                sp.wait_ge(w_ready, i * 2 + (c + 1))
                load(c, i * 2 + (c + 2))

    @block.scalar
    def _(act):
        def split(c, i, wait=None):
            act.wait_ge(loaded[c], i * 16 + 16)
            if wait is not None:
                act.wait_ge(product_done, wait)
            nc.scalar.activation(w_hi[c][:], raw[c][:], ACT.Copy).then_inc(w_hi_done, 1)

        def keep(c, i):
            act.wait_ge(product_done, i * 2 + (c + 1))
            nc.scalar.activation(nsa.fT[:, bass.ds(i * 2 + c, 1), :].rearrange("p a t -> p (a t)"),
                                 pair(chip.banks[:, 2 * c:2 * c + 2, :]), ACT.Copy).then_inc(kept, 1)

        def keep_keys(c, i):
            act.wait_ge(product_done, i * 2 + (c + 1))
            for g in range(2):
                for rows in range(2):
                    last = nc.scalar.activation(nsa.kT[64 * rows:64 * rows + 64, i - PLAIN, 2 * c + g, :],
                                                pair(chip.banks[64 * g:64 * g + 64, 2 * c:2 * c + 2, :]), ACT.Copy)
            last.then_inc(kept, 1)

        act.sem_inc(kept, 2)
        split(0, 0)
        split(1, 0)
        with act.Fori(0, PLAIN) as i:
            keep(0, i)
            split(0, i + 1, wait=i * 2 + 1)
            keep(1, i)
            split(1, i + 1, wait=i * 2 + 2)
        for i in range(PLAIN, ROUNDS):
            for c in range(2):
                keep_keys(c, i)
                if i < ROUNDS - 1:
                    split(c, i + 1, wait=i * 2 + c + 1)

    @block.gpsimd
    def _(pool):
        with pool.Fori(0, ROUNDS) as i:
            for c in range(2):
                pool.wait_ge(w_hi_done, i * 2 + (c + 1))
                nc.gpsimd.tensor_tensor(w_lo[c][:], raw[c][:], w_hi[c][:].bitcast(F32), ALU.subtract).then_inc(w_ready, 1)

    @block.tensor
    def _(pe):
        with pe.Fori(0, ROUNDS) as i:
            for c in range(2):
                pe.wait_ge(w_ready, i * 2 + (c + 1))
                pe.wait_ge(kept, i * 2 + (c + 1))
                feature_major_product(nc, chip, 2 * c, w_hi[c], w_lo[c]).then_inc(product_done, 1)


def nsa_value_stage(nc, chip, ctx, nsa, w_tok):
    sem = lambda n: chip.semaphore(f"val_{n}")
    loaded, w_hi_done, w_ready, product_done, kept = (
        sem(n) for n in ("loaded", "w_hi_done", "w_ready", "product_done", "kept"))
    widths = [KVW, KVW, GATES]
    raw = chip.at("val_raw", 164, [P, KD * KVW])
    w_hi = [chip.at(f"val_hi{b}", 172 + 16 * b, [P, KD * KVW], F32R) for b in range(2)]
    w_lo = [chip.at(f"val_lo{b}", 180 + 16 * b, [P, KD * KVW], F32R) for b in range(2)]
    hT_hi, hT_lo = chip.hT
    block = ctx.enter_context(nc.Block())

    @block.sync
    def _(sp):
        for p, width in enumerate(widths):
            if p:
                sp.wait_ge(w_ready, p)
            sp.dma_start(raw[:, 0:KD * width], w_tok[:, KD * KVW * p:KD * (KVW * p + width)]).then_inc(loaded, 16)

    @block.scalar
    def _(act):
        def split(p):
            n = KD * widths[p]
            act.wait_ge(loaded, 16 * (p + 1))
            if p == 2:
                act.wait_ge(product_done, NT)
            nc.scalar.activation(w_hi[p % 2][:, 0:n], raw[:, 0:n], ACT.Copy).then_inc(w_hi_done, 1)

        split(0)
        split(1)
        for p, width in enumerate(widths):
            for t in range(NT):
                act.wait_ge(product_done, NT * p + t + 1)
                source = chip.banks[:, t, 0:width]
                if p < 2:
                    nc.scalar.activation(nsa.v[:, t, KVW * p:KVW * (p + 1)], source, ACT.Copy).then_inc(kept, 1)
                else:
                    nc.scalar.activation(chip.gates[:, t, :], source, ACT.Sigmoid).then_inc(kept, 1)
            if p == 0:
                split(2)

    @block.gpsimd
    def _(pool):
        for p, width in enumerate(widths):
            n = KD * width
            pool.wait_ge(w_hi_done, p + 1)
            nc.gpsimd.tensor_tensor(w_lo[p % 2][:, 0:n], raw[:, 0:n], w_hi[p % 2][:, 0:n].bitcast(F32),
                                    ALU.subtract).then_inc(w_ready, 1)

    @block.tensor
    def _(pe):
        for p, width in enumerate(widths):
            pe.wait_ge(w_ready, p + 1)
            for t in range(NT):
                if p:
                    pe.wait_ge(kept, NT * (p - 1) + t + 1)
                for k in range(KD):
                    for j, (h, w) in enumerate(((hT_hi, w_hi), (hT_hi, w_lo), (hT_lo, w_hi))):
                        last = nc.tensor.matmul(chip.banks[:, t, 0:width], h[:, k, t * P:(t + 1) * P],
                                                w[p % 2][:, k * width:(k + 1) * width],
                                                start=(k == 0 and j == 0), stop=(k == KD - 1 and j == 2))
                last.then_inc(product_done, 1)


def nsa_compressed_stage(nc, chip, ctx, nsa, cmp_pe, cmp_w1, cmp_w2, p_cmp_out):
    sem = lambda n: chip.semaphore(f"cmp_{n}")
    zeroed, loaded = sem("zeroed"), sem("loaded")
    mask_filled, mask_made = sem("mask_filled"), sem("mask_made")
    hidden_done, pe_kept, hidden, compressed, kc_ready, vc_hi, vc_ready = (
        sem(n) for n in ("hidden_done", "pe_kept", "hidden", "compressed", "kc_ready", "vc_hi", "vc_ready"))
    scored, step, expd, masked, normed, gated = (
        sem(n) for n in ("scored", "step", "expd", "masked", "normed", "gated"))
    stored = [sem(f"stored{b}") for b in range(2)]
    shifted, chosen, sel_turned, sel_kept, late = (sem(n) for n in ("shifted", "chosen", "sel_turned", "sel_kept", "late"))

    w1 = [chip.at(f"cmp_w1_{c}", H_AT + 16 * j, [P, CMP_LEN, P]) for j, c in enumerate("kv")]
    w2 = [chip.at(f"cmp_w2_{c}", H_AT + 32 + 0.5 * j, [P, P]) for j, c in enumerate("kv")]
    pe_in = chip.at("cmp_pe", H_AT + 33, [P, 2, CMP_LEN])
    pe_out = chip.at("cmp_pe_out", H_AT + 33.5, [P, 2])
    hid = [chip.at(f"cmp_hid_{c}", H_AT + 34 + 0.5 * j, [P, 2, NCMP]) for j, c in enumerate("kv")]
    kc = chip.at("cmp_k", H_AT + 35, [P, GROUPS, NCMP])
    open_bias = chip.at("cmp_open_bias", H_AT + 36, [P, NT, 64])
    open_mask = chip.at("cmp_open_mask", H_AT + 38, [P, NT, 64])
    valid = chip.at("sel_valid", H_AT + 40, [P, NT, NSLC])
    invalid_score = chip.at("sel_invalid", H_AT + 40.5, [P, NT, NSLC])
    forced = chip.at("sel_forced", H_AT + 41, [P, NT, NSLC])
    e = [chip.at(f"cmp_e{b}", H_AT + 42 + 4 * b, [P, 2, 8, 64]) for b in range(2)]
    pg = [chip.at(f"cmp_pg{b}", H_AT + 50 + 4 * b, [P, 2, 8, 64]) for b in range(2)]
    top = chip.at("cmp_top", H_AT + 58, [P, 2, 16])
    den = chip.at("cmp_den", H_AT + 58.25, [P, 2, 3, 16])
    imp = chip.at("cmp_imp", H_AT + 59, [P, 2, GROUPS, 64])
    score = chip.at("cmp_score", H_AT + 61, [P, 2, GROUPS, NSLC])
    best = chip.at("cmp_best", H_AT + 62, [P, 2, GROUPS, 8])
    sel = chip.at("cmp_sel", H_AT + 62.5, [P, 2, GROUPS, NSLC])
    banks = chip.banks
    block = ctx.enter_context(nc.Block())
    n_loads = 2 * 2 + 2 * 2 + 2

    def heads_of(t, b):
        return banks[:, 2 * b:2 * b + 2, :].rearrange("p a (j n) -> p a j n", n=64)[:, :, :, 0:NCMP]

    flat = lambda ap: ap.rearrange("p a j n -> p (a j) n")

    @block.sync
    def _(sp):
        sp.wait_ge(zeroed, 4)
        for j in range(2):
            for half in range(2):
                rows = slice(64 * half, 64 * half + 64)
                sp.dma_start(w1[j][rows, :, rows], cmp_w1[j]).then_inc(loaded, 16)
                sp.dma_start(w2[j][rows, rows], cmp_w2[j]).then_inc(loaded, 16)
        for half in range(2):
            sp.dma_start(pe_in[64 * half:64 * half + 64, :, :], cmp_pe).then_inc(loaded, 16)
        for t in range(NT):
            sp.wait_ge(gated, t + 1)
            sp.dma_start(p_cmp_out[t * P:(t + 1) * P, :, :].rearrange("p (j a) n -> p a j n", a=2)[:, 0, :, 0:NCMP],
                         pg[t % 2][:, 0, :, 0:NCMP]).then_inc(stored[t % 2], 16)
            sp.dma_start(p_cmp_out[t * P:(t + 1) * P, :, :].rearrange("p (j a) n -> p a j n", a=2)[:, 1, :, 0:NCMP],
                         pg[t % 2][:, 1, :, 0:NCMP]).then_inc(stored[t % 2], 16)
        for b in range(2):
            sp.wait_ge(stored[b], 32 * (NT // 2))

    @block.gpsimd
    def _(pool):
        for m in (w1[0], w1[1], w2[0], w2[1]):
            nc.gpsimd.memset(m[:], 0.0).then_inc(zeroed, 1)
        fills = [(open_bias, 0.0), (open_mask, 1.0), (valid, 1.0), (invalid_score, 0.0), (forced, FORCE), (nsa.onehot, 0.0)]
        for m, value in fills:
            nc.gpsimd.memset(m[:], value).then_inc(mask_filled, 1)
        pool.wait_ge(mask_filled, len(fills))
        ended = dict(base=1 - CMP_LEN, pattern=[[P, NT], [-CMP_STRIDE, 64]], channel_multiplier=1)
        begun = dict(base=0, pattern=[[P, NT], [-SLC_LEN, NSLC]], channel_multiplier=1)
        near = dict(base=2 * SLC_LEN - 1, pattern=[[-P, NT], [SLC_LEN, NSLC]], channel_multiplier=-1)
        for m, fill, where in ((open_bias, NEG, ended), (open_mask, 0.0, ended), (valid, 0.0, begun),
                               (invalid_score, -FORCE, begun), (forced, 0.0, near)):
            nc.gpsimd.affine_select(out=m[:], in_=m[:], compare_op=ALU.is_ge, fill=fill, **where).then_inc(mask_made, 1)
        nc.gpsimd.affine_select(
            out=nsa.onehot[:].rearrange("r g (j k) -> r g j k", k=SLC_LEN),
            in_=nsa.onehot[:].rearrange("r g (j k) -> r g j k", k=SLC_LEN), compare_op=ALU.not_equal, fill=1.0,
            base=0, pattern=[[-NSLC, GROUPS], [-1, NSLC], [0, SLC_LEN]], channel_multiplier=1).then_inc(mask_made, 1)
        pool.wait_ge(mask_made, 6)
        nc.gpsimd.memset(forced[:, :, 0:1], FORCE).then_inc(mask_made, 1)
        for t in range(NT):
            b = t % 2
            pool.wait_ge(expd, t + 1)
            nc.gpsimd.tensor_tensor(flat(e[b][:])[:, :, 0:NCMP], flat(e[b][:])[:, :, 0:NCMP],
                                    open_mask[:, t:t + 1, 0:NCMP].broadcast_to([P, 16, NCMP]), ALU.mult).then_inc(masked, 1)
            pool.wait_ge(normed, t + 1)
            if t >= 2:
                pool.wait_ge(stored[b], 32 * (t // 2))
            for a in range(2):
                gate = chip.gates[:, t, :].rearrange("p (j a c) -> p a j c", a=2, c=3)[:, a, :, 0:1]
                last = nc.gpsimd.tensor_tensor(pg[b][:, a, :, 0:NCMP], e[b][:, a, :, 0:NCMP],
                                               gate.broadcast_to([P, 8, NCMP]), ALU.mult)
            last.then_inc(gated, 1)

    @block.tensor
    def _(pe):
        pe.wait_ge(loaded, 16 * n_loads)
        for j in range(2):
            for l in range(CMP_LEN):
                last_token = l + CMP_STRIDE * (NCMP - 1) + 1
                nc.tensor.matmul(banks[:, 2 * j, 0:2 * NCMP].rearrange("p (q n) -> p q n", q=2), w1[j][:, l, :],
                                 nsa.fT[:, 8 + 2 * j:10 + 2 * j, l:last_token:CMP_STRIDE],
                                 start=(l == 0), stop=(l == CMP_LEN - 1))
                last = nc.tensor.matmul(banks[:, 2 * j + 1, 0:1], w1[j][:, l, :], pe_in[:, j, l:l + 1],
                                        start=(l == 0), stop=(l == CMP_LEN - 1))
            last.then_inc(hidden_done, 1)
        pe.wait_ge(hidden, 1)
        nc.tensor.matmul(banks[:, 4, 0:2 * NCMP], w2[0][:], hid[0][:].rearrange("p q n -> p (q n)"),
                         start=True, stop=True).then_inc(compressed, 1)
        pe.wait_ge(hidden, 2)
        for q in range(2):
            last = nc.tensor.matmul(banks[0:NCMP, 5, q * P:(q + 1) * P], hid[1][:, q, :], w2[1][:], start=True, stop=True)
        last.then_inc(compressed, 1)
        pe.wait_ge(kc_ready, 8)

        def scores(t):
            b = t % 2
            if t >= 2:
                pe.wait_ge(step, 2 * (t - 2) + 1)
            for j in range(8):
                for a in range(2):
                    rows = slice(64 * a, 64 * a + 64)
                    last = nc.tensor.matmul(banks[:, 2 * b + a, 64 * j:64 * j + NCMP],
                                            nsa.fT[rows, j, t * P:(t + 1) * P], kc[rows, j // 2, :], start=True, stop=True)
            last.then_inc(scored, 1)

        def turn_selection(t):
            pe.wait_ge(chosen, t + 1)
            if t >= 2:
                pe.wait_ge(sel_kept, t - 1)
            nc.tensor.transpose(banks[0:GROUPS * NSLC, 6 + t % 2, 0:P], sel[:, t % 2].rearrange("p g j -> p (g j)"),
                                chip.ident[:]).then_inc(sel_turned, 1)

        scores(0)
        for t in range(1, NT):
            scores(t)
            if t >= 2:
                turn_selection(t - 2)
        turn_selection(NT - 2)
        turn_selection(NT - 1)

    @block.scalar
    def _(act):
        for j in range(2):
            act.wait_ge(hidden_done, j + 1)
            nc.scalar.activation(pe_out[:, j:j + 1], banks[:, 2 * j + 1, 0:1], ACT.Copy).then_inc(pe_kept, 1)
            act.wait_ge(pe_kept, j + 1)
            nc.scalar.activation(hid[j][:].rearrange("p q n -> p (q n)"), banks[:, 2 * j, 0:2 * NCMP],
                                 ACT.Gelu_apprx_tanh, bias=pe_out[:, j:j + 1]).then_inc(hidden, 1)
        act.wait_ge(compressed, 2)
        value = banks[0:NCMP, 5, 0:2 * P].rearrange("n (g d) -> n g d", d=DH)
        nc.scalar.activation(nsa.vc[:, :, 0:DH], value, ACT.Copy).then_inc(vc_hi, 1)
        for t in range(NT):
            act.wait_ge(shifted, t + 1)
            view = flat(e[t % 2][:])[:, :, 0:NCMP]
            nc.scalar.activation(view, view, ACT.Exp, scale=SCALE).then_inc(expd, 1)
            if t >= 1:
                act.wait_ge(sel_turned, t)
                nc.scalar.activation(nsa.selT[:, (t - 1) * P:t * P], banks[0:GROUPS * NSLC, 6 + (t - 1) % 2, 0:P],
                                     ACT.Copy).then_inc(sel_kept, 1)
        act.wait_ge(sel_turned, NT)
        nc.scalar.activation(nsa.selT[:, (NT - 1) * P:], banks[0:GROUPS * NSLC, 6 + (NT - 1) % 2, 0:P],
                             ACT.Copy).then_inc(sel_kept, 1)

    @block.vector
    def _(dve):
        done = [0]

        def then(instruction):
            done[0] += 1
            instruction.then_inc(late, 1)
            dve.wait_ge(late, done[0])

        dve.wait_ge(compressed, 1)
        for g in range(GROUPS):
            source = banks[64 * (g % 2):64 * (g % 2) + 64, 4, (g // 2) * NCMP:(g // 2 + 1) * NCMP]
            for half in range(2):
                nc.vector.tensor_copy(kc[64 * half:64 * half + 64, g, :], source).then_inc(kc_ready, 1)
        dve.wait_ge(vc_hi, 1)
        value = banks[0:NCMP, 5, 0:2 * P].rearrange("n (g d) -> n g d", d=DH)
        nc.vector.tensor_tensor(nsa.vc[:, :, DH:P], value, nsa.vc[:, :, 0:DH].bitcast(F32), ALU.subtract).then_inc(vc_ready, 1)
        dve.wait_ge(mask_made, 7)
        then(nc.vector.memset(imp[:], 0.0))

        def shift(t):
            b = t % 2
            dve.wait_ge(scored, t + 1)
            if t >= 2:
                dve.wait_ge(gated, t - 1)
            view = flat(e[b][:])[:, :, 0:NCMP]
            nc.vector.tensor_tensor(view, heads_of(t, b).rearrange("p a j n -> p (a j) n"),
                                    open_bias[:, t:t + 1, 0:NCMP].broadcast_to([P, 16, NCMP]), ALU.add).then_inc(step, 1)
            dve.wait_ge(step, 2 * t + 1)
            nc.vector.tensor_reduce(top[:, b, :], view, AX.X, ALU.max).then_inc(step, 1)
            dve.wait_ge(step, 2 * t + 2)
            nc.vector.tensor_tensor(view, view, top[:, b, :].unsqueeze(2).broadcast_to([P, 16, NCMP]),
                                    ALU.subtract).then_inc(shifted, 1)

        def select(t):
            b = t % 2
            view = flat(e[b][:])[:, :, 0:NCMP]
            dve.wait_ge(masked, t + 1)
            then(nc.vector.tensor_reduce(den[:, b, 0, :], view, AX.X, ALU.add))
            then(nc.vector.tensor_scalar(den[:, b, 1, :], den[:, b, 0, :], 1e-30, None, ALU.max))
            then(nc.vector.reciprocal(den[:, b, 2, :], den[:, b, 1, :]))
            nc.vector.tensor_tensor(view, view, den[:, b, 2, :].unsqueeze(2).broadcast_to([P, 16, NCMP]),
                                    ALU.mult).then_inc(normed, 1)
            dve.wait_ge(normed, t + 1)
            for g in range(GROUPS):
                last = nc.vector.tensor_reduce(imp[:, b, g, 0:NCMP],
                                               e[b][:, :, 2 * g:2 * g + 2, 0:NCMP].rearrange("p a j n -> p n a j"),
                                               AX.XY, ALU.add)
            then(last)
            quads = imp[:, b].rearrange("p g (j c) -> p g j c", c=4)
            s = score[:, b]
            then(nc.vector.tensor_tensor(s, quads[:, :, :, 0], quads[:, :, :, 1], ALU.add))
            then(nc.vector.tensor_tensor(s, s, quads[:, :, :, 2], ALU.add))
            then(nc.vector.tensor_scalar(quads[:, :, :, 3], quads[:, :, :, 3], 0.5, None, ALU.mult))
            then(nc.vector.tensor_tensor(s, s, quads[:, :, :, 3], ALU.add))
            then(nc.vector.tensor_tensor(s[:, :, 1:NSLC], s[:, :, 1:NSLC], quads[:, :, 0:NSLC - 1, 3], ALU.add))
            for m, op in ((forced, ALU.add), (valid, ALU.mult), (invalid_score, ALU.add)):
                then(nc.vector.tensor_tensor(s, s, m[:, t:t + 1, :].broadcast_to([P, GROUPS, NSLC]), op))
            for g in range(GROUPS):
                last = nc.vector.max(best[:, b, g, :], score[:, b, g, :])
            then(last)
            if t >= 2:
                dve.wait_ge(sel_turned, t - 1)
            for g in range(GROUPS):
                last = nc.vector.match_replace(sel[:, b, g, :], best[:, b, g, :], score[:, b, g, :], 1e30)
            then(last)
            nc.vector.tensor_scalar(sel[:, b], sel[:, b], 1e29, NEG, ALU.is_lt, ALU.mult).then_inc(chosen, 1)

        shift(0)
        for t in range(1, NT):
            shift(t)
            select(t - 1)
        select(NT - 1)


def attention_plan():
    jobs = [(branch, i) for i in range(NT) for branch in (SLC, WIN)]
    tiles, n = [], 0
    for branch, i in jobs:
        keys = list(range(0, i + 1)) + [None] if branch == SLC else list(range(max(0, i - WINDOW // P), i + 1))
        tiles.append([(n + x, key) for x, key in enumerate(keys)])
        n += len(keys)
    return jobs, tiles, n


def nsa_attention_stage(nc, chip, ctx, nsa, p_cmp_in, oT):
    sem = lambda n: chip.semaphore(f"att_{n}")
    jobs, tiles, TILES = attention_plan()
    JOBS, HEAD_JOBS = len(jobs), len(jobs) * HPG
    q_hi, q_lo, k_hi, k_lo, v_hi, v_lo, group_copied = (
        sem(n) for n in ("q_hi", "q_lo", "k_hi", "k_lo", "v_hi", "v_lo", "group_copied"))
    scored, maxed, expd, inverted, scaled = (sem(n) for n in ("scored", "maxed", "expd", "inverted", "scaled"))
    turned, hi_done, lo_done, multiplied = (sem(n) for n in ("turned", "hi_done", "lo_done", "multiplied"))
    pool_go, pe_go = sem("pool_go"), sem("pe_go")
    pc_loaded, upper_kept, folded = [sem(f"pc_loaded{b}") for b in range(2)], sem("upper_kept"), sem("folded")

    qS = chip.at("att_q", 36, [P, HPG, T], F32R)
    kS_hi = chip.at("att_k_hi", 52, [P, 2, T], F32R)
    kS_lo = chip.at("att_k_lo", 60, [P, 2, T], F32R)
    vS = chip.at("att_v", 100, [P, 2, NT, P], F32R)
    pT_hi = [chip.at(f"att_pT_hi{b}", 108 + 2 * b, [P, HALF], F32R) for b in range(2)]
    pT_lo = [chip.at(f"att_pT_lo{b}", 112 + 2 * b, [P, HALF], F32R) for b in range(2)]
    vc = chip.at("att_vc", 176, [NCMP, P], F32R)
    gates = chip.at("att_gates", 176.5, [P, NT, HPG, 3])
    prob = [chip.at("att_p_slc", 177, [P, HPG, T]), chip.at("att_p_win", 193, [P, HPG, WINDOW + P])]
    pc = [chip.at(f"att_p_cmp{b}", 203 + b, [P, HPG, 64]) for b in range(2)]
    negmax, den, inv = (chip.at(f"att_{n}", 205 + j / 8, [P, 8]) for j, n in enumerate(("negmax", "den", "inv")))
    upper = chip.at("att_upper", 205.5, [64, HALF])
    banks = chip.banks
    block = ctx.enter_context(nc.Block())

    def key_range(branch, i):
        return (0 if branch == SLC else max(0, i - WINDOW // P)) * P, (i + 1) * P

    def slot(m):
        return banks[:, 2 * (m % 2):2 * (m % 2) + 2, :]

    def portions(J):
        n = len(tiles[J])
        return [tiles[J][n * h // HPG:n * (h + 1) // HPG] for h in range(HPG)]

    def walk(head, tile):
        for h in range(HPG):
            head(0, h)
        for J in range(1, JOBS):
            for h, part in enumerate(portions(J - 1)):
                head(J, h)
                for n, key in part:
                    tile(J - 1, n, key)
        for n, key in tiles[JOBS - 1]:
            tile(JOBS - 1, n, key)

    def heads(g, m):
        return g * HEAD_JOBS + (m + 2)

    def keys(g, n):
        return g * TILES + (n + 2)

    def queries(g, i):
        return g * NT + (i + 2)

    @block.sync
    def _(sp):
        with sp.Fori(0, GROUPS) as g:
            for i in range(NT):
                before = tiles[2 * (i - 2)][-1][0] if i >= 2 else -1
                sp.wait_ge(turned, keys(g, before))
                sp.dma_start(pc[i % 2][:, :, 0:NCMP], p_cmp_in[i * P:(i + 1) * P, bass.ds(g * HPG, HPG), 0:NCMP]
                             ).then_inc(pc_loaded[i % 2], 16)

    @block.scalar
    def _(act):
        for count in (expd, hi_done, upper_kept):
            act.sem_inc(count, 1)
        with act.Fori(0, GROUPS) as g:
            act.wait_ge(scored, heads(g, -1))
            act.wait_ge(multiplied, keys(g, -1))
            for a in range(2):
                rows = slice(64 * a, 64 * a + 64)
                last = nc.scalar.activation(qS[rows, a:HPG:2, :], nsa.fT[rows, bass.ds(g * 2, 2), :], ACT.Copy, scale=SCALE)
            last.then_inc(q_hi, 1)
            nc.scalar.activation(kS_hi[:], nsa.kT[:, :, bass.ds(g, 1), :].rearrange("p b g t -> p b (g t)"),
                                 ACT.Copy).then_inc(k_hi, 1)
            for b in range(2):
                last = nc.scalar.activation(vS[:, b, :, 0:DH], nsa.v[:, :, bass.ds(g * DH + b * KVW, DH)], ACT.Copy)
            last.then_inc(v_hi, 1)

            def head(J, h):
                branch, i = jobs[J]
                m = J * HPG + h
                lo, hi = key_range(branch, i)
                act.wait_ge(maxed, heads(g, m))
                if J >= 2:
                    act.wait_ge(turned, keys(g, tiles[J - 2][-1][0]))
                nc.scalar.activation(prob[branch][:, h, 0:hi - lo], pair(slot(m))[:, 0:hi - lo], ACT.Exp,
                                     bias=negmax[:, m % 8:m % 8 + 1], accum_out=den[:, m % 8:m % 8 + 1]).then_inc(expd, 1)

            def tile(J, n, key):
                rows = P if key is not None else NCMP
                act.wait_ge(turned, keys(g, n))
                act.wait_ge(multiplied, keys(g, max(n - 2, -1)))
                nc.scalar.activation(pT_hi[n % 2][0:rows, :], banks[0:rows, 4 + n % 2, :], ACT.Copy).then_inc(hi_done, 1)
                branch, i = jobs[J]
                if branch == SLC and i >= 1 and n == tiles[J][0][0]:
                    keep_upper(i - 1)

            def keep_upper(i):
                act.wait_ge(multiplied, keys(g, tiles[2 * i + 1][-1][0]))
                act.wait_ge(folded, queries(g, i - 1))
                nc.scalar.activation(upper[:], banks[64:P, 6 + i % 2, :], ACT.Copy).then_inc(upper_kept, 1)

            walk(head, tile)
            keep_upper(NT - 1)

    @block.gpsimd
    def _(pool):
        pool.sem_inc(scaled, 1)
        with pool.Fori(0, GROUPS) as g:
            pool.wait_ge(k_hi, g + 1)
            nc.gpsimd.tensor_tensor(kS_lo[:], nsa.kT[:, :, bass.ds(g, 1), :].rearrange("p b g t -> p b (g t)"),
                                    kS_hi[:].bitcast(F32), ALU.subtract).then_inc(k_lo, 1)
            pool.wait_ge(group_copied, g * 2 + 2)
            for J, (branch, i) in enumerate(jobs):
                lo, hi = key_range(branch, i)
                for h in range(HPG):
                    m = J * HPG + h
                    pool.wait_ge(inverted, heads(g, m))
                    pool.sem_inc(pool_go, 1)
                    at = prob[branch][:, h, 0:hi - lo]
                    nc.gpsimd.tensor_scalar(at, at, inv[:, m % 8:m % 8 + 1], gates[:, i, h, 1 + branch:2 + branch],
                                            ALU.mult, ALU.mult).then_inc(scaled, 1)

    @block.vector
    def _(dve):
        for count in (maxed, inverted, lo_done, folded):
            dve.sem_inc(count, 1)
        with dve.Fori(0, GROUPS) as g:
            dve.wait_ge(scaled, heads(g, -1))
            nc.vector.tensor_copy(gates[:].rearrange("p t h c -> p t (h c)"),
                                  chip.gates[:, :, bass.ds(g * (3 * HPG), 3 * HPG)]).then_inc(group_copied, 1)
            dve.wait_ge(multiplied, keys(g, -1))
            nc.vector.tensor_copy(vc[:], nsa.vc[:, bass.ds(g, 1), :].rearrange("n g d -> n (g d)").bitcast(F32)).then_inc(group_copied, 1)
            dve.wait_ge(q_hi, g + 1)
            for a in range(2):
                own, other = slice(64 * a, 64 * a + 64), slice(64 - 64 * a, P - 64 * a)
                last = nc.vector.scalar_tensor_tensor(
                    out=qS[other, a:HPG:2, :], in0=nsa.fT[own, bass.ds(g * 2, 2), :], scalar=SCALE,
                    in1=qS[own, a:HPG:2, :].bitcast(F32), op0=ALU.mult, op1=ALU.subtract)
            last.then_inc(q_lo, 1)
            dve.wait_ge(v_hi, g + 1)
            for b in range(2):
                last = nc.vector.tensor_tensor(vS[:, b, :, DH:P], nsa.v[:, :, bass.ds(g * DH + b * KVW, DH)],
                                               vS[:, b, :, 0:DH].bitcast(F32), ALU.subtract)
            last.then_inc(v_lo, 1)
            waiting = []

            def invert(m):
                dve.wait_ge(expd, heads(g, m))
                if m >= 8:
                    dve.wait_ge(scaled, heads(g, m - 8))
                nc.vector.reciprocal(inv[:, m % 8:m % 8 + 1], den[:, m % 8:m % 8 + 1]).then_inc(inverted, 1)

            def head(J, h):
                branch, i = jobs[J]
                m = J * HPG + h
                lo, hi = key_range(branch, i)
                dve.wait_ge(scored, heads(g, m))
                nc.vector.tensor_reduce(negmax[:, m % 8:m % 8 + 1], pair(slot(m))[:, 0:hi - lo], AX.X, ALU.max,
                                        negate=True).then_inc(maxed, 1)
                if waiting:
                    invert(waiting.pop())
                waiting.append(m)
                if h == HPG - 1:
                    invert(waiting.pop())

            def tile(J, n, key):
                rows = P if key is not None else NCMP
                dve.wait_ge(hi_done, keys(g, n))
                nc.vector.tensor_tensor(pT_lo[n % 2][0:rows, :], banks[0:rows, 4 + n % 2, :],
                                        pT_hi[n % 2][0:rows, :].bitcast(F32), ALU.subtract).then_inc(lo_done, 1)
                branch, i = jobs[J]
                if branch == SLC and i >= 1 and n == tiles[J][0][0]:
                    fold(i - 1)

            def fold(i):
                dve.wait_ge(upper_kept, queries(g, i))
                for a in range(2):
                    pick = lambda ap: ap.rearrange("d (h q) -> d h q", q=P)[:, a:HPG:2, :]
                    last = nc.vector.tensor_tensor(oT[64 * a:64 * a + 64, bass.ds(g * 2, 2), i * P:(i + 1) * P],
                                                   pick(banks[0:64, 6 + i % 2, :]), pick(upper[:]), ALU.add)
                last.then_inc(folded, 1)

            walk(head, tile)
            fold(NT - 1)

    @block.tensor
    def _(pe):
        for count in (scored, turned, multiplied):
            pe.sem_inc(count, 1)
        with pe.Fori(0, GROUPS) as g:
            pe.wait_ge(q_lo, g + 1)
            pe.wait_ge(k_lo, g + 1)
            pe.wait_ge(v_lo, g + 1)
            pe.wait_ge(group_copied, g * 2 + 2)
            pending = []

            def head(J, h):
                branch, i = jobs[J]
                m = J * HPG + h
                lo, hi = key_range(branch, i)
                pe.wait_ge(expd, heads(g, max(m - 2, -1)))
                q = qS[:, h, i * P:(i + 1) * P]
                for c, at in enumerate(range(lo, hi, HALF)):
                    end = min(at + HALF, hi)
                    out = banks[:, 2 * (m % 2) + c, 0:end - at]
                    diagonal = end == hi
                    oldest = branch == WIN and c == 0 and i >= WINDOW // P
                    nc.tensor.matmul(out, q, kS_hi[:, branch, at:end], start=True, stop=False)
                    last = nc.tensor.matmul(out, q, kS_lo[:, branch, at:end], start=False,
                                            stop=not (diagonal or oldest or branch == SLC))
                    if branch == SLC:
                        last = nc.tensor.matmul(out, nsa.selT[:, i * P:(i + 1) * P],
                                                nsa.onehot[:, bass.ds(g, 1), at:end].rearrange("r g k -> r (g k)"),
                                                start=False, stop=not diagonal)
                    if oldest:
                        last = nc.tensor.matmul(out[:, 0:P], chip.ident_bf[:], chip.too_old[:], start=False, stop=not diagonal)
                    if diagonal:
                        last = nc.tensor.matmul(out[:, end - at - P:], chip.ident_bf[:], chip.causal[:], start=False, stop=True)
                last.then_inc(scored, 1)

            def values(J, n, key):
                branch, i = jobs[J]
                rows = P if key is not None else NCMP
                if n == tiles[2 * i][0][0]:
                    pe.wait_ge(folded, queries(g, max(i - 2, -1)))
                pe.wait_ge(hi_done, keys(g, n))
                pe.wait_ge(lo_done, keys(g, n))
                v = vS[:, branch, key, :] if key is not None else vc[:]
                out = banks[:, 6 + i % 2, :]
                nc.tensor.matmul(out, v, pT_hi[n % 2][0:rows, :], start=(n == tiles[2 * i][0][0]), stop=False)
                nc.tensor.matmul(out, v, pT_lo[n % 2][0:rows, :], start=False,
                                 stop=(n == tiles[2 * i + 1][-1][0])).then_inc(multiplied, 1)

            def tile(J, n, key):
                branch, i = jobs[J]
                lo, _ = key_range(branch, i)
                rows = P if key is not None else NCMP
                if key is None:
                    pe.wait_ge(pc_loaded[i % 2], g * (8 * NT) + 16 * (i // 2 + 1))
                elif n == tiles[J][0][0]:
                    pe.wait_ge(scaled, heads(g, (J + 1) * HPG - 1))
                pe.wait_ge(lo_done, keys(g, max(n - 2, -1)))
                if key is None:
                    pe.sem_inc(pe_go, 1)
                for h in range(HPG):
                    source = pc[i % 2][:, h, 0:NCMP] if key is None else prob[branch][:, h, key * P - lo:(key + 1) * P - lo]
                    last = nc.tensor.transpose(banks[0:rows, 4 + n % 2, h * P:(h + 1) * P], source, chip.ident[:])
                last.then_inc(turned, 1)
                if pending:
                    values(*pending.pop())
                pending.append((J, n, key))

            walk(head, tile)
            values(*pending.pop())


def nsa_output_stage(nc, chip, ctx, oT, w_out):
    sem = lambda n: chip.semaphore(f"out_{n}")
    loaded = [sem(f"loaded{b}") for b in range(2)]
    w_hi_done, w_ready, o_hi_done, o_ready, done, kept = (
        sem(n) for n in ("w_hi_done", "w_ready", "o_hi_done", "o_ready", "done", "kept"))
    o_hi = chip.at("out_o_hi", 100, [P, KD, T], F32R)
    o_lo = chip.at("out_o_lo", 132, [P, KD, T], F32R)
    w_hi = chip.at("out_w_hi", 36, [P, KD, D], F32R)
    w_lo = chip.at("out_w_lo", 164, [P, KD, D], F32R)
    raw = [chip.at(f"out_raw{b}", 196 + 4 * b, [P, D]) for b in range(2)]
    block = ctx.enter_context(nc.Block())

    @block.sync
    def _(sp):
        for k in range(KD):
            if k >= 2:
                sp.wait_ge(w_ready, k - 1)
            sp.dma_start(raw[k % 2][:], w_out[k * P:(k + 1) * P, :]).then_inc(loaded[k % 2], 16)

    @block.scalar
    def _(act):
        for k in range(KD):
            nc.scalar.activation(o_hi[:, k, :], oT[:, k, :], ACT.Copy).then_inc(o_hi_done, 1)
            act.wait_ge(loaded[k % 2], 16 * (k // 2 + 1))
            nc.scalar.activation(w_hi[:, k, :], raw[k % 2][:], ACT.Copy).then_inc(w_hi_done, 1)
        for t in range(NT):
            act.wait_ge(done, t + 1)
            b = 2 * (t % 4)
            nc.scalar.activation(chip.y[:, t, :], pair(chip.banks[:, b:b + 2, :]), ACT.Copy).then_inc(kept, 1)

    @block.gpsimd
    def _(pool):
        for k in range(KD):
            pool.wait_ge(w_hi_done, k + 1)
            nc.gpsimd.tensor_tensor(w_lo[:, k, :], raw[k % 2][:], w_hi[:, k, :].bitcast(F32), ALU.subtract).then_inc(w_ready, 1)

    @block.vector
    def _(dve):
        for k in range(KD):
            dve.wait_ge(o_hi_done, k + 1)
            nc.vector.tensor_tensor(o_lo[:, k, :], oT[:, k, :], o_hi[:, k, :].bitcast(F32), ALU.subtract).then_inc(o_ready, 1)

    @block.tensor
    def _(pe):
        for t in range(NT):
            b = 2 * (t % 4)
            if t >= 4:
                pe.wait_ge(kept, t - 3)
            for k in range(KD):
                if t == 0:
                    pe.wait_ge(w_ready, k + 1)
                    pe.wait_ge(o_ready, k + 1)
                for j, (o, w) in enumerate(((o_hi, w_hi), (o_hi, w_lo), (o_lo, w_hi))):
                    for half in range(2):
                        last = nc.tensor.matmul(chip.banks[:, b + half, :], o[:, k, t * P:(t + 1) * P],
                                                w[:, k, half * HALF:(half + 1) * HALF],
                                                start=(k == 0 and j == 0), stop=(k == KD - 1 and j == 2))
            last.then_inc(done, 1)


def build(nc, a, out):
    scratch = lambda name, shape: nc.dram_tensor(name, shape, F32, kind="Internal").ap()
    x_mid = [scratch(f"x_mid{j}", (T, D)) for j in range(3)]
    p_cmp = scratch("p_cmp", (T, HEADS, 64))
    v_normed = scratch("v_normed", (T, E))
    gain = lambda layer, j: a["norm_gains"][4 * layer + j:4 * layer + j + 1, :]
    with ExitStack() as whole:
        chip = Chip(nc, whole)
        nsa = NsaState(chip)
        oT = chip.at("oT", 4, [P, KD, T])

        def stage(build_stage, *args, **kwargs):
            with ExitStack() as ctx:
                build_stage(nc, chip, ctx, *args, **kwargs)
            chip.end_stage()

        stage(constants_stage)
        stage(norm_stage, "norm0", a["x"], pre_gain=gain(0, 0))
        stage(nsa_projection_stage, nsa, a["nsa_w_fm"])
        stage(nsa_value_stage, nsa, a["nsa_w_tok"])
        stage(nsa_compressed_stage, nsa, a["cmp_pe"], a["cmp_w1"], a["cmp_w2"], p_cmp)
        stage(nsa_attention_stage, nsa, p_cmp, oT)
        stage(nsa_output_stage, oT, a["nsa_w_out"])
        stage(norm_stage, "norm1", a["x"], x_out=x_mid[0], post_gain=gain(0, 1), pre_gain=gain(0, 2))
        stage(ffn_stage, "ffn0", a["ffn_w_up"][0], a["ffn_w_down"][0], a["ffn_conv"][0])
        stage(norm_stage, "norm2", x_mid[0], x_out=x_mid[1], post_gain=gain(0, 3), pre_gain=gain(1, 0))
        stage(gmlp_v_stage, a["sg_w_v"], v_normed)
        stage(gmlp_bias_stage, a["sg_w_sp"], a["sg_b_sp"], a["sg_ln_b"])
        stage(gmlp_stage, a["sg_w_u"], a["sg_w_out"], v_normed, a["sg_ln_g"])
        stage(norm_stage, "norm3", x_mid[1], x_out=x_mid[2], post_gain=gain(1, 1), pre_gain=gain(1, 2))
        stage(ffn_stage, "ffn1", a["ffn_w_up"][1], a["ffn_w_down"][1], a["ffn_conv"][1])
        stage(norm_stage, "norm4", x_mid[2], x_out=out, post_gain=gain(1, 3))


def lay_out(i):
    import numpy as np

    i = {k: np.asarray(v) for k, v in i.items()}
    flat = np.ascontiguousarray
    w_in = i["nsa_w_in"][0]
    q, kc, vc, ks, vs, kw, vw, gl = np.split(w_in, [HEADS * DH + k * KVW for k in range(7)], axis=1)
    piece = lambda w: w.reshape(KD, P, -1).transpose(1, 0, 2).reshape(P, -1)
    columns = lambda w: flat(w.reshape(KD, P, -1, P).transpose(2, 1, 0, 3).reshape(-1, P, KD * P))
    rows2 = lambda w: flat(w.reshape(-1, 2, P, D).transpose(0, 2, 1, 3).reshape(-1, P, 2 * D))
    sg_in = i["sg_w_in"][0]
    layers = i["ffn_w_up"].shape[0]
    conv = np.concatenate([i["ffn_conv_w"], i["ffn_conv_b"][:, None]], axis=1)
    return {
        "x": i["x"][0],
        "norm_gains": i["norm_gains"].reshape(-1, D),
        "nsa_w_fm": columns(np.concatenate([q, kc, vc, ks, kw], axis=1)),
        "nsa_w_tok": flat(np.concatenate([piece(vs), piece(vw), piece(gl)], axis=1)),
        "cmp_pe": flat(i["nsa_cmp_pe"][0].transpose(2, 0, 1)),
        "cmp_w1": flat(i["nsa_cmp_w1"][0].reshape(2, CMP_LEN, DH, DH).transpose(0, 2, 1, 3)),
        "cmp_w2": i["nsa_cmp_w2"][0],
        "nsa_w_out": i["nsa_w_out"][0],
        "sg_w_v": flat(sg_in[:, E:].reshape(4, 2, P, 4, HALF).transpose(3, 0, 2, 1, 4).reshape(16, P, 2 * HALF)),
        "sg_w_u": columns(sg_in[:, :E]),
        "sg_ln_g": flat(i["sg_ln_g"][0].reshape(KE, P).T),
        "sg_ln_b": i["sg_ln_b"][0].reshape(1, E),
        "sg_w_sp": flat(i["sg_w_sp"][0].transpose(2, 0, 1).reshape(P, KE * P)),
        "sg_b_sp": i["sg_b_sp"][0].reshape(1, KE * P),
        "sg_w_out": rows2(i["sg_w_out"][0]),
        "ffn_w_up": flat(i["ffn_w_up"].reshape(layers, KD, P, 2, KF, P).transpose(0, 4, 2, 3, 1, 5).reshape(layers, KF, P, -1)),
        "ffn_w_down": np.stack([rows2(w) for w in i["ffn_w_down"]]),
        "ffn_conv": flat(conv.reshape(layers, 4, 2, KF, P).transpose(0, 4, 3, 2, 1)),
    }


def kernel(**inputs):
    import numpy as np
    import concourse.bacc as bacc
    from concourse.bass_utils import run_bass_kernel_spmd

    nc = bacc.Bacc("TRN2", target_bir_lowering=False, num_devices=1)
    arrays = {f"in_{name}": np.ascontiguousarray(v) for name, v in lay_out(inputs).items()}
    args = {name[3:]: nc.dram_tensor(name, v.shape, mybir.dt.from_np(v.dtype), kind="ExternalInput").ap()
            for name, v in arrays.items()}
    out = nc.dram_tensor("out", (T, D), F32, kind="ExternalOutput").ap()
    build(nc, args, out)
    result = run_bass_kernel_spmd(nc, [arrays], core_ids=[0])
    return result.results[0]["out"].reshape(1, T, D)
```

```python
from contextlib import ExitStack

import concourse.bass as bass
from concourse import mybir

ALU = mybir.AluOpType
ACT = mybir.ActivationFunctionType
AX = mybir.AxisListType
F32 = mybir.dt.float32
F32R = mybir.dt.float32r
BF16 = mybir.dt.bfloat16

P = 128
D = 1024
T = 1024
NT = T // P
KD = D // P
HALF = 512
EPS = 1e-6
HEADS, GROUPS, DH = 16, 4, 64
HPG = HEADS // GROUPS
SCALE = DH ** -0.5
CMP_LEN, CMP_STRIDE = 32, 16
NCMP = (T - CMP_LEN) // CMP_STRIDE + 1
SLC_LEN, TOPN, WINDOW = 64, 8, 512
NSLC = T // SLC_LEN
FORCE, NEG = 1.0e4, -1.0e30
GATES = 3 * HEADS
KVW = GROUPS * DH
F = 2816
KF = F // P
E = 2 * D
KE = E // P
FM_TILES = (HEADS * DH + 4 * KVW) // P
BASE = 16640

CONST_AT, H_AT, Y_AT, WORK = 0, 4, 68, 100
GMLP_AT = 182


class Chip:

    def __init__(self, nc, ctx):
        self.nc, self.tensors, self.in_stage = nc, {}, []
        self.banks = ctx.enter_context(nc.psum_tensor("banks", [P, 8, HALF], F32))
        self.ident = self.at("ident", CONST_AT, [P, P])
        self.ident_bf = self.at("ident_bf", CONST_AT + 0.5, [P, P], BF16)
        self.causal = self.at("causal", CONST_AT + 0.75, [P, P], BF16)
        self.too_old = self.at("too_old", CONST_AT + 1.0, [P, P], BF16)
        self.eps = self.at("eps", CONST_AT + 1.25, [P, 1])
        self.gates = self.at("gates", CONST_AT + 1.5, [P, NT, GATES])
        self.hT = [self.at(n, H_AT + 32 * j, [P, KD, T], F32R) for j, n in enumerate(("hT_hi", "hT_lo"))]
        self.y = self.at("y", Y_AT, [P, NT, D])
        self.w_spT = self.at("w_spT", GMLP_AT, [P, KE, P])
        self.sg_bias = self.at("sg_bias", GMLP_AT + 8, [P, KE, P])

    def semaphore(self, name):
        self.in_stage.append(self.nc.alloc_semaphore(name=name))
        return self.in_stage[-1]

    def end_stage(self):
        self.nc.clear_and_free_semaphores(self.in_stage)
        self.nc.all_engine_barrier()
        self.in_stage = []

    def at(self, name, kb, shape, dt=F32):
        if name not in self.tensors:
            self.tensors[name] = self.nc.alloc_sbuf_tensor_at(name, shape, dt, offset=BASE + int(kb * 1024))
        return self.tensors[name]


def pair(ap):
    return ap.rearrange("p a c -> p (a c)")


def constants_stage(nc, chip, ctx):
    filled, cut = (chip.semaphore(f"const_{n}") for n in ("filled", "cut"))
    block = ctx.enter_context(nc.Block())

    @block.gpsimd
    def _(pool):
        nc.gpsimd.memset(chip.eps[:], EPS)
        for m in (chip.ident, chip.ident_bf, chip.causal, chip.too_old):
            nc.gpsimd.memset(m[:], 0.0).then_inc(filled, 1)
        pool.wait_ge(filled, 4)
        for m in (chip.ident, chip.ident_bf):
            nc.gpsimd.affine_select(out=m[:], in_=m[:], compare_op=ALU.not_equal, fill=1.0, base=0,
                                    pattern=[[-1, P]], channel_multiplier=1).then_inc(cut, 1)
        nc.gpsimd.affine_select(out=chip.causal[:], in_=chip.causal[:], compare_op=ALU.is_ge, fill=NEG, base=0,
                                pattern=[[-1, P]], channel_multiplier=1).then_inc(cut, 1)
        nc.gpsimd.affine_select(out=chip.too_old[:], in_=chip.too_old[:], compare_op=ALU.is_gt, fill=NEG, base=0,
                                pattern=[[1, P]], channel_multiplier=-1).then_inc(cut, 1)
        pool.wait_ge(cut, 4)


class Norm:
    PER_LOAD = 2

    def __init__(self, nc, chip, tag, x_in, x_out=None, post_gain=None, pre_gain=None, y_done=None,
                 x_at=WORK, rest_at=WORK + 32, lag=4):
        sem = lambda n: chip.semaphore(f"{tag}_{n}")
        self.nc, self.chip, self.x_in, self.x_out, self.y_done = nc, chip, x_in, x_out, y_done
        self.post_gain, self.pre_gain, self.lag = post_gain, pre_gain, lag
        self.x_loaded = [sem(f"x_loaded{j}") for j in range(NT // self.PER_LOAD)]
        self.gains_loaded, self.x_stored = sem("gains_loaded"), sem("x_stored")
        self.y_squared, self.y_root, self.y_inverse, self.y_normed = (
            sem("y_squared"), sem("y_root"), sem("y_inverse"), sem("y_normed"))
        self.x_new, self.x_squared, self.x_root, self.x_inverse = (
            sem("x_new"), sem("x_squared"), sem("x_root"), sem("x_inverse"))
        self.x_normed, self.turned, self.hi_done, self.lo_done = (
            sem("x_normed"), sem("turned"), sem("hi_done"), sem("lo_done"))
        self.x = chip.at(f"norm_x_{x_at}", x_at, [P, NT, D])
        self.g_post = chip.at(f"norm_g_post_{rest_at}", rest_at, [P, D])
        self.g_pre = chip.at(f"norm_g_pre_{rest_at}", rest_at + 4, [P, D])
        self.junk = chip.at(f"norm_junk_{rest_at}", rest_at + 8, [P, D], BF16)
        self.stats = chip.at(f"norm_stats_{rest_at}", rest_at + 10, [P, 6, NT])
        self.gains = 16 * ((post_gain is not None) + (pre_gain is not None))

    def stat(self, j, n):
        return self.stats[:, j, n:n + 1]

    def sync(self, sp):
        m = self.PER_LOAD
        if self.post_gain is not None:
            sp.dma_start(self.g_post[:], self.post_gain.broadcast_to([P, D])).then_inc(self.gains_loaded, 16)
        for j in range(NT // m):
            sp.dma_start(self.x[:, m * j:m * j + m, :],
                         self.x_in[m * j * P:m * (j + 1) * P, :].rearrange("(n p) d -> p n d", p=P)).then_inc(self.x_loaded[j], 16)
            if j == 0 and self.pre_gain is not None:
                sp.dma_start(self.g_pre[:], self.pre_gain.broadcast_to([P, D])).then_inc(self.gains_loaded, 16)
        if self.x_out is not None:
            for n in range(NT):
                sp.wait_ge(self.x_new, n + 1)
                sp.dma_start(self.x_out[n * P:(n + 1) * P, :], self.x[:, n, :]).then_inc(self.x_stored, 16)
            sp.wait_ge(self.x_stored, 16 * NT)

    def scalar(self, act, before=None):
        nc, chip, y, x = self.nc, self.chip, self.chip.y, self.x
        done = [0]

        def root_mean_square(j, source, squared, root, n):
            if done[0]:
                act.wait_ge(*done[1])
            nc.scalar.activation(self.junk[:], source, ACT.Square, accum_out=self.stat(j, n)).then_inc(squared, 1)
            act.wait_ge(squared, n + 1)
            nc.scalar.activation(self.stat(j + 1, n), self.stat(j, n), ACT.Sqrt, bias=chip.eps[:, 0:1],
                                 scale=1.0 / D).then_inc(root, 1)
            done[:] = [1, (squared, n + 1)]

        for s in range(NT + self.lag):
            if before is not None and s < NT:
                before(s)
            if self.post_gain is not None and s < NT:
                if self.y_done is not None:
                    act.wait_ge(self.y_done[0], self.y_done[1] + s + 1)
                root_mean_square(0, y[:, s, :], self.y_squared, self.y_root, s)
            n = s - 2
            if self.pre_gain is not None and 0 <= n < NT:
                if self.post_gain is not None:
                    act.wait_ge(self.x_new, n + 1)
                else:
                    act.wait_ge(self.x_loaded[n // self.PER_LOAD], 16)
                root_mean_square(3, x[:, n, :], self.x_squared, self.x_root, n)
            n = s - self.lag
            if self.pre_gain is not None and 0 <= n < NT:
                act.wait_ge(self.turned, n + 1)
                b = 2 * (n % 2)
                nc.scalar.activation(chip.hT[0][:, :, n * P:(n + 1) * P],
                                     chip.banks[:, b:b + 2, :].rearrange("p a (k t) -> p (a k) t", t=P),
                                     ACT.Copy).then_inc(self.hi_done, 1)

    def gpsimd(self, pool):
        if self.post_gain is None:
            return
        for n in range(NT):
            if n % self.PER_LOAD == 0:
                pool.wait_ge(self.x_loaded[n // self.PER_LOAD], 16)
            pool.wait_ge(self.y_normed, n + 1)
            self.nc.gpsimd.tensor_tensor(self.x[:, n, :], self.x[:, n, :], self.chip.y[:, n, :], ALU.add).then_inc(self.x_new, 1)

    def vector(self, dve, before=None):
        nc, chip, y, x = self.nc, self.chip, self.chip.y, self.x
        hT_hi, hT_lo = chip.hT

        def normed(j, source, root, inverse, gain, done, n):
            dve.wait_ge(root, n + 1)
            nc.vector.reciprocal(self.stat(j + 2, n), self.stat(j + 1, n)).then_inc(inverse, 1)
            dve.wait_ge(inverse, n + 1)
            nc.vector.scalar_tensor_tensor(out=y[:, n, :], in0=source, scalar=self.stat(j + 2, n), in1=gain[:],
                                           op0=ALU.mult, op1=ALU.mult).then_inc(done, 1)

        for s in range(NT + self.lag + 1):
            if before is not None and s < NT:
                before(s)
            if s == 0:
                dve.wait_ge(self.gains_loaded, self.gains)
            if self.post_gain is not None and 0 <= s - 1 < NT:
                normed(0, y[:, s - 1, :], self.y_root, self.y_inverse, self.g_post, self.y_normed, s - 1)
            if self.pre_gain is not None and 0 <= s - 3 < NT:
                normed(3, x[:, s - 3, :], self.x_root, self.x_inverse, self.g_pre, self.x_normed, s - 3)
            n = s - self.lag - 1
            if self.pre_gain is not None and 0 <= n < NT:
                dve.wait_ge(self.hi_done, n + 1)
                b = 2 * (n % 2)
                nc.vector.tensor_tensor(hT_lo[:, :, n * P:(n + 1) * P],
                                        chip.banks[:, b:b + 2, :].rearrange("p a (k t) -> p (a k) t", t=P),
                                        hT_hi[:, :, n * P:(n + 1) * P].bitcast(F32), ALU.subtract).then_inc(self.lo_done, 1)

    def tensor(self, pe):
        if self.pre_gain is None:
            return
        for n in range(NT):
            pe.wait_ge(self.x_normed, n + 1)
            if n >= 2:
                pe.wait_ge(self.lo_done, n - 1)
            for k in range(KD):
                last = self.nc.tensor.transpose(self.chip.banks[:, 2 * (n % 2) + k // 4, (k % 4) * P:(k % 4 + 1) * P],
                                                self.chip.y[:, n, k * P:(k + 1) * P], self.chip.ident[:])
            last.then_inc(self.turned, 1)


def first_norm_stage(nc, chip, ctx, norm):
    norm = Norm(nc, chip, **norm)
    block = ctx.enter_context(nc.Block())

    @block.sync
    def _(sp):
        norm.sync(sp)

    @block.scalar
    def _(act):
        norm.scalar(act)

    @block.vector
    def _(dve):
        norm.vector(dve)

    @block.tensor
    def _(pe):
        norm.tensor(pe)


def feature_major_product(nc, chip, first_bank, w_hi, w_lo):
    hT_hi, hT_lo = chip.hT
    for k in range(KD):
        for j, (w, h) in enumerate(((w_hi, hT_hi), (w_hi, hT_lo), (w_lo, hT_hi))):
            for half in range(2):
                last = nc.tensor.matmul(chip.banks[:, first_bank + half, :], w[:, k, :],
                                        h[:, k, half * HALF:(half + 1) * HALF],
                                        start=(k == 0 and j == 0), stop=(k == KD - 1 and j == 2))
    return last


def ffn_stage(nc, chip, ctx, tag, w_up, w_down, conv, norm):
    sem = lambda n: chip.semaphore(f"{tag}_{n}")
    ROUNDS = KF // 2
    up_loaded = [sem(f"up_loaded_{c}") for c in "ab"]
    down_loaded, conv_loaded = sem("down_loaded"), sem("conv_loaded")
    up_w_hi, up_w_ready = sem("up_w_hi"), sem("up_w_ready")
    down_w_hi, down_w_ready = sem("down_w_hi"), sem("down_w_ready")
    up_done = [sem(f"up_done_{c}") for c in "gv"]
    centre = [sem(f"centre_{c}") for c in "gv"]
    cur_ready = sem("cur_ready")
    conv_step, gated_ready, prod_ready = sem("conv_step"), sem("gated_ready"), sem("prod_ready")
    conv_done = [sem(f"conv_done_{c}") for c in "gv"]
    prod_hi, prod_split = sem("prod_hi"), sem("prod_split")
    down_done, y_free = sem("down_done"), sem("y_free")

    raw_up = [chip.at(f"ffn_raw_up{c}", WORK + 8 * j, [P, 2, KD, P]) for j, c in enumerate("ab")]
    raw_down = chip.at("ffn_raw_down", WORK + 48, [P, 2, D])
    up_hi = [chip.at(f"ffn_up_hi{c}", WORK + 16 + 16 * j, [P, 2, KD, P], F32R) for j, c in enumerate("ab")]
    up_lo = [chip.at(f"ffn_up_lo{c}", WORK + 24 + 16 * j, [P, 2, KD, P], F32R) for j, c in enumerate("ab")]
    down_hi = chip.at(f"ffn_down_hi", WORK + 56, [P, 2, D], F32R)
    down_lo = chip.at(f"ffn_down_lo", WORK + 64, [P, 2, D], F32R)
    p_hi = [chip.at(f"ffn_p_hi{c}", WORK + 72 + 8 * j, [P, T], F32R) for j, c in enumerate("ab")]
    p_lo = [chip.at(f"ffn_p_lo{c}", WORK + 76 + 8 * j, [P, T], F32R) for j, c in enumerate("ab")]
    cg = [chip.at(f"ffn_conv_{c}", WORK + 88 + 4 * j, [P, T]) for j, c in enumerate("gv")]
    prod = chip.at(f"ffn_prod", WORK + 96, [P, T])
    cw = chip.at(f"ffn_cw", WORK + 100, [P, KF, 2, 4])
    cur = [chip.at(f"ffn_cur{j}", WORK + 101 + 0.125 * j, [P, 2, 4]) for j in range(2)]
    banks, y = chip.banks, chip.y
    up_bank = [banks[:, 0:2, :], banks[:, 2:4, :]]
    norm = Norm(nc, chip, y_done=(y_free, (ROUNDS - 1) * NT + 2), **norm)
    block = ctx.enter_context(nc.Block())

    @block.sync
    def _(sp):
        def load_up(c, n, wait=None):
            if wait is not None:
                sp.wait_ge(up_w_ready, wait)
            sp.dma_start(raw_up[c][:], w_up[n].rearrange("p (s k c) -> p s k c", s=2, k=KD)).then_inc(up_loaded[c], 16)

        def load_down(i, wait=None):
            if wait is not None:
                sp.wait_ge(down_w_ready, wait)
            sp.dma_start(raw_down[:], w_down[i].rearrange("p (s n) -> p s n", s=2)).then_inc(down_loaded, 16)

        load_up(0, 0)
        sp.dma_start(cw[:], conv).then_inc(conv_loaded, 16)
        load_up(1, 1)
        load_down(0)
        with sp.Fori(0, ROUNDS - 1) as i:
            load_up(0, i * 2 + 2, wait=i * 2 + 1)
            load_up(1, i * 2 + 3, wait=i * 2 + 2)
            load_down(i + 1, wait=i + 1)
        sp.wait_ge(prod_split, KF)
        sp.wait_ge(down_w_ready, ROUNDS)
        norm.sync(sp)

    @block.scalar
    def _(act):
        def split_up(c, n, wait=None):
            act.wait_ge(up_loaded[c], (n - c) * 8 + 16)
            if wait is not None:
                act.wait_ge(up_done[1], wait)
            nc.scalar.activation(up_hi[c][:], raw_up[c][:], ACT.Copy).then_inc(up_w_hi, 1)

        def split_down(i, wait=None):
            act.wait_ge(down_loaded, i * 16 + 16)
            if wait is not None:
                act.wait_ge(down_done, wait)
            nc.scalar.activation(down_hi[:], raw_down[:], ACT.Copy).then_inc(down_w_hi, 1)

        def convolved(c, n):
            for s in range(2):
                act.wait_ge(up_done[s], n + 1)
                if s == 1:
                    act.wait_ge(prod_ready, n)
                act.wait_ge(cur_ready, n + 1)
                nc.scalar.activation(cg[s][:], pair(up_bank[s]), ACT.Identity, bias=cur[c][:, s, 3:4],
                                     scale=cur[c][:, s, 2:3]).then_inc(centre[s], 1)
            act.wait_ge(conv_done[0], n + 1)
            act.wait_ge(prod_split, n)
            nc.scalar.activation(prod[:], cg[0][:], ACT.Silu).then_inc(gated_ready, 1)

        def product_hi(c, n, wait=None):
            act.wait_ge(prod_ready, n + 1)
            if wait is not None:
                act.wait_ge(down_done, wait)
            nc.scalar.activation(p_hi[c][:], prod[:], ACT.Copy).then_inc(prod_hi, 1)

        split_up(0, 0)
        split_up(1, 1)
        convolved(0, 0)
        product_hi(0, 0)
        split_down(0)
        with act.Fori(0, ROUNDS - 1) as i:
            split_up(0, i * 2 + 2, wait=i * 2 + 1)
            convolved(1, i * 2 + 1)
            product_hi(1, i * 2 + 1)
            split_up(1, i * 2 + 3, wait=i * 2 + 2)
            convolved(0, i * 2 + 2)
            product_hi(0, i * 2 + 2, wait=i * NT + NT)
            split_down(i + 1, wait=i * NT + NT)
        convolved(1, KF - 1)
        product_hi(1, KF - 1)
        norm.scalar(act)

    @block.gpsimd
    def _(pool):
        def up_low(c, n):
            pool.wait_ge(up_w_hi, n + 1)
            nc.gpsimd.tensor_tensor(up_lo[c][:], raw_up[c][:], up_hi[c][:].bitcast(F32), ALU.subtract).then_inc(up_w_ready, 1)

        def down_low(i):
            pool.wait_ge(down_w_hi, i + 1)
            nc.gpsimd.tensor_tensor(down_lo[:], raw_down[:], down_hi[:].bitcast(F32), ALU.subtract).then_inc(down_w_ready, 1)

        def product_low(c, n):
            pool.wait_ge(prod_hi, n + 1)
            nc.gpsimd.tensor_tensor(p_lo[c][:], prod[:], p_hi[c][:].bitcast(F32), ALU.subtract).then_inc(prod_split, 1)

        up_low(0, 0)
        up_low(1, 1)
        product_low(0, 0)
        down_low(0)
        with pool.Fori(0, ROUNDS - 1) as i:
            up_low(0, i * 2 + 2)
            product_low(1, i * 2 + 1)
            up_low(1, i * 2 + 3)
            product_low(0, i * 2 + 2)
            down_low(i + 1)
        product_low(1, KF - 1)
        norm.gpsimd(pool)

    @block.vector
    def _(dve):
        def fetch_taps(c, n):
            nc.vector.tensor_copy(cur[c][:], cw[:, bass.ds(n, 1), :, :].rearrange("p a s j -> p (a s) j")).then_inc(cur_ready, 1)

        def convolve(c, n):
            dve.wait_ge(cur_ready, n + 1)
            for s in range(2):
                dve.wait_ge(centre[s], n + 1)
                h = pair(up_bank[s])
                nc.vector.scalar_tensor_tensor(out=cg[s][:, 1:T], in0=h[:, 0:T - 1], scalar=cur[c][:, s, 1:2],
                                               in1=cg[s][:, 1:T], op0=ALU.mult, op1=ALU.add).then_inc(conv_step, 1)
                dve.wait_ge(conv_step, n * 2 + (s + 1))
                nc.vector.scalar_tensor_tensor(out=cg[s][:, 2:T], in0=h[:, 0:T - 2], scalar=cur[c][:, s, 0:1],
                                               in1=cg[s][:, 2:T], op0=ALU.mult, op1=ALU.add).then_inc(conv_done[s], 1)
            dve.wait_ge(gated_ready, n + 1)
            dve.wait_ge(conv_done[1], n + 1)
            nc.vector.tensor_tensor(prod[:], prod[:], cg[1][:], ALU.mult).then_inc(prod_ready, 1)

        def add_down(i, t):
            dve.wait_ge(down_done, i * NT + (t + 1))
            b = 4 + 2 * (t % 2)
            nc.vector.tensor_tensor(y[:, t, :], y[:, t, :], pair(banks[:, b:b + 2, :]), ALU.add).then_inc(y_free, 1)

        dve.wait_ge(conv_loaded, 16)
        nc.vector.memset(y[:], 0.0).then_inc(y_free, 2)
        dve.wait_ge(y_free, 2)
        fetch_taps(0, 0)
        fetch_taps(1, 1)
        convolve(0, 0)
        with dve.Fori(0, ROUNDS - 1) as i:
            fetch_taps(0, i * 2 + 2)
            convolve(1, i * 2 + 1)
            fetch_taps(1, i * 2 + 3)
            convolve(0, i * 2 + 2)
            dve.wait_ge(y_free, i * NT + 2)
            for t in range(NT):
                add_down(i, t)
        convolve(1, KF - 1)
        dve.wait_ge(y_free, (ROUNDS - 1) * NT + 2)
        norm.vector(dve, before=lambda t: add_down(ROUNDS - 1, t))

    @block.tensor
    def _(pe):
        def up(c, n):
            pe.wait_ge(up_w_ready, n + 1)
            for s in range(2):
                pe.wait_ge(conv_done[s], n)
                feature_major_product(nc, chip, 2 * s, up_hi[c][:, s], up_lo[c][:, s]).then_inc(up_done[s], 1)

        up(0, 0)
        with pe.Fori(0, ROUNDS - 1) as i:
            up(1, i * 2 + 1)
            up(0, i * 2 + 2)
            down_product(nc, chip, pe, i, p_hi, p_lo, down_hi, down_lo, prod_split, down_w_ready, y_free, down_done)
        up(1, KF - 1)
        down_product(nc, chip, pe, ROUNDS - 1, p_hi, p_lo, down_hi, down_lo, prod_split, down_w_ready, y_free, down_done)
        norm.tensor(pe)


def down_product(nc, chip, pe, i, p_hi, p_lo, w_hi, w_lo, prod_split, w_ready, y_free, down_done):
    pe.wait_ge(w_ready, i + 1)
    pe.wait_ge(prod_split, i * 2 + 2)
    for t in range(NT):
        pe.wait_ge(y_free, i * NT + (t + 1))
        b = 4 + 2 * (t % 2)
        for c in range(2):
            for j, (p, w) in enumerate(((p_hi, w_hi), (p_hi, w_lo), (p_lo, w_hi))):
                for half in range(2):
                    last = nc.tensor.matmul(chip.banks[:, b + half, :], p[c][:, t * P:(t + 1) * P],
                                            w[:, c, half * HALF:(half + 1) * HALF],
                                            start=(c == 0 and j == 0), stop=(c == 1 and j == 2))
        last.then_inc(down_done, 1)


def gmlp_bias_stage(nc, chip, ctx, w_sp, b_sp, ln_b):
    sem = lambda n: chip.semaphore(f"bias_{n}")
    loaded, masked, ones_set, summed, sums_kept, spread, kept = (
        sem(n) for n in ("loaded", "masked", "ones_set", "summed", "sums_kept", "spread", "kept"))
    ones = chip.at("bias_ones", WORK, [P, P])
    rows = chip.at("bias_rows", WORK + 1, [1, 3, E])
    w_spT, bias = chip.w_spT, chip.sg_bias
    ln_row, sp_row, sum_row = (rows[0:1, j, :] for j in range(3))
    block = ctx.enter_context(nc.Block())

    @block.sync
    def _(sp):
        sp.dma_start(w_spT[:], w_sp.rearrange("s (g t) -> s g t", g=KE)).then_inc(loaded, 16)
        sp.dma_start(ln_row, ln_b).then_inc(loaded, 16)
        sp.dma_start(sp_row, b_sp).then_inc(loaded, 16)

    @block.gpsimd
    def _(pool):
        nc.gpsimd.memset(ones[:], 1.0).then_inc(ones_set, 1)
        pool.wait_ge(loaded, 48)
        nc.gpsimd.affine_select(out=w_spT[:], in_=w_spT[:], compare_op=ALU.is_ge, fill=0.0, base=0,
                                pattern=[[0, KE], [1, P]], channel_multiplier=-1).then_inc(masked, 1)

    @block.tensor
    def _(pe):
        pe.wait_ge(ones_set, 1)
        pe.wait_ge(masked, 1)
        for b in range(4):
            last = nc.tensor.matmul(chip.banks[0:1, b, :], ones[:, 0:1],
                                    w_spT[:, 4 * b:4 * b + 4, :].rearrange("s g t -> s (g t)"), start=True, stop=True)
        last.then_inc(summed, 1)
        pe.wait_ge(sums_kept, 1)
        for g in range(KE):
            at = chip.banks[:, 4 + g // 4, (g % 4) * P:(g % 4 + 1) * P]
            cols = slice(g * P, (g + 1) * P)
            nc.tensor.matmul(at, ln_row[:, cols], sum_row[:, cols], start=True, stop=False)
            last = nc.tensor.matmul(at, ones[0:1, :], sp_row[:, cols], start=False, stop=True)
        last.then_inc(spread, 1)

    @block.vector
    def _(dve):
        dve.wait_ge(summed, 1)
        nc.vector.tensor_copy(sum_row, pair(chip.banks[0:1, 0:4, :])).then_inc(sums_kept, 1)
        dve.wait_ge(spread, 1)
        nc.vector.tensor_copy(bias[:].rearrange("p g t -> p (g t)"), pair(chip.banks[:, 4:8, :])).then_inc(kept, 1)


def gmlp_v_stage(nc, chip, ctx, w_v, v_out):
    sem = lambda n: chip.semaphore(f"v_{n}")
    CHUNKS, PIECES, KP = E // HALF, 4, 2
    raw_loaded = [sem(f"raw_loaded{b}") for b in range(2)]
    w_hi_done, w_ready, v_done, gelu_done = sem("w_hi_done"), sem("w_ready"), sem("v_done"), sem("gelu_done")
    counted, averaged, root_done, inverse_done = sem("counted"), sem("averaged"), sem("root_done"), sem("inverse_done")
    v_normed, v_stored = sem("v_normed"), sem("v_stored")
    v = chip.at("v", Y_AT, [P, NT, E])
    w_hi = chip.at("v_w_hi", Y_AT + 64, [P, 2, KD, HALF], F32R)
    w_lo = chip.at("v_w_lo", Y_AT + 96, [P, 2, KD, HALF], F32R)
    raw = [chip.at(f"v_raw{b}", Y_AT + 128 + 4 * b, [P, KP, HALF]) for b in range(2)]
    stats = chip.at("v_stats", Y_AT + 136, [P, NT, CHUNKS, 6])
    mean_var = chip.at("v_mean_var", Y_AT + 137, [P, NT, 2])
    dev = chip.at("v_dev", Y_AT + 137.25, [P, NT])
    inv = chip.at("v_inv", Y_AT + 137.5, [P, NT])
    hT_hi, hT_lo = chip.hT
    block = ctx.enter_context(nc.Block())

    @block.sync
    def _(sp):
        for q in range(2):
            sp.dma_start(raw[q][:], w_v[q].rearrange("p (k n) -> p k n", k=KP)).then_inc(raw_loaded[q], 16)
        with sp.Fori(0, CHUNKS * PIECES // 2 - 1) as i:
            for q in range(2):
                sp.wait_ge(w_ready, i * 2 + (q + 1))
                sp.dma_start(raw[q][:], w_v[i * 2 + (q + 2)].rearrange("p (k n) -> p k n", k=KP)).then_inc(raw_loaded[q], 16)
        for t in range(NT):
            sp.wait_ge(v_normed, t + 1)
            sp.dma_start(v_out[t * P:(t + 1) * P, :], v[:, t, :]).then_inc(v_stored, 16)
        sp.wait_ge(v_stored, 16 * NT)

    @block.scalar
    def _(act):
        def split(c, wait=None):
            if wait is not None:
                act.wait_ge(v_done, wait)
            for q in range(PIECES):
                act.wait_ge(raw_loaded[q % 2], c * 32 + (q // 2 + 1) * 16)
                nc.scalar.activation(w_hi[:, bass.ds(c % 2, 1), KP * q:KP * (q + 1), :].rearrange("p a k n -> p (a k) n"),
                                     raw[q % 2][:], ACT.Copy).then_inc(w_hi_done, 1)

        def gelu(c):
            for t in range(NT):
                act.wait_ge(v_done, c * NT + (t + 2))
                nc.scalar.activation(v[:, t, bass.ds(c * HALF, HALF)], chip.banks[:, t, :],
                                     ACT.Gelu_apprx_tanh).then_inc(gelu_done, 1)

        act.sem_inc(gelu_done, 1)
        split(0)
        with act.Fori(0, CHUNKS - 1) as c:
            split(c + 1, wait=c * NT + 1)
            gelu(c)
        gelu(CHUNKS - 1)
        act.wait_ge(averaged, NT)
        nc.scalar.activation(dev[:], mean_var[:, :, 1], ACT.Sqrt, bias=chip.eps[:, 0:1]).then_inc(root_done, 1)

    @block.gpsimd
    def _(pool):
        with pool.Fori(0, CHUNKS) as c:
            for q in range(PIECES):
                pool.wait_ge(w_hi_done, c * PIECES + (q + 1))
                at = lambda w: w[:, bass.ds(c % 2, 1), KP * q:KP * (q + 1), :].rearrange("p a k n -> p (a k) n")
                nc.gpsimd.tensor_tensor(at(w_lo), raw[q % 2][:], at(w_hi).bitcast(F32), ALU.subtract).then_inc(w_ready, 1)

    @block.vector
    def _(dve):
        with dve.Fori(0, CHUNKS) as c:
            for t in range(NT):
                dve.wait_ge(gelu_done, c * NT + (t + 2))
                nc.vector.bn_stats(stats[:, t, bass.ds(c, 1), :].rearrange("p a s -> p (a s)"),
                                   v[:, t, bass.ds(c * HALF, HALF)]).then_inc(counted, 1)
        dve.wait_ge(counted, CHUNKS * NT)
        for t in range(NT):
            nc.vector.bn_aggr(mean_var[:, t, :], stats[:, t]).then_inc(averaged, 1)
        dve.wait_ge(root_done, 1)
        nc.vector.reciprocal(inv[:], dev[:]).then_inc(inverse_done, 1)
        dve.wait_ge(inverse_done, 1)
        for t in range(NT):
            nc.vector.tensor_scalar(v[:, t, :], v[:, t, :], mean_var[:, t, 0:1], inv[:, t:t + 1],
                                    ALU.subtract, ALU.mult).then_inc(v_normed, 1)

    @block.tensor
    def _(pe):
        pe.sem_inc(v_done, 1)
        with pe.Fori(0, CHUNKS) as c:
            pe.wait_ge(w_ready, c * PIECES + PIECES)
            half = c % 2
            for t in range(NT):
                pe.wait_ge(gelu_done, c * NT + 1)
                for k in range(KD):
                    for j, (h, w) in enumerate(((hT_hi, w_hi), (hT_hi, w_lo), (hT_lo, w_hi))):
                        last = nc.tensor.matmul(chip.banks[:, t, :], h[:, k, t * P:(t + 1) * P],
                                                w[:, bass.ds(half, 1), k, :].rearrange("p a n -> p (a n)"),
                                                start=(k == 0 and j == 0), stop=(k == KD - 1 and j == 2))
                last.then_inc(v_done, 1)


def gmlp_stage(nc, chip, ctx, w_u, w_down, v_in, ln_g, norm):
    sem = lambda n: chip.semaphore(f"sg_{n}")
    ROUNDS = KE // 2
    up_loaded, v_loaded = ([sem(f"{n}_{c}") for c in "ab"] for n in ("up_loaded", "v_loaded"))
    down_loaded, gain_loaded = sem("down_loaded"), sem("gain_loaded")
    up_w_hi, up_w_ready, down_w_hi, down_w_ready = sem("up_w_hi"), sem("up_w_ready"), sem("down_w_hi"), sem("down_w_ready")
    u_done, mix_done, gelu_done, cur_ready, mix_biased = (
        sem("u_done"), sem("mix_done"), sem("gelu_done"), sem("cur_ready"), sem("mix_biased"))
    prod_ready, prod_hi, prod_split = sem("prod_ready"), sem("prod_hi"), sem("prod_split")
    down_done, y_free = sem("down_done"), sem("y_free")

    raw_up = [chip.at(f"sg_raw_up{c}", WORK + 4 * j, [P, KD, P]) for j, c in enumerate("ab")]
    raw_down = chip.at("sg_raw_down", WORK + 40, [P, 2, D])
    up_hi = [chip.at(f"sg_up_hi{c}", WORK + 8 + 8 * j, [P, KD, P], F32R) for j, c in enumerate("ab")]
    up_lo = [chip.at(f"sg_up_lo{c}", WORK + 12 + 8 * j, [P, KD, P], F32R) for j, c in enumerate("ab")]
    down_hi = chip.at("sg_down_hi", WORK + 48, [P, 2, D], F32R)
    down_lo = chip.at("sg_down_lo", WORK + 56, [P, 2, D], F32R)
    p_hi = [chip.at(f"sg_p_hi{c}", WORK + 64 + 8 * j, [P, T], F32R) for j, c in enumerate("ab")]
    p_lo = [chip.at(f"sg_p_lo{c}", WORK + 68 + 8 * j, [P, T], F32R) for j, c in enumerate("ab")]
    u = chip.at("sg_u", WORK + 32, [P, T])
    prod = chip.at("sg_prod", WORK + 36, [P, T])
    vg = [chip.at(f"sg_v{c}", WORK + 24 + 4 * j, [P, NT, P]) for j, c in enumerate("ab")]
    gain = chip.at("sg_gain", WORK + 80, [P, KE])
    cur = [chip.at(f"sg_cur{j}", WORK + 80.5 + 0.125 * j, [P, 1]) for j in range(2)]
    w_spT, bias, banks, y = chip.w_spT, chip.sg_bias, chip.banks, chip.y
    norm = Norm(nc, chip, y_done=(y_free, (ROUNDS - 1) * NT + 2), **norm)
    block = ctx.enter_context(nc.Block())

    @block.sync
    def _(sp):
        def load_up(c, n, wait=None):
            if wait is not None:
                sp.wait_ge(up_w_ready, wait)
            sp.dma_start(raw_up[c][:], w_u[n].rearrange("p (k c) -> p k c", k=KD)).then_inc(up_loaded[c], 16)
            if wait is not None:
                sp.wait_ge(mix_done, wait)
            sp.dma_start(vg[c][:], v_in[:, bass.ds(n * P, P)].rearrange("(n p) f -> p n f", p=P)).then_inc(v_loaded[c], 16)

        def load_down(i, wait=None):
            if wait is not None:
                sp.wait_ge(down_w_ready, wait)
            sp.dma_start(raw_down[:], w_down[i].rearrange("p (s n) -> p s n", s=2)).then_inc(down_loaded, 16)

        load_up(0, 0)
        sp.dma_start(gain[:], ln_g).then_inc(gain_loaded, 16)
        load_up(1, 1)
        load_down(0)
        with sp.Fori(0, ROUNDS - 1) as i:
            load_up(0, i * 2 + 2, wait=i * 2 + 1)
            load_up(1, i * 2 + 3, wait=i * 2 + 2)
            load_down(i + 1, wait=i + 1)
        sp.wait_ge(prod_split, KE)
        sp.wait_ge(down_w_ready, ROUNDS)
        norm.sync(sp)

    @block.scalar
    def _(act):
        def split_up(c, n, wait=None):
            act.wait_ge(up_loaded[c], (n - c) * 8 + 16)
            if wait is not None:
                act.wait_ge(u_done, wait)
            nc.scalar.activation(up_hi[c][:], raw_up[c][:], ACT.Copy).then_inc(up_w_hi, 1)

        def split_down(i, wait=None):
            act.wait_ge(down_loaded, i * 16 + 16)
            if wait is not None:
                act.wait_ge(down_done, wait)
            nc.scalar.activation(down_hi[:], raw_down[:], ACT.Copy).then_inc(down_w_hi, 1)

        def gelu(n):
            act.wait_ge(u_done, n + 1)
            act.wait_ge(prod_ready, n)
            nc.scalar.activation(u[:], pair(banks[:, 0:2, :]), ACT.Gelu_apprx_tanh).then_inc(gelu_done, 1)

        def product_hi(c, n, wait=None):
            act.wait_ge(prod_ready, n + 1)
            if wait is not None:
                act.wait_ge(down_done, wait)
            nc.scalar.activation(p_hi[c][:], prod[:], ACT.Copy).then_inc(prod_hi, 1)

        split_up(0, 0)
        split_up(1, 1)
        gelu(0)
        product_hi(0, 0)
        split_down(0)
        with act.Fori(0, ROUNDS - 1) as i:
            split_up(0, i * 2 + 2, wait=i * 2 + 1)
            gelu(i * 2 + 1)
            product_hi(1, i * 2 + 1)
            split_up(1, i * 2 + 3, wait=i * 2 + 2)
            gelu(i * 2 + 2)
            product_hi(0, i * 2 + 2, wait=i * NT + NT)
            split_down(i + 1, wait=i * NT + NT)
        gelu(KE - 1)
        product_hi(1, KE - 1)
        norm.scalar(act)

    @block.gpsimd
    def _(pool):
        def up_low(c, n):
            pool.wait_ge(up_w_hi, n + 1)
            nc.gpsimd.tensor_tensor(up_lo[c][:], raw_up[c][:], up_hi[c][:].bitcast(F32), ALU.subtract).then_inc(up_w_ready, 1)

        def down_low(i):
            pool.wait_ge(down_w_hi, i + 1)
            nc.gpsimd.tensor_tensor(down_lo[:], raw_down[:], down_hi[:].bitcast(F32), ALU.subtract).then_inc(down_w_ready, 1)

        def product_low(c, n):
            pool.wait_ge(prod_hi, n + 1)
            nc.gpsimd.tensor_tensor(p_lo[c][:], prod[:], p_hi[c][:].bitcast(F32), ALU.subtract).then_inc(prod_split, 1)

        up_low(0, 0)
        up_low(1, 1)
        product_low(0, 0)
        down_low(0)
        with pool.Fori(0, ROUNDS - 1) as i:
            up_low(0, i * 2 + 2)
            product_low(1, i * 2 + 1)
            up_low(1, i * 2 + 3)
            product_low(0, i * 2 + 2)
            down_low(i + 1)
        product_low(1, KE - 1)
        norm.gpsimd(pool)

    @block.vector
    def _(dve):
        def fetch_gain(c, n):
            nc.vector.tensor_copy(cur[c][:], gain[:, bass.ds(n, 1)]).then_inc(cur_ready, 1)

        def combine(c, n):
            dve.wait_ge(cur_ready, n + 1)
            dve.wait_ge(mix_done, n + 1)
            dve.wait_ge(prod_split, n)
            nc.vector.scalar_tensor_tensor(
                out=prod[:].rearrange("p (n t) -> p n t", t=P),
                in0=pair(banks[:, 2:4, :]).rearrange("p (n t) -> p n t", t=P), scalar=cur[c][:, 0:1],
                in1=bias[:, bass.ds(n, 1), :].broadcast_to([P, NT, P]),
                op0=ALU.mult, op1=ALU.add).then_inc(mix_biased, 1)
            dve.wait_ge(mix_biased, n + 1)
            dve.wait_ge(gelu_done, n + 1)
            nc.vector.tensor_tensor(prod[:], prod[:], u[:], ALU.mult).then_inc(prod_ready, 1)

        def add_down(i, t):
            dve.wait_ge(down_done, i * NT + (t + 1))
            b = 4 + 2 * (t % 2)
            nc.vector.tensor_tensor(y[:, t, :], y[:, t, :], pair(banks[:, b:b + 2, :]), ALU.add).then_inc(y_free, 1)

        dve.wait_ge(gain_loaded, 16)
        nc.vector.memset(y[:], 0.0).then_inc(y_free, 2)
        dve.wait_ge(y_free, 2)
        fetch_gain(0, 0)
        fetch_gain(1, 1)
        combine(0, 0)
        with dve.Fori(0, ROUNDS - 1) as i:
            fetch_gain(0, i * 2 + 2)
            combine(1, i * 2 + 1)
            fetch_gain(1, i * 2 + 3)
            combine(0, i * 2 + 2)
            dve.wait_ge(y_free, i * NT + 2)
            for t in range(NT):
                add_down(i, t)
        combine(1, KE - 1)
        dve.wait_ge(y_free, (ROUNDS - 1) * NT + 2)
        norm.vector(dve, before=lambda t: add_down(ROUNDS - 1, t))

    @block.tensor
    def _(pe):
        def up(c, n):
            pe.wait_ge(up_w_ready, n + 1)
            pe.wait_ge(gelu_done, n)
            feature_major_product(nc, chip, 0, up_hi[c], up_lo[c]).then_inc(u_done, 1)
            pe.wait_ge(v_loaded[c], (n - c) * 8 + 16)
            pe.wait_ge(mix_biased, n)
            for s in range(NT):
                last = nc.tensor.matmul(banks[:, 2 + s // 4, (s % 4) * P:(s % 4 + 1) * P], vg[c][:, s, :],
                                        w_spT[:, bass.ds(n, 1), :].rearrange("s a t -> s (a t)"), start=True, stop=True)
            last.then_inc(mix_done, 1)

        up(0, 0)
        with pe.Fori(0, ROUNDS - 1) as i:
            up(1, i * 2 + 1)
            up(0, i * 2 + 2)
            down_product(nc, chip, pe, i, p_hi, p_lo, down_hi, down_lo, prod_split, down_w_ready, y_free, down_done)
        up(1, KE - 1)
        down_product(nc, chip, pe, ROUNDS - 1, p_hi, p_lo, down_hi, down_lo, prod_split, down_w_ready, y_free, down_done)
        norm.tensor(pe)


FT_AT, KT_AT, V_AT, SEL_AT, ONEHOT_AT, VC_AT = 68, 116, 148, 164, 166, 174
SLC, WIN = 0, 1


class NsaState:

    def __init__(self, chip):
        self.fT = chip.at("fT", FT_AT, [P, 12, T])
        self.kT = chip.at("kT", KT_AT, [P, 2, GROUPS, T])
        self.v = chip.at("v_tok", V_AT, [P, NT, 2 * KVW])
        self.selT = chip.at("selT", SEL_AT, [GROUPS * NSLC, T], BF16)
        self.onehot = chip.at("onehot", ONEHOT_AT, [GROUPS * NSLC, GROUPS, T], BF16)
        self.vc = chip.at("vc_split", VC_AT, [NCMP, GROUPS, P], F32R)


def nsa_projection_stage(nc, chip, ctx, nsa, w_fm):
    sem = lambda n: chip.semaphore(f"proj_{n}")
    loaded = [sem(f"loaded_{c}") for c in "ab"]
    w_hi_done, w_ready, product_done, kept = sem("w_hi_done"), sem("w_ready"), sem("product_done"), sem("kept")
    at = 164
    raw = [chip.at(f"proj_raw_{c}", at + 4 * j, [P, KD, P]) for j, c in enumerate("ab")]
    w_hi = [chip.at(f"proj_hi_{c}", at + 8 + 8 * j, [P, KD, P], F32R) for j, c in enumerate("ab")]
    w_lo = [chip.at(f"proj_lo_{c}", at + 12 + 8 * j, [P, KD, P], F32R) for j, c in enumerate("ab")]
    ROUNDS, PLAIN = FM_TILES // 2, 12 // 2
    block = ctx.enter_context(nc.Block())

    @block.sync
    def _(sp):
        def load(c, n):
            sp.dma_start(raw[c][:], w_fm[n].rearrange("p (k c) -> p k c", k=KD)).then_inc(loaded[c], 16)
        load(0, 0)
        load(1, 1)
        with sp.Fori(0, ROUNDS - 1) as i:
            for c in range(2):
                sp.wait_ge(w_ready, i * 2 + (c + 1))
                load(c, i * 2 + (c + 2))

    @block.scalar
    def _(act):
        def split(c, i, wait=None):
            act.wait_ge(loaded[c], i * 16 + 16)
            if wait is not None:
                act.wait_ge(product_done, wait)
            nc.scalar.activation(w_hi[c][:], raw[c][:], ACT.Copy).then_inc(w_hi_done, 1)

        def keep(c, i):
            act.wait_ge(product_done, i * 2 + (c + 1))
            nc.scalar.activation(nsa.fT[:, bass.ds(i * 2 + c, 1), :].rearrange("p a t -> p (a t)"),
                                 pair(chip.banks[:, 2 * c:2 * c + 2, :]), ACT.Copy).then_inc(kept, 1)

        def keep_keys(c, i):
            act.wait_ge(product_done, i * 2 + (c + 1))
            for g in range(2):
                for rows in range(2):
                    last = nc.scalar.activation(nsa.kT[64 * rows:64 * rows + 64, i - PLAIN, 2 * c + g, :],
                                                pair(chip.banks[64 * g:64 * g + 64, 2 * c:2 * c + 2, :]), ACT.Copy)
            last.then_inc(kept, 1)

        act.sem_inc(kept, 2)
        split(0, 0)
        split(1, 0)
        with act.Fori(0, PLAIN) as i:
            keep(0, i)
            split(0, i + 1, wait=i * 2 + 1)
            keep(1, i)
            split(1, i + 1, wait=i * 2 + 2)
        for i in range(PLAIN, ROUNDS):
            for c in range(2):
                keep_keys(c, i)
                if i < ROUNDS - 1:
                    split(c, i + 1, wait=i * 2 + c + 1)

    @block.gpsimd
    def _(pool):
        with pool.Fori(0, ROUNDS) as i:
            for c in range(2):
                pool.wait_ge(w_hi_done, i * 2 + (c + 1))
                nc.gpsimd.tensor_tensor(w_lo[c][:], raw[c][:], w_hi[c][:].bitcast(F32), ALU.subtract).then_inc(w_ready, 1)

    @block.tensor
    def _(pe):
        with pe.Fori(0, ROUNDS) as i:
            for c in range(2):
                pe.wait_ge(w_ready, i * 2 + (c + 1))
                pe.wait_ge(kept, i * 2 + (c + 1))
                feature_major_product(nc, chip, 2 * c, w_hi[c], w_lo[c]).then_inc(product_done, 1)


def nsa_value_stage(nc, chip, ctx, nsa, w_tok):
    sem = lambda n: chip.semaphore(f"val_{n}")
    loaded, w_hi_done, w_ready, product_done, kept = (
        sem(n) for n in ("loaded", "w_hi_done", "w_ready", "product_done", "kept"))
    widths = [KVW, KVW, GATES]
    raw = chip.at("val_raw", 164, [P, KD * KVW])
    w_hi = [chip.at(f"val_hi{b}", 172 + 16 * b, [P, KD * KVW], F32R) for b in range(2)]
    w_lo = [chip.at(f"val_lo{b}", 180 + 16 * b, [P, KD * KVW], F32R) for b in range(2)]
    hT_hi, hT_lo = chip.hT
    block = ctx.enter_context(nc.Block())

    @block.sync
    def _(sp):
        for p, width in enumerate(widths):
            if p:
                sp.wait_ge(w_ready, p)
            sp.dma_start(raw[:, 0:KD * width], w_tok[:, KD * KVW * p:KD * (KVW * p + width)]).then_inc(loaded, 16)

    @block.scalar
    def _(act):
        def split(p):
            n = KD * widths[p]
            act.wait_ge(loaded, 16 * (p + 1))
            if p == 2:
                act.wait_ge(product_done, NT)
            nc.scalar.activation(w_hi[p % 2][:, 0:n], raw[:, 0:n], ACT.Copy).then_inc(w_hi_done, 1)

        split(0)
        split(1)
        for p, width in enumerate(widths):
            for t in range(NT):
                act.wait_ge(product_done, NT * p + t + 1)
                source = chip.banks[:, t, 0:width]
                if p < 2:
                    nc.scalar.activation(nsa.v[:, t, KVW * p:KVW * (p + 1)], source, ACT.Copy).then_inc(kept, 1)
                else:
                    nc.scalar.activation(chip.gates[:, t, :], source, ACT.Sigmoid).then_inc(kept, 1)
            if p == 0:
                split(2)

    @block.gpsimd
    def _(pool):
        for p, width in enumerate(widths):
            n = KD * width
            pool.wait_ge(w_hi_done, p + 1)
            nc.gpsimd.tensor_tensor(w_lo[p % 2][:, 0:n], raw[:, 0:n], w_hi[p % 2][:, 0:n].bitcast(F32),
                                    ALU.subtract).then_inc(w_ready, 1)

    @block.tensor
    def _(pe):
        for p, width in enumerate(widths):
            pe.wait_ge(w_ready, p + 1)
            for t in range(NT):
                if p:
                    pe.wait_ge(kept, NT * (p - 1) + t + 1)
                for k in range(KD):
                    for j, (h, w) in enumerate(((hT_hi, w_hi), (hT_hi, w_lo), (hT_lo, w_hi))):
                        last = nc.tensor.matmul(chip.banks[:, t, 0:width], h[:, k, t * P:(t + 1) * P],
                                                w[p % 2][:, k * width:(k + 1) * width],
                                                start=(k == 0 and j == 0), stop=(k == KD - 1 and j == 2))
                last.then_inc(product_done, 1)


def nsa_compressed_stage(nc, chip, ctx, nsa, cmp_pe, cmp_w1, cmp_w2, p_cmp_out):
    sem = lambda n: chip.semaphore(f"cmp_{n}")
    zeroed, loaded = sem("zeroed"), sem("loaded")
    mask_filled, mask_made = sem("mask_filled"), sem("mask_made")
    hidden_done, pe_kept, hidden, compressed, kc_ready, vc_hi, vc_ready = (
        sem(n) for n in ("hidden_done", "pe_kept", "hidden", "compressed", "kc_ready", "vc_hi", "vc_ready"))
    scored, step, expd, masked, normed, gated = (
        sem(n) for n in ("scored", "step", "expd", "masked", "normed", "gated"))
    stored = [sem(f"stored{b}") for b in range(2)]
    shifted, chosen, sel_turned, sel_kept, late = (sem(n) for n in ("shifted", "chosen", "sel_turned", "sel_kept", "late"))

    w1 = [chip.at(f"cmp_w1_{c}", H_AT + 16 * j, [P, CMP_LEN, P]) for j, c in enumerate("kv")]
    w2 = [chip.at(f"cmp_w2_{c}", H_AT + 32 + 0.5 * j, [P, P]) for j, c in enumerate("kv")]
    pe_in = chip.at("cmp_pe", H_AT + 33, [P, 2, CMP_LEN])
    pe_out = chip.at("cmp_pe_out", H_AT + 33.5, [P, 2])
    hid = [chip.at(f"cmp_hid_{c}", H_AT + 34 + 0.5 * j, [P, 2, NCMP]) for j, c in enumerate("kv")]
    kc = chip.at("cmp_k", H_AT + 35, [P, GROUPS, NCMP])
    open_bias = chip.at("cmp_open_bias", H_AT + 36, [P, NT, 64])
    open_mask = chip.at("cmp_open_mask", H_AT + 38, [P, NT, 64])
    valid = chip.at("sel_valid", H_AT + 40, [P, NT, NSLC])
    invalid_score = chip.at("sel_invalid", H_AT + 40.5, [P, NT, NSLC])
    forced = chip.at("sel_forced", H_AT + 41, [P, NT, NSLC])
    e = [chip.at(f"cmp_e{b}", H_AT + 42 + 4 * b, [P, 2, 8, 64]) for b in range(2)]
    pg = [chip.at(f"cmp_pg{b}", H_AT + 50 + 4 * b, [P, 2, 8, 64]) for b in range(2)]
    top = chip.at("cmp_top", H_AT + 58, [P, 2, 16])
    den = chip.at("cmp_den", H_AT + 58.25, [P, 2, 3, 16])
    imp = chip.at("cmp_imp", H_AT + 59, [P, 2, GROUPS, 64])
    score = chip.at("cmp_score", H_AT + 61, [P, 2, GROUPS, NSLC])
    best = chip.at("cmp_best", H_AT + 62, [P, 2, GROUPS, 8])
    sel = chip.at("cmp_sel", H_AT + 62.5, [P, 2, GROUPS, NSLC])
    banks = chip.banks
    block = ctx.enter_context(nc.Block())
    n_loads = 2 * 2 + 2 * 2 + 2

    def heads_of(t, b):
        return banks[:, 2 * b:2 * b + 2, :].rearrange("p a (j n) -> p a j n", n=64)[:, :, :, 0:NCMP]

    flat = lambda ap: ap.rearrange("p a j n -> p (a j) n")

    @block.sync
    def _(sp):
        sp.wait_ge(zeroed, 4)
        for j in range(2):
            for half in range(2):
                rows = slice(64 * half, 64 * half + 64)
                sp.dma_start(w1[j][rows, :, rows], cmp_w1[j]).then_inc(loaded, 16)
                sp.dma_start(w2[j][rows, rows], cmp_w2[j]).then_inc(loaded, 16)
        for half in range(2):
            sp.dma_start(pe_in[64 * half:64 * half + 64, :, :], cmp_pe).then_inc(loaded, 16)
        for t in range(NT):
            sp.wait_ge(gated, t + 1)
            sp.dma_start(p_cmp_out[t * P:(t + 1) * P, :, :].rearrange("p (j a) n -> p a j n", a=2)[:, 0, :, 0:NCMP],
                         pg[t % 2][:, 0, :, 0:NCMP]).then_inc(stored[t % 2], 16)
            sp.dma_start(p_cmp_out[t * P:(t + 1) * P, :, :].rearrange("p (j a) n -> p a j n", a=2)[:, 1, :, 0:NCMP],
                         pg[t % 2][:, 1, :, 0:NCMP]).then_inc(stored[t % 2], 16)
        for b in range(2):
            sp.wait_ge(stored[b], 32 * (NT // 2))

    @block.gpsimd
    def _(pool):
        for m in (w1[0], w1[1], w2[0], w2[1]):
            nc.gpsimd.memset(m[:], 0.0).then_inc(zeroed, 1)
        fills = [(open_bias, 0.0), (open_mask, 1.0), (valid, 1.0), (invalid_score, 0.0), (forced, FORCE), (nsa.onehot, 0.0)]
        for m, value in fills:
            nc.gpsimd.memset(m[:], value).then_inc(mask_filled, 1)
        pool.wait_ge(mask_filled, len(fills))
        ended = dict(base=1 - CMP_LEN, pattern=[[P, NT], [-CMP_STRIDE, 64]], channel_multiplier=1)
        begun = dict(base=0, pattern=[[P, NT], [-SLC_LEN, NSLC]], channel_multiplier=1)
        near = dict(base=2 * SLC_LEN - 1, pattern=[[-P, NT], [SLC_LEN, NSLC]], channel_multiplier=-1)
        for m, fill, where in ((open_bias, NEG, ended), (open_mask, 0.0, ended), (valid, 0.0, begun),
                               (invalid_score, -FORCE, begun), (forced, 0.0, near)):
            nc.gpsimd.affine_select(out=m[:], in_=m[:], compare_op=ALU.is_ge, fill=fill, **where).then_inc(mask_made, 1)
        nc.gpsimd.affine_select(
            out=nsa.onehot[:].rearrange("r g (j k) -> r g j k", k=SLC_LEN),
            in_=nsa.onehot[:].rearrange("r g (j k) -> r g j k", k=SLC_LEN), compare_op=ALU.not_equal, fill=1.0,
            base=0, pattern=[[-NSLC, GROUPS], [-1, NSLC], [0, SLC_LEN]], channel_multiplier=1).then_inc(mask_made, 1)
        pool.wait_ge(mask_made, 6)
        nc.gpsimd.memset(forced[:, :, 0:1], FORCE).then_inc(mask_made, 1)
        for t in range(NT):
            b = t % 2
            pool.wait_ge(expd, t + 1)
            nc.gpsimd.tensor_tensor(flat(e[b][:])[:, :, 0:NCMP], flat(e[b][:])[:, :, 0:NCMP],
                                    open_mask[:, t:t + 1, 0:NCMP].broadcast_to([P, 16, NCMP]), ALU.mult).then_inc(masked, 1)
            pool.wait_ge(normed, t + 1)
            if t >= 2:
                pool.wait_ge(stored[b], 32 * (t // 2))
            for a in range(2):
                gate = chip.gates[:, t, :].rearrange("p (j a c) -> p a j c", a=2, c=3)[:, a, :, 0:1]
                last = nc.gpsimd.tensor_tensor(pg[b][:, a, :, 0:NCMP], e[b][:, a, :, 0:NCMP],
                                               gate.broadcast_to([P, 8, NCMP]), ALU.mult)
            last.then_inc(gated, 1)

    @block.tensor
    def _(pe):
        pe.wait_ge(loaded, 16 * n_loads)
        for j in range(2):
            for l in range(CMP_LEN):
                last_token = l + CMP_STRIDE * (NCMP - 1) + 1
                nc.tensor.matmul(banks[:, 2 * j, 0:2 * NCMP].rearrange("p (q n) -> p q n", q=2), w1[j][:, l, :],
                                 nsa.fT[:, 8 + 2 * j:10 + 2 * j, l:last_token:CMP_STRIDE],
                                 start=(l == 0), stop=(l == CMP_LEN - 1))
                last = nc.tensor.matmul(banks[:, 2 * j + 1, 0:1], w1[j][:, l, :], pe_in[:, j, l:l + 1],
                                        start=(l == 0), stop=(l == CMP_LEN - 1))
            last.then_inc(hidden_done, 1)
        pe.wait_ge(hidden, 1)
        nc.tensor.matmul(banks[:, 4, 0:2 * NCMP], w2[0][:], hid[0][:].rearrange("p q n -> p (q n)"),
                         start=True, stop=True).then_inc(compressed, 1)
        pe.wait_ge(hidden, 2)
        for q in range(2):
            last = nc.tensor.matmul(banks[0:NCMP, 5, q * P:(q + 1) * P], hid[1][:, q, :], w2[1][:], start=True, stop=True)
        last.then_inc(compressed, 1)
        pe.wait_ge(kc_ready, 8)

        def scores(t):
            b = t % 2
            if t >= 2:
                pe.wait_ge(step, 2 * (t - 2) + 1)
            for j in range(8):
                for a in range(2):
                    rows = slice(64 * a, 64 * a + 64)
                    last = nc.tensor.matmul(banks[:, 2 * b + a, 64 * j:64 * j + NCMP],
                                            nsa.fT[rows, j, t * P:(t + 1) * P], kc[rows, j // 2, :], start=True, stop=True)
            last.then_inc(scored, 1)

        def turn_selection(t):
            pe.wait_ge(chosen, t + 1)
            if t >= 2:
                pe.wait_ge(sel_kept, t - 1)
            nc.tensor.transpose(banks[0:GROUPS * NSLC, 6 + t % 2, 0:P], sel[:, t % 2].rearrange("p g j -> p (g j)"),
                                chip.ident[:]).then_inc(sel_turned, 1)

        scores(0)
        for t in range(1, NT):
            scores(t)
            if t >= 2:
                turn_selection(t - 2)
        turn_selection(NT - 2)
        turn_selection(NT - 1)

    @block.scalar
    def _(act):
        for j in range(2):
            act.wait_ge(hidden_done, j + 1)
            nc.scalar.activation(pe_out[:, j:j + 1], banks[:, 2 * j + 1, 0:1], ACT.Copy).then_inc(pe_kept, 1)
            act.wait_ge(pe_kept, j + 1)
            nc.scalar.activation(hid[j][:].rearrange("p q n -> p (q n)"), banks[:, 2 * j, 0:2 * NCMP],
                                 ACT.Gelu_apprx_tanh, bias=pe_out[:, j:j + 1]).then_inc(hidden, 1)
        act.wait_ge(compressed, 2)
        value = banks[0:NCMP, 5, 0:2 * P].rearrange("n (g d) -> n g d", d=DH)
        nc.scalar.activation(nsa.vc[:, :, 0:DH], value, ACT.Copy).then_inc(vc_hi, 1)
        for t in range(NT):
            act.wait_ge(shifted, t + 1)
            view = flat(e[t % 2][:])[:, :, 0:NCMP]
            nc.scalar.activation(view, view, ACT.Exp, scale=SCALE).then_inc(expd, 1)
            if t >= 1:
                act.wait_ge(sel_turned, t)
                nc.scalar.activation(nsa.selT[:, (t - 1) * P:t * P], banks[0:GROUPS * NSLC, 6 + (t - 1) % 2, 0:P],
                                     ACT.Copy).then_inc(sel_kept, 1)
        act.wait_ge(sel_turned, NT)
        nc.scalar.activation(nsa.selT[:, (NT - 1) * P:], banks[0:GROUPS * NSLC, 6 + (NT - 1) % 2, 0:P],
                             ACT.Copy).then_inc(sel_kept, 1)

    @block.vector
    def _(dve):
        done = [0]

        def then(instruction):
            done[0] += 1
            instruction.then_inc(late, 1)
            dve.wait_ge(late, done[0])

        dve.wait_ge(compressed, 1)
        for g in range(GROUPS):
            source = banks[64 * (g % 2):64 * (g % 2) + 64, 4, (g // 2) * NCMP:(g // 2 + 1) * NCMP]
            for half in range(2):
                nc.vector.tensor_copy(kc[64 * half:64 * half + 64, g, :], source).then_inc(kc_ready, 1)
        dve.wait_ge(vc_hi, 1)
        value = banks[0:NCMP, 5, 0:2 * P].rearrange("n (g d) -> n g d", d=DH)
        nc.vector.tensor_tensor(nsa.vc[:, :, DH:P], value, nsa.vc[:, :, 0:DH].bitcast(F32), ALU.subtract).then_inc(vc_ready, 1)
        dve.wait_ge(mask_made, 7)
        then(nc.vector.memset(imp[:], 0.0))

        def shift(t):
            b = t % 2
            dve.wait_ge(scored, t + 1)
            if t >= 2:
                dve.wait_ge(gated, t - 1)
            view = flat(e[b][:])[:, :, 0:NCMP]
            nc.vector.tensor_tensor(view, heads_of(t, b).rearrange("p a j n -> p (a j) n"),
                                    open_bias[:, t:t + 1, 0:NCMP].broadcast_to([P, 16, NCMP]), ALU.add).then_inc(step, 1)
            dve.wait_ge(step, 2 * t + 1)
            nc.vector.tensor_reduce(top[:, b, :], view, AX.X, ALU.max).then_inc(step, 1)
            dve.wait_ge(step, 2 * t + 2)
            nc.vector.tensor_tensor(view, view, top[:, b, :].unsqueeze(2).broadcast_to([P, 16, NCMP]),
                                    ALU.subtract).then_inc(shifted, 1)

        def select(t):
            b = t % 2
            view = flat(e[b][:])[:, :, 0:NCMP]
            dve.wait_ge(masked, t + 1)
            then(nc.vector.tensor_reduce(den[:, b, 0, :], view, AX.X, ALU.add))
            then(nc.vector.tensor_scalar(den[:, b, 1, :], den[:, b, 0, :], 1e-30, None, ALU.max))
            then(nc.vector.reciprocal(den[:, b, 2, :], den[:, b, 1, :]))
            nc.vector.tensor_tensor(view, view, den[:, b, 2, :].unsqueeze(2).broadcast_to([P, 16, NCMP]),
                                    ALU.mult).then_inc(normed, 1)
            dve.wait_ge(normed, t + 1)
            for g in range(GROUPS):
                last = nc.vector.tensor_reduce(imp[:, b, g, 0:NCMP],
                                               e[b][:, :, 2 * g:2 * g + 2, 0:NCMP].rearrange("p a j n -> p n a j"),
                                               AX.XY, ALU.add)
            then(last)
            quads = imp[:, b].rearrange("p g (j c) -> p g j c", c=4)
            s = score[:, b]
            then(nc.vector.tensor_tensor(s, quads[:, :, :, 0], quads[:, :, :, 1], ALU.add))
            then(nc.vector.tensor_tensor(s, s, quads[:, :, :, 2], ALU.add))
            then(nc.vector.tensor_scalar(quads[:, :, :, 3], quads[:, :, :, 3], 0.5, None, ALU.mult))
            then(nc.vector.tensor_tensor(s, s, quads[:, :, :, 3], ALU.add))
            then(nc.vector.tensor_tensor(s[:, :, 1:NSLC], s[:, :, 1:NSLC], quads[:, :, 0:NSLC - 1, 3], ALU.add))
            for m, op in ((forced, ALU.add), (valid, ALU.mult), (invalid_score, ALU.add)):
                then(nc.vector.tensor_tensor(s, s, m[:, t:t + 1, :].broadcast_to([P, GROUPS, NSLC]), op))
            for g in range(GROUPS):
                last = nc.vector.max(best[:, b, g, :], score[:, b, g, :])
            then(last)
            if t >= 2:
                dve.wait_ge(sel_turned, t - 1)
            for g in range(GROUPS):
                last = nc.vector.match_replace(sel[:, b, g, :], best[:, b, g, :], score[:, b, g, :], 1e30)
            then(last)
            nc.vector.tensor_scalar(sel[:, b], sel[:, b], 1e29, NEG, ALU.is_lt, ALU.mult).then_inc(chosen, 1)

        shift(0)
        for t in range(1, NT):
            shift(t)
            select(t - 1)
        select(NT - 1)


def attention_plan():
    jobs = [(branch, i) for i in range(NT) for branch in (SLC, WIN)]
    tiles, n = [], 0
    for branch, i in jobs:
        keys = list(range(0, i + 1)) + [None] if branch == SLC else list(range(max(0, i - WINDOW // P), i + 1))
        tiles.append([(n + x, key) for x, key in enumerate(keys)])
        n += len(keys)
    return jobs, tiles, n


def nsa_attention_stage(nc, chip, ctx, nsa, p_cmp_in, oT):
    sem = lambda n: chip.semaphore(f"att_{n}")
    jobs, tiles, TILES = attention_plan()
    JOBS, HEAD_JOBS = len(jobs), len(jobs) * HPG
    LAG = 2
    q_hi, q_lo, k_hi, k_lo, v_hi, v_lo, group_copied = (
        sem(n) for n in ("q_hi", "q_lo", "k_hi", "k_lo", "v_hi", "v_lo", "group_copied"))
    scored, maxed, expd, inverted, scaled = (sem(n) for n in ("scored", "maxed", "expd", "inverted", "scaled"))
    turned, hi_done, lo_done, multiplied = (sem(n) for n in ("turned", "hi_done", "lo_done", "multiplied"))
    pool_go, pe_go = sem("pool_go"), sem("pe_go")
    pc_loaded, upper_kept, folded = [sem(f"pc_loaded{b}") for b in range(2)], sem("upper_kept"), sem("folded")

    qS = chip.at("att_q", 36, [P, HPG, T], F32R)
    kS_hi = chip.at("att_k_hi", 52, [P, 2, T], F32R)
    kS_lo = chip.at("att_k_lo", 60, [P, 2, T], F32R)
    vS = chip.at("att_v", 100, [P, 2, NT, P], F32R)
    pT_hi = [chip.at(f"att_pT_hi{b}", kb, [P, HALF], F32R) for b, kb in enumerate((108, 110, 205.5))]
    pT_lo = [chip.at(f"att_pT_lo{b}", 112 + 2 * b, [P, HALF], F32R) for b in range(2)]
    vc = chip.at("att_vc", 176, [NCMP, P], F32R)
    gates = chip.at("att_gates", 176.5, [P, NT, HPG, 3])
    prob = [chip.at("att_p_slc", 177, [P, HPG, T]), chip.at("att_p_win", 193, [P, HPG, WINDOW + P])]
    pc = [chip.at(f"att_p_cmp{b}", 203 + b, [P, HPG, 64]) for b in range(2)]
    negmax, den, inv = (chip.at(f"att_{n}", 205 + j / 8, [P, 8]) for j, n in enumerate(("negmax", "den", "inv")))
    upper = chip.at("att_upper", VC_AT, [P, HALF])[64:P]
    banks = chip.banks
    block = ctx.enter_context(nc.Block())

    def key_range(branch, i):
        return (0 if branch == SLC else max(0, i - WINDOW // P)) * P, (i + 1) * P

    def slot(m):
        return banks[:, 2 * (m % 2):2 * (m % 2) + 2, :]

    def beside(J, h):
        if J == 0 or h == 0:
            return []
        n = len(tiles[J - 1])
        return tiles[J - 1][n * (h - 1) // (HPG - 1):n * h // (HPG - 1)]

    def walk(score, soften, tile):
        score(0, 0)
        for m in range(HEAD_JOBS):
            J, h = divmod(m, HPG)
            if m + 1 < HEAD_JOBS:
                score(*divmod(m + 1, HPG))
            soften(J, h)
            for n, key in beside(J, h):
                tile(J - 1, n, key)
        for n, key in tiles[JOBS - 1]:
            tile(JOBS - 1, n, key)

    def folds_before(J, n):
        branch, i = jobs[J]
        return i - 1 if branch == SLC and i >= 1 and n == tiles[J][0][0] + LAG else None

    def nothing(*_):
        pass

    def heads(g, m):
        return g * HEAD_JOBS + (m + 2)

    def keys(g, n):
        return g * TILES + (n + 2)

    def queries(g, i):
        return g * NT + (i + 2)

    @block.sync
    def _(sp):
        with sp.Fori(0, GROUPS) as g:
            for i in range(NT):
                before = tiles[2 * (i - 2)][-1][0] if i >= 2 else -1
                sp.wait_ge(turned, keys(g, before))
                sp.dma_start(pc[i % 2][:, :, 0:NCMP], p_cmp_in[i * P:(i + 1) * P, bass.ds(g * HPG, HPG), 0:NCMP]
                             ).then_inc(pc_loaded[i % 2], 16)

    @block.scalar
    def _(act):
        for count in (expd, hi_done, upper_kept):
            act.sem_inc(count, 1)
        with act.Fori(0, GROUPS) as g:
            act.wait_ge(scored, heads(g, -1))
            act.wait_ge(multiplied, keys(g, -1))
            for a in range(2):
                rows = slice(64 * a, 64 * a + 64)
                last = nc.scalar.activation(qS[rows, a:HPG:2, :], nsa.fT[rows, bass.ds(g * 2, 2), :], ACT.Copy, scale=SCALE)
            last.then_inc(q_hi, 1)
            nc.scalar.activation(kS_hi[:], nsa.kT[:, :, bass.ds(g, 1), :].rearrange("p b g t -> p b (g t)"),
                                 ACT.Copy).then_inc(k_hi, 1)
            for b in range(2):
                last = nc.scalar.activation(vS[:, b, :, 0:DH], nsa.v[:, :, bass.ds(g * DH + b * KVW, DH)], ACT.Copy)
            last.then_inc(v_hi, 1)

            def soften(J, h):
                branch, i = jobs[J]
                m = J * HPG + h
                lo, hi = key_range(branch, i)
                act.wait_ge(maxed, heads(g, m))
                if J >= 2:
                    act.wait_ge(turned, keys(g, tiles[J - 2][-1][0]))
                nc.scalar.activation(prob[branch][:, h, 0:hi - lo], pair(slot(m))[:, 0:hi - lo], ACT.Exp,
                                     bias=negmax[:, m % 8:m % 8 + 1], accum_out=den[:, m % 8:m % 8 + 1]).then_inc(expd, 1)

            def tile(J, n, key):
                rows = P if key is not None else NCMP
                act.wait_ge(turned, keys(g, n))
                act.wait_ge(multiplied, keys(g, max(n - 3, -1)))
                nc.scalar.activation(pT_hi[n % 3][0:rows, :], banks[0:rows, 4 + n % 2, :], ACT.Copy).then_inc(hi_done, 1)
                if folds_before(J, n) is not None:
                    keep_upper(folds_before(J, n))

            def keep_upper(i):
                act.wait_ge(multiplied, keys(g, tiles[2 * i + 1][-1][0]))
                act.wait_ge(folded, queries(g, i - 1))
                nc.scalar.activation(upper, banks[64:P, 6 + i % 2, :], ACT.Copy).then_inc(upper_kept, 1)

            walk(nothing, soften, tile)
            keep_upper(NT - 1)

    @block.gpsimd
    def _(pool):
        pool.sem_inc(scaled, 1)
        with pool.Fori(0, GROUPS) as g:
            pool.wait_ge(k_hi, g + 1)
            nc.gpsimd.tensor_tensor(kS_lo[:], nsa.kT[:, :, bass.ds(g, 1), :].rearrange("p b g t -> p b (g t)"),
                                    kS_hi[:].bitcast(F32), ALU.subtract).then_inc(k_lo, 1)
            pool.wait_ge(group_copied, g * 2 + 2)
            for J, (branch, i) in enumerate(jobs):
                lo, hi = key_range(branch, i)
                for h in range(HPG):
                    m = J * HPG + h
                    pool.wait_ge(inverted, heads(g, m))
                    pool.sem_inc(pool_go, 1)
                    at = prob[branch][:, h, 0:hi - lo]
                    nc.gpsimd.tensor_scalar(at, at, inv[:, m % 8:m % 8 + 1], gates[:, i, h, 1 + branch:2 + branch],
                                            ALU.mult, ALU.mult).then_inc(scaled, 1)

    @block.vector
    def _(dve):
        for count in (maxed, inverted, lo_done, folded):
            dve.sem_inc(count, 1)
        with dve.Fori(0, GROUPS) as g:
            dve.wait_ge(scaled, heads(g, -1))
            nc.vector.tensor_copy(gates[:].rearrange("p t h c -> p t (h c)"),
                                  chip.gates[:, :, bass.ds(g * (3 * HPG), 3 * HPG)]).then_inc(group_copied, 1)
            dve.wait_ge(multiplied, keys(g, -1))
            nc.vector.tensor_copy(vc[:], nsa.vc[:, bass.ds(g, 1), :].rearrange("n g d -> n (g d)").bitcast(F32)).then_inc(group_copied, 1)
            dve.wait_ge(q_hi, g + 1)
            for a in range(2):
                own, other = slice(64 * a, 64 * a + 64), slice(64 - 64 * a, P - 64 * a)
                last = nc.vector.scalar_tensor_tensor(
                    out=qS[other, a:HPG:2, :], in0=nsa.fT[own, bass.ds(g * 2, 2), :], scalar=SCALE,
                    in1=qS[own, a:HPG:2, :].bitcast(F32), op0=ALU.mult, op1=ALU.subtract)
            last.then_inc(q_lo, 1)
            dve.wait_ge(v_hi, g + 1)
            for b in range(2):
                last = nc.vector.tensor_tensor(vS[:, b, :, DH:P], nsa.v[:, :, bass.ds(g * DH + b * KVW, DH)],
                                               vS[:, b, :, 0:DH].bitcast(F32), ALU.subtract)
            last.then_inc(v_lo, 1)
            def invert(J, h):
                m = J * HPG + h
                dve.wait_ge(expd, heads(g, m))
                if m >= 8:
                    dve.wait_ge(scaled, heads(g, m - 8))
                nc.vector.reciprocal(inv[:, m % 8:m % 8 + 1], den[:, m % 8:m % 8 + 1]).then_inc(inverted, 1)

            def largest(J, h):
                branch, i = jobs[J]
                m = J * HPG + h
                lo, hi = key_range(branch, i)
                dve.wait_ge(scored, heads(g, m))
                nc.vector.tensor_reduce(negmax[:, m % 8:m % 8 + 1], pair(slot(m))[:, 0:hi - lo], AX.X, ALU.max,
                                        negate=True).then_inc(maxed, 1)

            def tile(J, n, key):
                rows = P if key is not None else NCMP
                dve.wait_ge(hi_done, keys(g, n))
                dve.wait_ge(multiplied, keys(g, max(n - 2, -1)))
                nc.vector.tensor_tensor(pT_lo[n % 2][0:rows, :], banks[0:rows, 4 + n % 2, :],
                                        pT_hi[n % 3][0:rows, :].bitcast(F32), ALU.subtract).then_inc(lo_done, 1)
                if folds_before(J, n) is not None:
                    fold(folds_before(J, n))

            def fold(i):
                dve.wait_ge(upper_kept, queries(g, i))
                for a in range(2):
                    pick = lambda ap: ap.rearrange("d (h q) -> d h q", q=P)[:, a:HPG:2, :]
                    last = nc.vector.tensor_tensor(oT[64 * a:64 * a + 64, bass.ds(g * 2, 2), i * P:(i + 1) * P],
                                                   pick(banks[0:64, 6 + i % 2, :]), pick(upper), ALU.add)
                last.then_inc(folded, 1)

            walk(largest, invert, tile)
            fold(NT - 1)

    @block.tensor
    def _(pe):
        for count in (scored, turned, multiplied):
            pe.sem_inc(count, 1)
        with pe.Fori(0, GROUPS) as g:
            pe.wait_ge(q_lo, g + 1)
            pe.wait_ge(k_lo, g + 1)
            pe.wait_ge(v_lo, g + 1)
            pe.wait_ge(group_copied, g * 2 + 2)
            pending = []

            def score(J, h):
                branch, i = jobs[J]
                m = J * HPG + h
                lo, hi = key_range(branch, i)
                pe.wait_ge(expd, heads(g, max(m - 2, -1)))
                q = qS[:, h, i * P:(i + 1) * P]
                for c, at in enumerate(range(lo, hi, HALF)):
                    end = min(at + HALF, hi)
                    out = banks[:, 2 * (m % 2) + c, 0:end - at]
                    diagonal = end == hi
                    oldest = branch == WIN and c == 0 and i >= WINDOW // P
                    nc.tensor.matmul(out, q, kS_hi[:, branch, at:end], start=True, stop=False)
                    last = nc.tensor.matmul(out, q, kS_lo[:, branch, at:end], start=False,
                                            stop=not (diagonal or oldest or branch == SLC))
                    if branch == SLC:
                        last = nc.tensor.matmul(out, nsa.selT[:, i * P:(i + 1) * P],
                                                nsa.onehot[:, bass.ds(g, 1), at:end].rearrange("r g k -> r (g k)"),
                                                start=False, stop=not diagonal)
                    if oldest:
                        last = nc.tensor.matmul(out[:, 0:P], chip.ident_bf[:], chip.too_old[:], start=False, stop=not diagonal)
                    if diagonal:
                        last = nc.tensor.matmul(out[:, end - at - P:], chip.ident_bf[:], chip.causal[:], start=False, stop=True)
                last.then_inc(scored, 1)

            def values(J, n, key):
                branch, i = jobs[J]
                rows = P if key is not None else NCMP
                if n == tiles[2 * i][0][0]:
                    pe.wait_ge(folded, queries(g, max(i - 2, -1)))
                pe.wait_ge(hi_done, keys(g, n))
                pe.wait_ge(lo_done, keys(g, n))
                v = vS[:, branch, key, :] if key is not None else vc[:]
                out = banks[:, 6 + i % 2, :]
                nc.tensor.matmul(out, v, pT_hi[n % 3][0:rows, :], start=(n == tiles[2 * i][0][0]), stop=False)
                nc.tensor.matmul(out, v, pT_lo[n % 2][0:rows, :], start=False,
                                 stop=(n == tiles[2 * i + 1][-1][0])).then_inc(multiplied, 1)

            def tile(J, n, key):
                branch, i = jobs[J]
                lo, _ = key_range(branch, i)
                rows = P if key is not None else NCMP
                if key is None:
                    pe.wait_ge(pc_loaded[i % 2], g * (8 * NT) + 16 * (i // 2 + 1))
                elif n == tiles[J][0][0]:
                    pe.wait_ge(scaled, heads(g, (J + 1) * HPG - 1))
                pe.wait_ge(lo_done, keys(g, max(n - 2, -1)))
                if key is None:
                    pe.sem_inc(pe_go, 1)
                for h in range(HPG):
                    source = pc[i % 2][:, h, 0:NCMP] if key is None else prob[branch][:, h, key * P - lo:(key + 1) * P - lo]
                    last = nc.tensor.transpose(banks[0:rows, 4 + n % 2, h * P:(h + 1) * P], source, chip.ident[:])
                last.then_inc(turned, 1)
                pending.append((J, n, key))
                if len(pending) > LAG:
                    values(*pending.pop(0))

            walk(score, nothing, tile)
            for tile_left in pending:
                values(*tile_left)


def nsa_output_stage(nc, chip, ctx, oT, w_out, norm):
    sem = lambda n: chip.semaphore(f"out_{n}")
    loaded = [sem(f"loaded{b}") for b in range(2)]
    w_hi_done, w_ready, o_hi_done, o_ready, done, kept = (
        sem(n) for n in ("w_hi_done", "w_ready", "o_hi_done", "o_ready", "done", "kept"))
    o_hi = chip.at("out_o_hi", 100, [P, KD, T], F32R)
    o_lo = chip.at("out_o_lo", 4, [P, KD, T], F32R)
    w_hi = chip.at("out_w_hi", 36, [P, KD, D], F32R)
    w_lo = chip.at("out_w_lo", 164, [P, KD, D], F32R)
    raw = [chip.at(f"out_raw{b}", 196 + 4 * b, [P, D]) for b in range(2)]
    norm = Norm(nc, chip, y_done=(kept, 0), x_at=132, rest_at=196, lag=NT, **norm)
    block = ctx.enter_context(nc.Block())

    @block.sync
    def _(sp):
        for k in range(KD):
            if k >= 2:
                sp.wait_ge(w_ready, k - 1)
            sp.dma_start(raw[k % 2][:], w_out[k * P:(k + 1) * P, :]).then_inc(loaded[k % 2], 16)
        sp.wait_ge(w_ready, KD)
        norm.sync(sp)

    @block.scalar
    def _(act):
        for k in range(KD):
            nc.scalar.activation(o_hi[:, k, :], oT[:, k, :], ACT.Copy).then_inc(o_hi_done, 1)
            act.wait_ge(loaded[k % 2], 16 * (k // 2 + 1))
            nc.scalar.activation(w_hi[:, k, :], raw[k % 2][:], ACT.Copy).then_inc(w_hi_done, 1)

        def keep(t):
            act.wait_ge(done, t + 1)
            b = 2 * (t % 4)
            nc.scalar.activation(chip.y[:, t, :], pair(chip.banks[:, b:b + 2, :]), ACT.Copy).then_inc(kept, 1)

        norm.scalar(act, before=keep)

    @block.gpsimd
    def _(pool):
        for k in range(KD):
            pool.wait_ge(w_hi_done, k + 1)
            nc.gpsimd.tensor_tensor(w_lo[:, k, :], raw[k % 2][:], w_hi[:, k, :].bitcast(F32), ALU.subtract).then_inc(w_ready, 1)
        norm.gpsimd(pool)

    @block.vector
    def _(dve):
        for k in range(KD):
            dve.wait_ge(o_hi_done, k + 1)
            nc.vector.tensor_tensor(o_lo[:, k, :], oT[:, k, :], o_hi[:, k, :].bitcast(F32), ALU.subtract).then_inc(o_ready, 1)
        norm.vector(dve)

    @block.tensor
    def _(pe):
        for t in range(NT):
            b = 2 * (t % 4)
            if t >= 4:
                pe.wait_ge(kept, t - 3)
            for k in range(KD):
                if t == 0:
                    pe.wait_ge(w_ready, k + 1)
                    pe.wait_ge(o_ready, k + 1)
                for j, (o, w) in enumerate(((o_hi, w_hi), (o_hi, w_lo), (o_lo, w_hi))):
                    for half in range(2):
                        last = nc.tensor.matmul(chip.banks[:, b + half, :], o[:, k, t * P:(t + 1) * P],
                                                w[:, k, half * HALF:(half + 1) * HALF],
                                                start=(k == 0 and j == 0), stop=(k == KD - 1 and j == 2))
            last.then_inc(done, 1)
        pe.wait_ge(kept, NT)
        norm.tensor(pe)


def build(nc, a, out):
    scratch = lambda name, shape: nc.dram_tensor(name, shape, F32, kind="Internal").ap()
    x_mid = [scratch(f"x_mid{j}", (T, D)) for j in range(3)]
    p_cmp = scratch("p_cmp", (T, HEADS, 64))
    v_normed = scratch("v_normed", (T, E))
    gain = lambda layer, j: a["norm_gains"][4 * layer + j:4 * layer + j + 1, :]
    with ExitStack() as whole:
        chip = Chip(nc, whole)
        nsa = NsaState(chip)
        oT = chip.at("oT", 4, [P, KD, T])

        def stage(build_stage, *args, **kwargs):
            with ExitStack() as ctx:
                build_stage(nc, chip, ctx, *args, **kwargs)
            chip.end_stage()

        stage(constants_stage)
        stage(first_norm_stage, dict(tag="norm0", x_in=a["x"], pre_gain=gain(0, 0)))
        stage(nsa_projection_stage, nsa, a["nsa_w_fm"])
        stage(nsa_value_stage, nsa, a["nsa_w_tok"])
        stage(nsa_compressed_stage, nsa, a["cmp_pe"], a["cmp_w1"], a["cmp_w2"], p_cmp)
        stage(nsa_attention_stage, nsa, p_cmp, oT)
        stage(nsa_output_stage, oT, a["nsa_w_out"],
              norm=dict(tag="norm1", x_in=a["x"], x_out=x_mid[0], post_gain=gain(0, 1), pre_gain=gain(0, 2)))
        stage(ffn_stage, "ffn0", a["ffn_w_up"][0], a["ffn_w_down"][0], a["ffn_conv"][0],
              norm=dict(tag="norm2", x_in=x_mid[0], x_out=x_mid[1], post_gain=gain(0, 3), pre_gain=gain(1, 0)))
        stage(gmlp_v_stage, a["sg_w_v"], v_normed)
        stage(gmlp_bias_stage, a["sg_w_sp"], a["sg_b_sp"], a["sg_ln_b"])
        stage(gmlp_stage, a["sg_w_u"], a["sg_w_out"], v_normed, a["sg_ln_g"],
              norm=dict(tag="norm3", x_in=x_mid[1], x_out=x_mid[2], post_gain=gain(1, 1), pre_gain=gain(1, 2)))
        stage(ffn_stage, "ffn1", a["ffn_w_up"][1], a["ffn_w_down"][1], a["ffn_conv"][1],
              norm=dict(tag="norm4", x_in=x_mid[2], x_out=out, post_gain=gain(1, 3)))


def lay_out(i):
    import numpy as np

    i = {k: np.asarray(v) for k, v in i.items()}
    flat = np.ascontiguousarray
    w_in = i["nsa_w_in"][0]
    q, kc, vc, ks, vs, kw, vw, gl = np.split(w_in, [HEADS * DH + k * KVW for k in range(7)], axis=1)
    piece = lambda w: w.reshape(KD, P, -1).transpose(1, 0, 2).reshape(P, -1)
    columns = lambda w: flat(w.reshape(KD, P, -1, P).transpose(2, 1, 0, 3).reshape(-1, P, KD * P))
    rows2 = lambda w: flat(w.reshape(-1, 2, P, D).transpose(0, 2, 1, 3).reshape(-1, P, 2 * D))
    sg_in = i["sg_w_in"][0]
    layers = i["ffn_w_up"].shape[0]
    conv = np.concatenate([i["ffn_conv_w"], i["ffn_conv_b"][:, None]], axis=1)
    return {
        "x": i["x"][0],
        "norm_gains": i["norm_gains"].reshape(-1, D),
        "nsa_w_fm": columns(np.concatenate([q, kc, vc, ks, kw], axis=1)),
        "nsa_w_tok": flat(np.concatenate([piece(vs), piece(vw), piece(gl)], axis=1)),
        "cmp_pe": flat(i["nsa_cmp_pe"][0].transpose(2, 0, 1)),
        "cmp_w1": flat(i["nsa_cmp_w1"][0].reshape(2, CMP_LEN, DH, DH).transpose(0, 2, 1, 3)),
        "cmp_w2": i["nsa_cmp_w2"][0],
        "nsa_w_out": i["nsa_w_out"][0],
        "sg_w_v": flat(sg_in[:, E:].reshape(4, 2, P, 4, HALF).transpose(3, 0, 2, 1, 4).reshape(16, P, 2 * HALF)),
        "sg_w_u": columns(sg_in[:, :E]),
        "sg_ln_g": flat(i["sg_ln_g"][0].reshape(KE, P).T),
        "sg_ln_b": i["sg_ln_b"][0].reshape(1, E),
        "sg_w_sp": flat(i["sg_w_sp"][0].transpose(2, 0, 1).reshape(P, KE * P)),
        "sg_b_sp": i["sg_b_sp"][0].reshape(1, KE * P),
        "sg_w_out": rows2(i["sg_w_out"][0]),
        "ffn_w_up": flat(i["ffn_w_up"].reshape(layers, KD, P, 2, KF, P).transpose(0, 4, 2, 3, 1, 5).reshape(layers, KF, P, -1)),
        "ffn_w_down": np.stack([rows2(w) for w in i["ffn_w_down"]]),
        "ffn_conv": flat(conv.reshape(layers, 4, 2, KF, P).transpose(0, 4, 3, 2, 1)),
    }


def kernel(**inputs):
    import numpy as np
    import concourse.bacc as bacc
    from concourse.bass_utils import run_bass_kernel_spmd

    nc = bacc.Bacc("TRN2", target_bir_lowering=False, num_devices=1)
    arrays = {f"in_{name}": np.ascontiguousarray(v) for name, v in lay_out(inputs).items()}
    args = {name[3:]: nc.dram_tensor(name, v.shape, mybir.dt.from_np(v.dtype), kind="ExternalInput").ap()
            for name, v in arrays.items()}
    out = nc.dram_tensor("out", (T, D), F32, kind="ExternalOutput").ap()
    build(nc, args, out)
    result = run_bass_kernel_spmd(nc, [arrays], core_ids=[0])
    return result.results[0]["out"].reshape(1, T, D)
```

```python
from contextlib import ExitStack

import concourse.bass as bass
from concourse import mybir

ALU = mybir.AluOpType
ACT = mybir.ActivationFunctionType
AX = mybir.AxisListType
F32 = mybir.dt.float32
F32R = mybir.dt.float32r
BF16 = mybir.dt.bfloat16

P = 128
D = 1024
T = 1024
NT = T // P
KD = D // P
HALF = 512
EPS = 1e-6
HEADS, GROUPS, DH = 16, 4, 64
HPG = HEADS // GROUPS
SCALE = DH ** -0.5
CMP_LEN, CMP_STRIDE = 32, 16
NCMP = (T - CMP_LEN) // CMP_STRIDE + 1
SLC_LEN, TOPN, WINDOW = 64, 8, 512
NSLC = T // SLC_LEN
FIRST_SEL = TOPN * SLC_LEN // P
FORCE, NEG = 1.0e4, -1.0e30
GATES = 3 * HEADS
KVW = GROUPS * DH
F = 2816
KF = F // P
E = 2 * D
KE = E // P
FM_TILES = (HEADS * DH + 4 * KVW) // P
BASE = 16640

CONST_AT, H_AT, Y_AT, WORK = 0, 4, 68, 100


class Chip:

    def __init__(self, nc, ctx):
        self.nc, self.tensors, self.in_stage = nc, {}, []
        self.banks = ctx.enter_context(nc.psum_tensor("banks", [P, 8, HALF], F32))
        self.ident = self.at("ident", CONST_AT, [P, P])
        self.ident_bf = self.at("ident_bf", CONST_AT + 0.5, [P, P], BF16)
        self.causal = self.at("causal", CONST_AT + 0.75, [P, P], BF16)
        self.too_old = self.at("too_old", CONST_AT + 1.0, [P, P], BF16)
        self.eps = self.at("eps", CONST_AT + 1.25, [P, 1])
        self.gates = self.at("gates", CONST_AT + 1.5, [P, NT, GATES])
        self.hT = [self.at(n, H_AT + 32 * j, [P, KD, T], F32R) for j, n in enumerate(("hT_hi", "hT_lo"))]
        self.y = self.at("y", Y_AT, [P, NT, D])

    def semaphore(self, name):
        self.in_stage.append(self.nc.alloc_semaphore(name=name))
        return self.in_stage[-1]

    def end_stage(self):
        self.nc.clear_and_free_semaphores(self.in_stage)
        self.nc.all_engine_barrier()
        self.in_stage = []

    def at(self, name, kb, shape, dt=F32):
        if name not in self.tensors:
            self.tensors[name] = self.nc.alloc_sbuf_tensor_at(name, shape, dt, offset=BASE + int(kb * 1024))
        return self.tensors[name]


def pair(ap):
    return ap.rearrange("p a c -> p (a c)")


def make_constants(nc, chip, pool, filled, cut):
    nc.gpsimd.memset(chip.eps[:], EPS).then_inc(filled, 1)
    for m in (chip.ident, chip.ident_bf, chip.causal, chip.too_old):
        nc.gpsimd.memset(m[:], 0.0).then_inc(filled, 1)
    pool.wait_ge(filled, 5)
    for m in (chip.ident, chip.ident_bf):
        nc.gpsimd.affine_select(out=m[:], in_=m[:], compare_op=ALU.not_equal, fill=1.0, base=0,
                                pattern=[[-1, P]], channel_multiplier=1).then_inc(cut, 1)
    nc.gpsimd.affine_select(out=chip.causal[:], in_=chip.causal[:], compare_op=ALU.is_ge, fill=NEG, base=0,
                            pattern=[[-1, P]], channel_multiplier=1).then_inc(cut, 1)
    nc.gpsimd.affine_select(out=chip.too_old[:], in_=chip.too_old[:], compare_op=ALU.is_gt, fill=NEG, base=0,
                            pattern=[[1, P]], channel_multiplier=-1).then_inc(cut, 1)
    pool.wait_ge(cut, 4)


class Norm:
    PER_LOAD = 2

    def __init__(self, nc, chip, tag, x_in, x_out=None, post_gain=None, pre_gain=None, y_done=None,
                 x_at=WORK, rest_at=WORK + 32, lag=4, coming=(), coming_after=None):
        sem = lambda n: chip.semaphore(f"{tag}_{n}")
        self.nc, self.chip, self.x_in, self.x_out, self.y_done = nc, chip, x_in, x_out, y_done
        self.post_gain, self.pre_gain, self.lag = post_gain, pre_gain, lag
        self.coming, self.coming_after, self.came = coming, coming_after, sem("came")
        self.x_loaded = [sem(f"x_loaded{j}") for j in range(NT // self.PER_LOAD)]
        self.gains_loaded, self.x_stored = sem("gains_loaded"), sem("x_stored")
        self.y_squared, self.y_root, self.y_inverse, self.y_normed = (
            sem("y_squared"), sem("y_root"), sem("y_inverse"), sem("y_normed"))
        self.x_new, self.x_squared, self.x_root, self.x_inverse = (
            sem("x_new"), sem("x_squared"), sem("x_root"), sem("x_inverse"))
        self.x_normed, self.turned, self.hi_done, self.lo_done = (
            sem("x_normed"), sem("turned"), sem("hi_done"), sem("lo_done"))
        self.x = chip.at(f"norm_x_{x_at}", x_at, [P, NT, D])
        self.g_post = chip.at(f"norm_g_post_{rest_at}", rest_at, [P, D])
        self.g_pre = chip.at(f"norm_g_pre_{rest_at}", rest_at + 4, [P, D])
        self.junk = chip.at(f"norm_junk_{rest_at}", rest_at + 8, [P, D], BF16)
        self.stats = chip.at(f"norm_stats_{rest_at}", rest_at + 10, [P, 6, NT])
        self.gains = 16 * ((post_gain is not None) + (pre_gain is not None))

    def stat(self, j, n):
        return self.stats[:, j, n:n + 1]

    def sync(self, sp):
        m = self.PER_LOAD
        if self.post_gain is not None:
            sp.dma_start(self.g_post[:], self.post_gain.broadcast_to([P, D])).then_inc(self.gains_loaded, 16)
        for j in range(NT // m):
            sp.dma_start(self.x[:, m * j:m * j + m, :],
                         self.x_in[m * j * P:m * (j + 1) * P, :].rearrange("(n p) d -> p n d", p=P)).then_inc(self.x_loaded[j], 16)
            if j == 0 and self.pre_gain is not None:
                sp.dma_start(self.g_pre[:], self.pre_gain.broadcast_to([P, D])).then_inc(self.gains_loaded, 16)
        if self.coming_after is None:
            self.fetch_coming(sp)
        if self.x_out is not None:
            for n in range(NT):
                sp.wait_ge(self.x_new, n + 1)
                sp.dma_start(self.x_out[n * P:(n + 1) * P, :], self.x[:, n, :]).then_inc(self.x_stored, 16)
            if self.coming_after is not None:
                sp.wait_ge(*self.coming_after)
                self.fetch_coming(sp)
            sp.wait_ge(self.x_stored, 16 * NT)
        if self.coming:
            sp.wait_ge(self.came, 16 * len(self.coming))

    def fetch_coming(self, sp):
        for buffer, source in self.coming:
            sp.dma_start(buffer, source).then_inc(self.came, 16)

    def scalar(self, act, before=None):
        nc, chip, y, x = self.nc, self.chip, self.chip.y, self.x
        done = [0]

        def root_mean_square(j, source, squared, root, n):
            if done[0]:
                act.wait_ge(*done[1])
            nc.scalar.activation(self.junk[:], source, ACT.Square, accum_out=self.stat(j, n)).then_inc(squared, 1)
            act.wait_ge(squared, n + 1)
            nc.scalar.activation(self.stat(j + 1, n), self.stat(j, n), ACT.Sqrt, bias=chip.eps[:, 0:1],
                                 scale=1.0 / D).then_inc(root, 1)
            done[:] = [1, (squared, n + 1)]

        for s in range(NT + self.lag):
            if before is not None and s < NT:
                before(s)
            if self.post_gain is not None and s < NT:
                if self.y_done is not None:
                    act.wait_ge(self.y_done[0], self.y_done[1] + s + 1)
                root_mean_square(0, y[:, s, :], self.y_squared, self.y_root, s)
            n = s - 2
            if self.pre_gain is not None and 0 <= n < NT:
                if self.post_gain is not None:
                    act.wait_ge(self.x_new, n + 1)
                else:
                    act.wait_ge(self.x_loaded[n // self.PER_LOAD], 16)
                root_mean_square(3, x[:, n, :], self.x_squared, self.x_root, n)
            n = s - self.lag
            if self.pre_gain is not None and 0 <= n < NT:
                act.wait_ge(self.turned, n + 1)
                b = 2 * (n % 2)
                nc.scalar.activation(chip.hT[0][:, :, n * P:(n + 1) * P],
                                     chip.banks[:, b:b + 2, :].rearrange("p a (k t) -> p (a k) t", t=P),
                                     ACT.Copy).then_inc(self.hi_done, 1)

    def gpsimd(self, pool):
        if self.post_gain is None:
            return
        for n in range(NT):
            if n % self.PER_LOAD == 0:
                pool.wait_ge(self.x_loaded[n // self.PER_LOAD], 16)
            pool.wait_ge(self.y_normed, n + 1)
            self.nc.gpsimd.tensor_tensor(self.x[:, n, :], self.x[:, n, :], self.chip.y[:, n, :], ALU.add).then_inc(self.x_new, 1)

    def vector(self, dve, before=None):
        nc, chip, y, x = self.nc, self.chip, self.chip.y, self.x
        hT_hi, hT_lo = chip.hT

        def normed(j, source, root, inverse, gain, done, n):
            dve.wait_ge(root, n + 1)
            nc.vector.reciprocal(self.stat(j + 2, n), self.stat(j + 1, n)).then_inc(inverse, 1)
            dve.wait_ge(inverse, n + 1)
            nc.vector.scalar_tensor_tensor(out=y[:, n, :], in0=source, scalar=self.stat(j + 2, n), in1=gain[:],
                                           op0=ALU.mult, op1=ALU.mult).then_inc(done, 1)

        for s in range(NT + self.lag + 1):
            if before is not None and s < NT:
                before(s)
            if s == 0:
                dve.wait_ge(self.gains_loaded, self.gains)
            if self.post_gain is not None and 0 <= s - 1 < NT:
                normed(0, y[:, s - 1, :], self.y_root, self.y_inverse, self.g_post, self.y_normed, s - 1)
            if self.pre_gain is not None and 0 <= s - 3 < NT:
                normed(3, x[:, s - 3, :], self.x_root, self.x_inverse, self.g_pre, self.x_normed, s - 3)
            n = s - self.lag - 1
            if self.pre_gain is not None and 0 <= n < NT:
                dve.wait_ge(self.hi_done, n + 1)
                b = 2 * (n % 2)
                nc.vector.tensor_tensor(hT_lo[:, :, n * P:(n + 1) * P],
                                        chip.banks[:, b:b + 2, :].rearrange("p a (k t) -> p (a k) t", t=P),
                                        hT_hi[:, :, n * P:(n + 1) * P].bitcast(F32), ALU.subtract).then_inc(self.lo_done, 1)

    def tensor(self, pe):
        if self.pre_gain is None:
            return
        for n in range(NT):
            pe.wait_ge(self.x_normed, n + 1)
            if n >= 2:
                pe.wait_ge(self.lo_done, n - 1)
            for k in range(KD):
                last = self.nc.tensor.transpose(self.chip.banks[:, 2 * (n % 2) + k // 4, (k % 4) * P:(k % 4 + 1) * P],
                                                self.chip.y[:, n, k * P:(k + 1) * P], self.chip.ident[:])
            last.then_inc(self.turned, 1)


def first_norm_stage(nc, chip, ctx, norm, w_fm):
    coming = [(raw[:], w_fm[c].rearrange("p (k c) -> p k c", k=KD)) for c, raw in enumerate(projection_raw(chip))]
    norm = Norm(nc, chip, coming=coming, **norm)
    filled, cut = (chip.semaphore(f"const_{n}") for n in ("filled", "cut"))
    block = ctx.enter_context(nc.Block())

    @block.gpsimd
    def _(pool):
        make_constants(nc, chip, pool, filled, cut)

    @block.sync
    def _(sp):
        norm.sync(sp)

    @block.scalar
    def _(act):
        act.wait_ge(filled, 1)
        norm.scalar(act)

    @block.vector
    def _(dve):
        norm.vector(dve)

    @block.tensor
    def _(pe):
        pe.wait_ge(cut, 4)
        norm.tensor(pe)


def feature_major_product(nc, chip, first_bank, w_hi, w_lo):
    hT_hi, hT_lo = chip.hT
    for k in range(KD):
        for j, (w, h) in enumerate(((w_hi, hT_hi), (w_hi, hT_lo), (w_lo, hT_hi))):
            for half in range(2):
                last = nc.tensor.matmul(chip.banks[:, first_bank + half, :], w[:, k, :],
                                        h[:, k, half * HALF:(half + 1) * HALF],
                                        start=(k == 0 and j == 0), stop=(k == KD - 1 and j == 2))
    return last


def ffn_raw_up(chip):
    return [chip.at(f"ffn_raw_up{c}", WORK + 64 + 8 * j, [P, 2, KD, P]) for j, c in enumerate("ab")]


def ffn_coming(chip, w_up):
    return [(raw[:], w_up[c].rearrange("p (s k c) -> p s k c", s=2, k=KD)) for c, raw in enumerate(ffn_raw_up(chip))]


def gmlp_v_raw(chip):
    return [chip.at(f"v_raw{b}", Y_AT + 128 + 4 * b, [P, 2, HALF]) for b in range(2)]


def gmlp_v_coming(chip, w_v):
    return [(raw[:], w_v[q].rearrange("p (k n) -> p k n", k=2)) for q, raw in enumerate(gmlp_v_raw(chip))]


def gmlp_raw_up(chip):
    return [chip.at(f"sg_raw_up{c}", WORK + 98 + 4 * j, [P, KD, P]) for j, c in enumerate("ab")]


def gmlp_up_split(chip):
    return [[chip.at(f"sg_up_{n}{c}", WORK + 32 + 8 * j + 4 * x, [P, KD, P], F32R) for j, c in enumerate("ab")]
            for x, n in enumerate(("hi", "lo"))]


def gmlp_spatial(chip):
    return chip.at("sg_w_spT", WORK + 64, [P, KE, P]), chip.at("sg_ones", WORK + 107.5, [P, 1])


def ffn_stage(nc, chip, ctx, tag, w_up, w_down, conv, norm):
    sem = lambda n: chip.semaphore(f"{tag}_{n}")
    ROUNDS = KF // 2
    up_loaded = [sem(f"up_loaded_{c}") for c in "ab"]
    down_loaded, conv_loaded = sem("down_loaded"), sem("conv_loaded")
    up_w_hi, up_w_ready = sem("up_w_hi"), sem("up_w_ready")
    down_w_hi, down_w_ready = sem("down_w_hi"), sem("down_w_ready")
    up_done = [sem(f"up_done_{c}") for c in "gv"]
    centre = [sem(f"centre_{c}") for c in "gv"]
    cur_ready = sem("cur_ready")
    conv_step, gated_ready, prod_ready = sem("conv_step"), sem("gated_ready"), sem("prod_ready")
    conv_done = [sem(f"conv_done_{c}") for c in "gv"]
    prod_hi, prod_split = sem("prod_hi"), sem("prod_split")
    down_done, y_free = sem("down_done"), sem("y_free")

    first_hi, first_low = sem("first_hi"), [sem(f"first_low_{c}") for c in "gv"]

    raw_up = ffn_raw_up(chip)
    raw_down = chip.at("ffn_raw_down", WORK + 96, [P, 2, D])
    up_hi = [chip.at(f"ffn_up_hi{c}", WORK + 16 * j, [P, 2, KD, P], F32R) for j, c in enumerate("ab")]
    up_lo = [chip.at(f"ffn_up_lo{c}", WORK + 8 + 16 * j, [P, 2, KD, P], F32R) for j, c in enumerate("ab")]
    down_hi = chip.at(f"ffn_down_hi", WORK + 46, [P, 2, D], F32R)
    down_lo = chip.at(f"ffn_down_lo", WORK + 54, [P, 2, D], F32R)
    p_hi = [chip.at(f"ffn_p_hi{c}", WORK + 80 + 8 * j, [P, T], F32R) for j, c in enumerate("ab")]
    p_lo = [chip.at(f"ffn_p_lo{c}", WORK + 84 + 8 * j, [P, T], F32R) for j, c in enumerate("ab")]
    cg = [chip.at(f"ffn_conv_{c}", WORK + 32 + 4 * j, [P, T]) for j, c in enumerate("gv")]
    prod = chip.at("ffn_prod", WORK + 40, [P, T])
    cw = chip.at("ffn_cw", WORK + 44, [P, KF, 2, 4])
    cur = [chip.at(f"ffn_cur{j}", WORK + 45.5 + 0.125 * j, [P, 2, 4]) for j in range(2)]
    banks, y = chip.banks, chip.y
    up_bank = [banks[:, 0:2, :], banks[:, 2:4, :]]
    norm = Norm(nc, chip, y_done=(y_free, (ROUNDS - 1) * NT + 2), lag=6, **norm)
    block = ctx.enter_context(nc.Block())

    @block.sync
    def _(sp):
        def load_up(c, n, wait):
            sp.wait_ge(up_w_ready, wait)
            sp.dma_start(raw_up[c][:], w_up[n].rearrange("p (s k c) -> p s k c", s=2, k=KD)).then_inc(up_loaded[c], 16)

        def load_down(i, wait=None):
            if wait is not None:
                sp.wait_ge(down_w_ready, wait)
            sp.dma_start(raw_down[:], w_down[i].rearrange("p (s n) -> p s n", s=2)).then_inc(down_loaded, 16)

        sp.dma_start(cw[:], conv).then_inc(conv_loaded, 16)
        load_down(0)
        for s in range(2):
            sp.wait_ge(first_low[s], 1)
        with sp.Fori(0, ROUNDS - 1) as i:
            load_up(0, i * 2 + 2, wait=i * 2 + 1)
            load_up(1, i * 2 + 3, wait=i * 2 + 2)
            load_down(i + 1, wait=i + 1)
        sp.wait_ge(prod_split, KF)
        sp.wait_ge(down_w_ready, ROUNDS)
        norm.sync(sp)

    @block.scalar
    def _(act):
        def split_up(c, n, wait=None):
            if wait is not None:
                act.wait_ge(up_loaded[c], (n - c) * 8)
                act.wait_ge(up_done[1], wait)
            nc.scalar.activation(up_hi[c][:], raw_up[c][:], ACT.Copy).then_inc(up_w_hi, 1)

        def split_down(i, wait=None):
            act.wait_ge(down_loaded, i * 16 + 16)
            if wait is not None:
                act.wait_ge(down_done, wait)
            nc.scalar.activation(down_hi[:], raw_down[:], ACT.Copy).then_inc(down_w_hi, 1)

        def convolved(c, n):
            for s in range(2):
                act.wait_ge(up_done[s], n + 1)
                if s == 1:
                    act.wait_ge(prod_ready, n)
                act.wait_ge(cur_ready, n + 1)
                nc.scalar.activation(cg[s][:], pair(up_bank[s]), ACT.Identity, bias=cur[c][:, s, 3:4],
                                     scale=cur[c][:, s, 2:3]).then_inc(centre[s], 1)
            act.wait_ge(conv_done[0], n + 1)
            act.wait_ge(prod_split, n)
            nc.scalar.activation(prod[:], cg[0][:], ACT.Silu).then_inc(gated_ready, 1)

        def product_hi(c, n, wait=None):
            act.wait_ge(prod_ready, n + 1)
            if wait is not None:
                act.wait_ge(down_done, wait)
            nc.scalar.activation(p_hi[c][:], prod[:], ACT.Copy).then_inc(prod_hi, 1)

        for s in range(2):
            nc.scalar.activation(up_hi[0][:, s], raw_up[0][:, s], ACT.Copy).then_inc(first_hi, 1)
        split_up(1, 1)
        convolved(0, 0)
        product_hi(0, 0)
        split_down(0)
        with act.Fori(0, ROUNDS - 1) as i:
            split_up(0, i * 2 + 2, wait=i * 2 + 1)
            convolved(1, i * 2 + 1)
            product_hi(1, i * 2 + 1)
            split_up(1, i * 2 + 3, wait=i * 2 + 2)
            convolved(0, i * 2 + 2)
            product_hi(0, i * 2 + 2, wait=i * NT + NT)
            split_down(i + 1, wait=i * NT + NT)
        convolved(1, KF - 1)
        product_hi(1, KF - 1)
        norm.scalar(act)

    @block.gpsimd
    def _(pool):
        def up_low(c, n):
            pool.wait_ge(up_w_hi, n)
            nc.gpsimd.tensor_tensor(up_lo[c][:], raw_up[c][:], up_hi[c][:].bitcast(F32), ALU.subtract).then_inc(up_w_ready, 1)

        def down_low(i):
            pool.wait_ge(down_w_hi, i + 1)
            nc.gpsimd.tensor_tensor(down_lo[:], raw_down[:], down_hi[:].bitcast(F32), ALU.subtract).then_inc(down_w_ready, 1)

        def product_low(c, n):
            pool.wait_ge(prod_hi, n + 1)
            nc.gpsimd.tensor_tensor(p_lo[c][:], prod[:], p_hi[c][:].bitcast(F32), ALU.subtract).then_inc(prod_split, 1)

        def first_up_low(s):
            pool.wait_ge(first_hi, s + 1)
            nc.gpsimd.tensor_tensor(up_lo[0][:, s], raw_up[0][:, s], up_hi[0][:, s].bitcast(F32),
                                    ALU.subtract).then_inc(first_low[s], 1)

        pool.sem_inc(up_w_ready, 1)
        first_up_low(1)
        up_low(1, 1)
        product_low(0, 0)
        down_low(0)
        with pool.Fori(0, ROUNDS - 1) as i:
            up_low(0, i * 2 + 2)
            product_low(1, i * 2 + 1)
            up_low(1, i * 2 + 3)
            product_low(0, i * 2 + 2)
            down_low(i + 1)
        product_low(1, KF - 1)
        norm.gpsimd(pool)

    @block.vector
    def _(dve):
        def fetch_taps(c, n):
            nc.vector.tensor_copy(cur[c][:], cw[:, bass.ds(n, 1), :, :].rearrange("p a s j -> p (a s) j")).then_inc(cur_ready, 1)

        def convolve(c, n):
            dve.wait_ge(cur_ready, n + 1)
            for s in range(2):
                dve.wait_ge(centre[s], n + 1)
                h = pair(up_bank[s])
                nc.vector.scalar_tensor_tensor(out=cg[s][:, 1:T], in0=h[:, 0:T - 1], scalar=cur[c][:, s, 1:2],
                                               in1=cg[s][:, 1:T], op0=ALU.mult, op1=ALU.add).then_inc(conv_step, 1)
                dve.wait_ge(conv_step, n * 2 + (s + 1))
                nc.vector.scalar_tensor_tensor(out=cg[s][:, 2:T], in0=h[:, 0:T - 2], scalar=cur[c][:, s, 0:1],
                                               in1=cg[s][:, 2:T], op0=ALU.mult, op1=ALU.add).then_inc(conv_done[s], 1)

        def gate_value(n):
            dve.wait_ge(gated_ready, n + 1)
            dve.wait_ge(conv_done[1], n + 1)
            nc.vector.tensor_tensor(prod[:], prod[:], cg[1][:], ALU.mult).then_inc(prod_ready, 1)

        def add_down(i, t):
            dve.wait_ge(down_done, i * NT + (t + 1))
            b = 4 + 2 * (t % 2)
            nc.vector.tensor_tensor(y[:, t, :], y[:, t, :], pair(banks[:, b:b + 2, :]), ALU.add).then_inc(y_free, 1)

        dve.wait_ge(first_hi, 1)
        nc.vector.tensor_tensor(up_lo[0][:, 0], raw_up[0][:, 0], up_hi[0][:, 0].bitcast(F32),
                                ALU.subtract).then_inc(first_low[0], 1)
        dve.wait_ge(conv_loaded, 16)
        nc.vector.memset(y[:], 0.0).then_inc(y_free, 2)
        dve.wait_ge(y_free, 2)
        fetch_taps(0, 0)
        fetch_taps(1, 1)
        convolve(0, 0)
        gate_value(0)
        with dve.Fori(0, ROUNDS - 1) as i:
            fetch_taps(0, i * 2 + 2)
            convolve(1, i * 2 + 1)
            gate_value(i * 2 + 1)
            fetch_taps(1, i * 2 + 3)
            convolve(0, i * 2 + 2)
            dve.wait_ge(y_free, i * NT + 2)
            add_down(i, 0)
            gate_value(i * 2 + 2)
            for t in range(1, NT):
                add_down(i, t)
        convolve(1, KF - 1)
        gate_value(KF - 1)
        dve.wait_ge(y_free, (ROUNDS - 1) * NT + 2)
        norm.vector(dve, before=lambda t: add_down(ROUNDS - 1, t))

    @block.tensor
    def _(pe):
        def up(c, n, first=False):
            if not first:
                pe.wait_ge(up_w_ready, n + 1)
            for s in range(2):
                if first:
                    pe.wait_ge(first_low[s], 1)
                pe.wait_ge(conv_done[s], n)
                feature_major_product(nc, chip, 2 * s, up_hi[c][:, s], up_lo[c][:, s]).then_inc(up_done[s], 1)

        up(0, 0, first=True)
        with pe.Fori(0, ROUNDS - 1) as i:
            up(1, i * 2 + 1)
            up(0, i * 2 + 2)
            down_product(nc, chip, pe, i, p_hi, p_lo, down_hi, down_lo, prod_split, down_w_ready, y_free, down_done)
        up(1, KF - 1)
        down_product(nc, chip, pe, ROUNDS - 1, p_hi, p_lo, down_hi, down_lo, prod_split, down_w_ready, y_free, down_done,
                     a_first=2)
        norm.tensor(pe)


def down_product(nc, chip, pe, i, p_hi, p_lo, w_hi, w_lo, prod_split, w_ready, y_free, down_done, a_first=0):
    def product(c, t):
        b = 4 + 2 * (t % 2)
        for j, (p, w) in enumerate(((p_hi, w_hi), (p_hi, w_lo), (p_lo, w_hi))):
            for half in range(2):
                last = nc.tensor.matmul(chip.banks[:, b + half, :], p[c][:, t * P:(t + 1) * P],
                                        w[:, c, half * HALF:(half + 1) * HALF],
                                        start=(c == 0 and j == 0), stop=(c == 1 and j == 2))
        return last

    pe.wait_ge(w_ready, i + 1)
    if a_first:
        pe.wait_ge(prod_split, i * 2 + 1)
        for t in range(a_first):
            pe.wait_ge(y_free, i * NT + (t + 1))
            product(0, t)
    pe.wait_ge(prod_split, i * 2 + 2)
    for t in range(NT):
        if t >= a_first:
            pe.wait_ge(y_free, i * NT + (t + 1))
            product(0, t)
        product(1, t).then_inc(down_done, 1)


def gmlp_v_stage(nc, chip, ctx, w_v, v_out, w_u, w_sp):
    sem = lambda n: chip.semaphore(f"v_{n}")
    CHUNKS, PIECES, KP = E // HALF, 4, 2
    raw_loaded = [sem(f"raw_loaded{b}") for b in range(2)]
    w_hi_done, w_ready, v_done, gelu_done = sem("w_hi_done"), sem("w_ready"), sem("v_done"), sem("gelu_done")
    counted, averaged, root_done, inverse_done = sem("counted"), sem("averaged"), sem("root_done"), sem("inverse_done")
    v_normed, v_stored = sem("v_normed"), sem("v_stored")
    up_came, up_w_hi, up_w_ready, u_done = sem("up_came"), sem("up_w_hi"), sem("up_w_ready"), sem("u_done")
    ones_set, w_sp_came, masked, summed = sem("ones_set"), sem("w_sp_came"), sem("masked"), sem("summed")
    raw_up, (up_hi, up_lo), (w_spT, ones) = gmlp_raw_up(chip), gmlp_up_split(chip), gmlp_spatial(chip)
    v = chip.at("v", Y_AT, [P, NT, E])
    w_hi = chip.at("v_w_hi", Y_AT + 64, [P, 2, KD, HALF], F32R)
    w_lo = chip.at("v_w_lo", Y_AT + 96, [P, 2, KD, HALF], F32R)
    raw = gmlp_v_raw(chip)
    stats = chip.at("v_stats", Y_AT + 138.25, [P, NT, CHUNKS, 6])
    mean_var = chip.at("v_mean_var", Y_AT + 139, [P, NT, 2])
    dev = chip.at("v_dev", Y_AT + 139.125, [P, NT])
    inv = chip.at("v_inv", Y_AT + 139.25, [P, NT])
    hT_hi, hT_lo = chip.hT
    block = ctx.enter_context(nc.Block())

    @block.sync
    def _(sp):
        with sp.Fori(0, CHUNKS * PIECES // 2 - 1) as i:
            for q in range(2):
                sp.wait_ge(w_ready, i * 2 + (q + 1))
                sp.dma_start(raw[q][:], w_v[i * 2 + (q + 2)].rearrange("p (k n) -> p k n", k=KP)).then_inc(raw_loaded[q], 16)
        sp.wait_ge(w_ready, CHUNKS * PIECES)
        for c, buffer in enumerate(raw_up):
            sp.dma_start(buffer[:], w_u[c].rearrange("p (k c) -> p k c", k=KD)).then_inc(up_came, 16)
        sp.wait_ge(v_done, (CHUNKS - 1) * NT + 1)
        sp.dma_start(w_spT[:], w_sp.rearrange("s (g t) -> s g t", g=KE)).then_inc(w_sp_came, 16)
        sp.wait_ge(up_came, 32)
        for t in range(NT):
            sp.wait_ge(v_normed, t + 1)
            sp.dma_start(v_out[t * P:(t + 1) * P, :], v[:, t, :]).then_inc(v_stored, 16)
        sp.wait_ge(v_stored, 16 * NT)

    @block.scalar
    def _(act):
        def split(c, wait=None):
            if wait is not None:
                act.wait_ge(v_done, wait)
            for q in range(PIECES):
                if wait is not None or q >= 2:
                    act.wait_ge(raw_loaded[q % 2], c * 32 + (q // 2) * 16)
                nc.scalar.activation(w_hi[:, bass.ds(c % 2, 1), KP * q:KP * (q + 1), :].rearrange("p a k n -> p (a k) n"),
                                     raw[q % 2][:], ACT.Copy).then_inc(w_hi_done, 1)

        def gelu(c, t):
            act.wait_ge(v_done, c * NT + (t + 2))
            nc.scalar.activation(v[:, t, bass.ds(c * HALF, HALF)], chip.banks[:, t, :],
                                 ACT.Gelu_apprx_tanh).then_inc(gelu_done, 1)

        act.sem_inc(gelu_done, 1)
        split(0)
        with act.Fori(0, CHUNKS - 1) as c:
            split(c + 1, wait=c * NT + 1)
            for t in range(NT):
                gelu(c, t)

        def root(t):
            act.wait_ge(averaged, t + 1)
            nc.scalar.activation(dev[:, t:t + 1], mean_var[:, t, 1:2], ACT.Sqrt, bias=chip.eps[:, 0:1]).then_inc(root_done, 1)

        act.wait_ge(up_came, 32)
        act.wait_ge(v_done, (CHUNKS - 1) * NT + 1)
        for c in range(2):
            nc.scalar.activation(up_hi[c][:], raw_up[c][:], ACT.Copy).then_inc(up_w_hi, 1)
        for t in range(NT):
            gelu(CHUNKS - 1, t)
            if t >= 1:
                root(t - 1)
        root(NT - 1)

    @block.gpsimd
    def _(pool):
        nc.gpsimd.memset(ones[:], 1.0).then_inc(ones_set, 1)
        with pool.Fori(0, CHUNKS) as c:
            for q in range(PIECES):
                pool.wait_ge(w_hi_done, c * PIECES + (q + 1))
                at = lambda w: w[:, bass.ds(c % 2, 1), KP * q:KP * (q + 1), :].rearrange("p a k n -> p (a k) n")
                nc.gpsimd.tensor_tensor(at(w_lo), raw[q % 2][:], at(w_hi).bitcast(F32), ALU.subtract).then_inc(w_ready, 1)
        for c in range(2):
            pool.wait_ge(up_w_hi, c + 1)
            nc.gpsimd.tensor_tensor(up_lo[c][:], raw_up[c][:], up_hi[c][:].bitcast(F32), ALU.subtract).then_inc(up_w_ready, 1)
        pool.wait_ge(w_sp_came, 16)
        nc.gpsimd.affine_select(out=w_spT[:], in_=w_spT[:], compare_op=ALU.is_ge, fill=0.0, base=0,
                                pattern=[[0, KE], [1, P]], channel_multiplier=-1).then_inc(masked, 1)

    @block.vector
    def _(dve):
        def count(c, t):
            dve.wait_ge(gelu_done, c * NT + (t + 2))
            nc.vector.bn_stats(stats[:, t, bass.ds(c, 1), :].rearrange("p a s -> p (a s)"),
                               v[:, t, bass.ds(c * HALF, HALF)]).then_inc(counted, 1)

        def normalise(t):
            dve.wait_ge(root_done, t + 1)
            nc.vector.reciprocal(inv[:, t:t + 1], dev[:, t:t + 1]).then_inc(inverse_done, 1)
            dve.wait_ge(inverse_done, t + 1)
            nc.vector.tensor_scalar(v[:, t, :], v[:, t, :], mean_var[:, t, 0:1], inv[:, t:t + 1],
                                    ALU.subtract, ALU.mult).then_inc(v_normed, 1)

        with dve.Fori(0, CHUNKS - 1) as c:
            for t in range(NT):
                count(c, t)
        for t in range(NT):
            count(CHUNKS - 1, t)
            dve.wait_ge(counted, (CHUNKS - 1) * NT + t + 1)
            nc.vector.bn_aggr(mean_var[:, t, :], stats[:, t]).then_inc(averaged, 1)
            if t >= 1:
                normalise(t - 1)
        normalise(NT - 1)

    @block.tensor
    def _(pe):
        pe.sem_inc(v_done, 1)
        with pe.Fori(0, CHUNKS) as c:
            half = c % 2
            for t in range(NT):
                pe.wait_ge(gelu_done, c * NT + 1)
                for k in range(KD):
                    if t == 0 and k % KP == 0:
                        pe.wait_ge(w_ready, c * PIECES + (k // KP + 1))
                    for j, (h, w) in enumerate(((hT_hi, w_hi), (hT_hi, w_lo), (hT_lo, w_hi))):
                        last = nc.tensor.matmul(chip.banks[:, t, :], h[:, k, t * P:(t + 1) * P],
                                                w[:, bass.ds(half, 1), k, :].rearrange("p a n -> p (a n)"),
                                                start=(k == 0 and j == 0), stop=(k == KD - 1 and j == 2))
                last.then_inc(v_done, 1)
        pe.wait_ge(up_w_ready, 1)
        pe.wait_ge(gelu_done, (CHUNKS - 1) * NT + 3)
        feature_major_product(nc, chip, 0, up_hi[0], up_lo[0]).then_inc(u_done, 1)
        pe.wait_ge(ones_set, 1)
        pe.wait_ge(masked, 1)
        pe.wait_ge(gelu_done, CHUNKS * NT + 1)
        for b in range(4):
            last = nc.tensor.matmul(chip.banks[0:1, 4 + b, :], ones[:, 0:1],
                                    w_spT[:, 4 * b:4 * b + 4, :].rearrange("s g t -> s (g t)"), start=True, stop=True)
        last.then_inc(summed, 1)


def gmlp_stage(nc, chip, ctx, w_u, w_down, v_in, ln_g, ln_b, b_sp, norm):
    sem = lambda n: chip.semaphore(f"sg_{n}")
    ROUNDS = KE // 2
    up_loaded, v_loaded = ([sem(f"{n}_{c}") for c in "ab"] for n in ("up_loaded", "v_loaded"))
    down_loaded, gain_loaded = sem("down_loaded"), sem("gain_loaded")
    up_w_hi, up_w_ready, down_w_hi, down_w_ready = sem("up_w_hi"), sem("up_w_ready"), sem("down_w_hi"), sem("down_w_ready")
    u_done, mix_done, gelu_done, cur_ready, mix_biased = (
        sem("u_done"), sem("mix_done"), sem("gelu_done"), sem("cur_ready"), sem("mix_biased"))
    prod_ready, prod_hi, prod_split = sem("prod_ready"), sem("prod_hi"), sem("prod_split")
    down_done, y_free = sem("down_done"), sem("y_free")
    ones_set, rows_loaded, sums_kept, spread, bias_kept = (
        sem(n) for n in ("ones_set", "rows_loaded", "sums_kept", "spread", "bias_kept"))

    raw_up = gmlp_raw_up(chip)
    raw_down = chip.at("sg_raw_down", WORK + 8, [P, 2, D])
    up_hi, up_lo = gmlp_up_split(chip)
    down_hi = chip.at("sg_down_hi", WORK + 48, [P, 2, D], F32R)
    down_lo = chip.at("sg_down_lo", WORK + 56, [P, 2, D], F32R)
    p_hi = [chip.at(f"sg_p_hi{c}", WORK + 82 + 8 * j, [P, T], F32R) for j, c in enumerate("ab")]
    p_lo = [chip.at(f"sg_p_lo{c}", WORK + 86 + 8 * j, [P, T], F32R) for j, c in enumerate("ab")]
    u = chip.at("sg_u", WORK, [P, T])
    prod = chip.at("sg_prod", WORK + 4, [P, T])
    vg = [chip.at(f"sg_v{c}", WORK + 24 + 4 * j, [P, NT, P]) for j, c in enumerate("ab")]
    gain = chip.at("sg_gain", WORK + 80, [P, KE])
    cur = [chip.at(f"sg_cur{j}", WORK + 80.5 + 0.125 * j, [P, 1]) for j in range(2)]
    w_spT, _ = gmlp_spatial(chip)
    bias = chip.at("sg_bias", WORK + 72, [P, KE, P])
    left, right = (chip.at(f"sg_rows{j}", WORK + 82 + 8 * j, [2, E]) for j in range(2))
    banks, y = chip.banks, chip.y
    norm = Norm(nc, chip, y_done=(y_free, (ROUNDS - 1) * NT + 2), lag=6, **norm)
    block = ctx.enter_context(nc.Block())

    @block.sync
    def _(sp):
        def load_up(c, n, wait=None):
            if wait is not None:
                sp.wait_ge(up_w_ready, wait)
                sp.dma_start(raw_up[c][:], w_u[n].rearrange("p (k c) -> p k c", k=KD)).then_inc(up_loaded[c], 16)
                sp.wait_ge(mix_done, wait)
            sp.dma_start(vg[c][:], v_in[:, bass.ds(n * P, P)].rearrange("(n p) f -> p n f", p=P)).then_inc(v_loaded[c], 16)

        def load_down(i, wait=None):
            if wait is not None:
                sp.wait_ge(down_w_ready, wait)
            sp.dma_start(raw_down[:], w_down[i].rearrange("p (s n) -> p s n", s=2)).then_inc(down_loaded, 16)

        load_up(0, 0)
        sp.wait_ge(ones_set, 1)
        sp.dma_start(left[0:1, :], ln_b).then_inc(rows_loaded, 16)
        sp.dma_start(right[1:2, :], b_sp).then_inc(rows_loaded, 16)
        sp.dma_start(gain[:], ln_g).then_inc(gain_loaded, 16)
        load_up(1, 1)
        load_down(0)
        with sp.Fori(0, ROUNDS - 1) as i:
            load_up(0, i * 2 + 2, wait=i * 2 + 1)
            load_up(1, i * 2 + 3, wait=i * 2 + 2)
            load_down(i + 1, wait=i + 1)
        sp.wait_ge(prod_split, KE)
        sp.wait_ge(down_w_ready, ROUNDS)
        norm.sync(sp)

    @block.scalar
    def _(act):
        def split_up(c, n, wait):
            act.wait_ge(up_loaded[c], (n - c) * 8)
            act.wait_ge(u_done, wait)
            nc.scalar.activation(up_hi[c][:], raw_up[c][:], ACT.Copy).then_inc(up_w_hi, 1)

        def split_down(i, wait=None):
            act.wait_ge(down_loaded, i * 16 + 16)
            if wait is not None:
                act.wait_ge(down_done, wait)
            nc.scalar.activation(down_hi[:], raw_down[:], ACT.Copy).then_inc(down_w_hi, 1)

        def gelu(n):
            act.wait_ge(u_done, n + 1)
            act.wait_ge(prod_ready, n)
            nc.scalar.activation(u[:], pair(banks[:, 0:2, :]), ACT.Gelu_apprx_tanh).then_inc(gelu_done, 1)

        def product_hi(c, n, wait=None):
            act.wait_ge(prod_ready, n + 1)
            if wait is not None:
                act.wait_ge(down_done, wait)
            nc.scalar.activation(p_hi[c][:], prod[:], ACT.Copy).then_inc(prod_hi, 1)

        gelu(0)
        product_hi(0, 0)
        split_down(0)
        with act.Fori(0, ROUNDS - 1) as i:
            split_up(0, i * 2 + 2, wait=i * 2 + 1)
            gelu(i * 2 + 1)
            product_hi(1, i * 2 + 1)
            split_up(1, i * 2 + 3, wait=i * 2 + 2)
            gelu(i * 2 + 2)
            product_hi(0, i * 2 + 2, wait=i * NT + NT)
            split_down(i + 1, wait=i * NT + NT)
        gelu(KE - 1)
        product_hi(1, KE - 1)
        norm.scalar(act)

    @block.gpsimd
    def _(pool):
        def up_low(c, n):
            pool.wait_ge(up_w_hi, n - 1)
            nc.gpsimd.tensor_tensor(up_lo[c][:], raw_up[c][:], up_hi[c][:].bitcast(F32), ALU.subtract).then_inc(up_w_ready, 1)

        def down_low(i):
            pool.wait_ge(down_w_hi, i + 1)
            nc.gpsimd.tensor_tensor(down_lo[:], raw_down[:], down_hi[:].bitcast(F32), ALU.subtract).then_inc(down_w_ready, 1)

        def product_low(c, n):
            pool.wait_ge(prod_hi, n + 1)
            nc.gpsimd.tensor_tensor(p_lo[c][:], prod[:], p_hi[c][:].bitcast(F32), ALU.subtract).then_inc(prod_split, 1)

        nc.gpsimd.memset(left[:], 1.0).then_inc(ones_set, 1)
        pool.sem_inc(up_w_ready, 2)
        product_low(0, 0)
        down_low(0)
        with pool.Fori(0, ROUNDS - 1) as i:
            up_low(0, i * 2 + 2)
            product_low(1, i * 2 + 1)
            up_low(1, i * 2 + 3)
            product_low(0, i * 2 + 2)
            down_low(i + 1)
        product_low(1, KE - 1)
        norm.gpsimd(pool)

    @block.vector
    def _(dve):
        def fetch_gain(c, n):
            nc.vector.tensor_copy(cur[c][:], gain[:, bass.ds(n, 1)]).then_inc(cur_ready, 1)

        def combine(c, n):
            dve.wait_ge(cur_ready, n + 1)
            dve.wait_ge(mix_done, n + 1)
            dve.wait_ge(bias_kept, 1)
            dve.wait_ge(prod_split, n)
            nc.vector.scalar_tensor_tensor(
                out=prod[:].rearrange("p (n t) -> p n t", t=P),
                in0=pair(banks[:, 2:4, :]).rearrange("p (n t) -> p n t", t=P), scalar=cur[c][:, 0:1],
                in1=bias[:, bass.ds(n, 1), :].broadcast_to([P, NT, P]),
                op0=ALU.mult, op1=ALU.add).then_inc(mix_biased, 1)
            dve.wait_ge(mix_biased, n + 1)
            dve.wait_ge(gelu_done, n + 1)
            nc.vector.tensor_tensor(prod[:], prod[:], u[:], ALU.mult).then_inc(prod_ready, 1)

        def add_down(i, t):
            dve.wait_ge(down_done, i * NT + (t + 1))
            b = 4 + 2 * (t % 2)
            nc.vector.tensor_tensor(y[:, t, :], y[:, t, :], pair(banks[:, b:b + 2, :]), ALU.add).then_inc(y_free, 1)

        nc.vector.tensor_copy(right[0:1, :], pair(banks[0:1, 4:8, :])).then_inc(sums_kept, 1)
        dve.wait_ge(gain_loaded, 16)
        nc.vector.memset(y[:], 0.0).then_inc(y_free, 2)
        dve.wait_ge(y_free, 2)
        fetch_gain(0, 0)
        fetch_gain(1, 1)
        dve.wait_ge(spread, 1)
        nc.vector.tensor_copy(bias[:].rearrange("p g t -> p (g t)"), pair(banks[:, 4:8, :])).then_inc(bias_kept, 1)
        combine(0, 0)
        with dve.Fori(0, ROUNDS - 1) as i:
            fetch_gain(0, i * 2 + 2)
            combine(1, i * 2 + 1)
            fetch_gain(1, i * 2 + 3)
            combine(0, i * 2 + 2)
            dve.wait_ge(y_free, i * NT + 2)
            for t in range(NT):
                add_down(i, t)
        combine(1, KE - 1)
        dve.wait_ge(y_free, (ROUNDS - 1) * NT + 2)
        norm.vector(dve, before=lambda t: add_down(ROUNDS - 1, t))

    @block.tensor
    def _(pe):
        def gate(c, n):
            pe.wait_ge(up_w_ready, n + 1)
            pe.wait_ge(gelu_done, n)
            feature_major_product(nc, chip, 0, up_hi[c], up_lo[c]).then_inc(u_done, 1)

        def mix(c, n):
            pe.wait_ge(v_loaded[c], (n - c) * 8 + 16)
            pe.wait_ge(mix_biased, n)
            for s in range(NT):
                last = nc.tensor.matmul(banks[:, 2 + s // 4, (s % 4) * P:(s % 4 + 1) * P], vg[c][:, s, :],
                                        w_spT[:, bass.ds(n, 1), :].rearrange("s a t -> s (a t)"), start=True, stop=True)
            last.then_inc(mix_done, 1)

        def up(c, n):
            gate(c, n)
            mix(c, n)

        pe.sem_inc(u_done, 1)
        mix(0, 0)
        pe.wait_ge(rows_loaded, 32)
        pe.wait_ge(sums_kept, 1)
        for g in range(KE):
            last = nc.tensor.matmul(banks[:, 4 + g // 4, (g % 4) * P:(g % 4 + 1) * P], left[:, g * P:(g + 1) * P],
                                    right[:, g * P:(g + 1) * P], start=True, stop=True)
        last.then_inc(spread, 1)
        with pe.Fori(0, ROUNDS - 1) as i:
            up(1, i * 2 + 1)
            up(0, i * 2 + 2)
            down_product(nc, chip, pe, i, p_hi, p_lo, down_hi, down_lo, prod_split, down_w_ready, y_free, down_done)
        up(1, KE - 1)
        down_product(nc, chip, pe, ROUNDS - 1, p_hi, p_lo, down_hi, down_lo, prod_split, down_w_ready, y_free, down_done,
                     a_first=2)
        norm.tensor(pe)


FT_AT, KT_AT, V_AT, SEL_AT, ONEHOT_AT, VC_AT = 68, 116, 148, 164, 166, 174
SLC, WIN = 0, 1


class NsaState:

    def __init__(self, chip):
        self.qT = chip.at("qT", FT_AT, [P, HEADS // 2, T])
        self.cmp_in = chip.at("cmp_in", FT_AT + 32, [P, 2, GROUPS, T // 2])
        self.kT = chip.at("kT", KT_AT, [P, 2, GROUPS, T])
        self.v = chip.at("v_tok", V_AT, [P, NT, 2 * KVW])
        self.selT = chip.at("selT", SEL_AT, [GROUPS * NSLC, T], BF16)
        self.onehot = chip.at("onehot", ONEHOT_AT, [GROUPS * NSLC, GROUPS, T], BF16)
        self.p_cmp_stored = [chip.nc.alloc_semaphore(name=f"p_cmp_stored{b}") for b in range(2)]
        self.vc = chip.at("vc_split", VC_AT, [NCMP, GROUPS, P], F32R)


def projection_raw(chip):
    return [chip.at(f"proj_raw_{c}", 164 + 4 * j, [P, KD, P]) for j, c in enumerate("ab")]


def nsa_projection_stage(nc, chip, ctx, nsa, w_fm, w_tok):
    sem = lambda n: chip.semaphore(f"proj_{n}")
    loaded, value_loaded = ([sem(f"{n}_{c}") for c in "ab"] for n in ("loaded", "value_loaded"))
    w_hi_done, w_ready, product_done, kept = sem("w_hi_done"), sem("w_ready"), sem("product_done"), sem("kept")
    value_w_hi, value_w_ready = sem("value_w_hi"), sem("value_w_ready")
    raw = projection_raw(chip)
    w_hi = [chip.at(f"proj_hi_{c}", 172 + 8 * j, [P, KD, P], F32R) for j, c in enumerate("ab")]
    w_lo = [chip.at(f"proj_lo_{c}", 176 + 8 * j, [P, KD, P], F32R) for j, c in enumerate("ab")]
    ROUNDS, Q_ROUNDS = FM_TILES // 2, HEADS // 4
    WIDTHS = [KVW, KVW + GATES]
    RAW_AT, HI_AT = (188, 164), (196, 176)
    value_raw = [chip.at(f"proj_value_raw{p}", RAW_AT[p], [P, KD, WIDTHS[p]]) for p in range(2)]
    value_lo = [chip.at(f"proj_value_lo{p}", RAW_AT[p], [P, KD, WIDTHS[p]], F32R) for p in range(2)]
    value_hi = [chip.at(f"proj_value_hi{p}", HI_AT[p], [P, KD, WIDTHS[p]], F32R) for p in range(2)]
    hT_hi, hT_lo = chip.hT
    bank_of = lambda t: (t + 4) % 8
    block = ctx.enter_context(nc.Block())

    @block.sync
    def _(sp):
        def load(c, n):
            sp.dma_start(raw[c][:], w_fm[n].rearrange("p (k c) -> p k c", k=KD)).then_inc(loaded[c], 16)

        def load_values(p):
            sp.dma_start(value_raw[p][:], w_tok[:, KD * KVW * p:KD * (KVW * p + WIDTHS[p])].rearrange(
                "p (k n) -> p k n", k=KD)).then_inc(value_loaded[p], 16)

        load_values(0)
        with sp.Fori(0, ROUNDS - 1) as i:
            for c in range(2):
                sp.wait_ge(w_ready, i * 2 + (c + 1))
                load(c, i * 2 + (c + 2))
        sp.wait_ge(w_ready, FM_TILES)
        sp.wait_ge(product_done, FM_TILES - 1)
        load_values(1)

    @block.scalar
    def _(act):
        def split(c, i, wait=None):
            if wait is not None:
                act.wait_ge(loaded[c], i * 16)
                act.wait_ge(product_done, wait)
            nc.scalar.activation(w_hi[c][:], raw[c][:], ACT.Copy).then_inc(w_hi_done, 1)

        def split_values(p):
            act.wait_ge(value_loaded[p], 16)
            nc.scalar.activation(value_hi[p][:], value_raw[p][:], ACT.Copy).then_inc(value_w_hi, 1)

        def keep(c, i):
            act.wait_ge(product_done, i * 2 + (c + 1))
            nc.scalar.activation(nsa.qT[:, bass.ds(i * 2 + c, 1), :].rearrange("p a t -> p (a t)"),
                                 pair(chip.banks[:, 2 * c:2 * c + 2, :]), ACT.Copy).then_inc(kept, 1)

        def keep_to_compress(c, i):
            act.wait_ge(product_done, i * 2 + (c + 1))
            for g in range(2):
                for parity in range(2):
                    last = nc.scalar.activation(nsa.cmp_in[64 * parity:64 * parity + 64, i - Q_ROUNDS, 2 * c + g, :],
                                                pair(chip.banks[64 * g:64 * g + 64, 2 * c:2 * c + 2, :])[:, parity::2], ACT.Copy)
            last.then_inc(kept, 1)

        def keep_keys(c, i):
            act.wait_ge(product_done, i * 2 + (c + 1))
            for g in range(2):
                for rows in range(2):
                    last = nc.scalar.activation(nsa.kT[64 * rows:64 * rows + 64, i - Q_ROUNDS - 2, 2 * c + g, :],
                                                pair(chip.banks[64 * g:64 * g + 64, 2 * c:2 * c + 2, :]), ACT.Copy)
            last.then_inc(kept, 1)

        def keep_values(p, t):
            act.wait_ge(product_done, FM_TILES + NT * p + t + 1)
            source = chip.banks[:, bank_of(t), 0:WIDTHS[p]]
            last = nc.scalar.activation(nsa.v[:, t, KVW * p:KVW * (p + 1)], source[:, 0:KVW], ACT.Copy)
            if p == 1:
                last = nc.scalar.activation(chip.gates[:, t, :], source[:, KVW:], ACT.Sigmoid)
            last.then_inc(kept, 1)

        act.sem_inc(kept, 2)
        split(0, 0)
        split(1, 0)
        with act.Fori(0, Q_ROUNDS) as i:
            keep(0, i)
            split(0, i + 1, wait=i * 2 + 1)
            keep(1, i)
            split(1, i + 1, wait=i * 2 + 2)
        split_values(0)
        for i in range(Q_ROUNDS, ROUNDS):
            for c in range(2):
                if i < Q_ROUNDS + 2:
                    keep_to_compress(c, i)
                else:
                    keep_keys(c, i)
                if i < ROUNDS - 1:
                    split(c, i + 1, wait=i * 2 + c + 1)
        split_values(1)
        for p in range(2):
            for t in range(NT):
                keep_values(p, t)

    @block.gpsimd
    def _(pool):
        with pool.Fori(0, ROUNDS) as i:
            for c in range(2):
                pool.wait_ge(w_hi_done, i * 2 + (c + 1))
                nc.gpsimd.tensor_tensor(w_lo[c][:], raw[c][:], w_hi[c][:].bitcast(F32), ALU.subtract).then_inc(w_ready, 1)
        for p in range(2):
            pool.wait_ge(value_w_hi, p + 1)
            nc.gpsimd.tensor_tensor(value_lo[p][:], value_raw[p][:], value_hi[p][:].bitcast(F32),
                                    ALU.subtract).then_inc(value_w_ready, 1)

    @block.tensor
    def _(pe):
        with pe.Fori(0, ROUNDS) as i:
            for c in range(2):
                pe.wait_ge(w_ready, i * 2 + (c + 1))
                pe.wait_ge(kept, i * 2 + (c + 1))
                feature_major_product(nc, chip, 2 * c, w_hi[c], w_lo[c]).then_inc(product_done, 1)
        for p in range(2):
            pe.wait_ge(value_w_ready, p + 1)
            for t in range(NT):
                if p or t >= 4:
                    pe.wait_ge(kept, 2 + FM_TILES + (t + 1 if p else 0))
                for k in range(KD):
                    for j, (h, w) in enumerate(((hT_hi, value_hi), (hT_hi, value_lo), (hT_lo, value_hi))):
                        last = nc.tensor.matmul(chip.banks[:, bank_of(t), 0:WIDTHS[p]], h[:, k, t * P:(t + 1) * P],
                                                w[p][:, k, :], start=(k == 0 and j == 0), stop=(k == KD - 1 and j == 2))
                last.then_inc(product_done, 1)


def nsa_compressed_stage(nc, chip, ctx, nsa, cmp_pe, cmp_w1, cmp_w2, p_cmp_out):
    sem = lambda n: chip.semaphore(f"cmp_{n}")
    k_loaded, v_loaded, mask_filled, mask_made = (sem(n) for n in ("k_loaded", "v_loaded", "mask_filled", "mask_made"))
    hidden_done, pe_kept, hidden, compressed, kc_ready, vc_hi, vc_ready = (
        sem(n) for n in ("hidden_done", "pe_kept", "hidden", "compressed", "kc_ready", "vc_hi", "vc_ready"))
    scored, biased, topped, expd, masked, inverted, normed, gated = (
        sem(n) for n in ("scored", "biased", "topped", "expd", "masked", "inverted", "normed", "gated"))
    stored = nsa.p_cmp_stored
    kc_zeroed = sem("kc_zeroed")
    importance_zeroed, importance_done, step, chosen, sel_turned, sel_kept = (
        sem(n) for n in ("importance_zeroed", "importance_done", "step", "chosen", "sel_turned", "sel_kept"))
    PAIRS, RING, BATCH = CMP_LEN // 2, 4, 2
    BATCHES = (NT - FIRST_SEL) // BATCH
    ORDER = [(FIRST_SEL + s) % NT for s in range(NT)]

    w1 = chip.at("cmp_w1", H_AT, [P, 2, PAIRS, DH])
    w2 = chip.at("cmp_w2", H_AT + 8, [DH, 2, DH])
    pe_in = chip.at("cmp_pe", H_AT + 8.5, [P, 2, PAIRS])
    pe_out = chip.at("cmp_pe_out", H_AT + 8.75, [DH, 2])
    hid = [chip.at(f"cmp_hid_{c}", H_AT + 9 + j, [DH, GROUPS, NCMP]) for j, c in enumerate("kv")]
    kc = chip.at("cmp_k", H_AT + 48, [P, GROUPS, 2, 64])
    open_bias = chip.at("cmp_open_bias", H_AT + 12, [P, NT, 64])
    open_mask = chip.at("cmp_open_mask", H_AT + 14, [P, 1, 64])
    valid = chip.at("sel_valid", H_AT + 14.5, [P, NT, NSLC])
    invalid_score = chip.at("sel_invalid", H_AT + 15, [P, NT, NSLC])
    forced = chip.at("sel_forced", H_AT + 15.5, [P, NT, NSLC])
    e = [chip.at(f"cmp_e{b}", H_AT + kb, [P, HEADS, 64]) for b, kb in enumerate((24, 28, 32, 41))]
    pg = [chip.at(f"cmp_pg{b}", H_AT + 16 + 4 * b, [P, HEADS, 64]) for b in range(2)]
    negmax, den, inv = (chip.at(f"cmp_{n}", H_AT + 36 + j / 4, [P, RING, HEADS]) for j, n in enumerate(("negmax", "den", "inv")))
    imp = chip.at("cmp_imp", H_AT + 37, [P, NT - FIRST_SEL, GROUPS, 64])
    score, sel = (chip.at(f"cmp_{n}", H_AT + 45 + j, [P, BATCH, GROUPS, NSLC]) for j, n in enumerate(("score", "sel")))
    best = chip.at("cmp_best", H_AT + 47, [P, BATCH, GROUPS, 8])
    banks = chip.banks
    block = ctx.enter_context(nc.Block())

    @block.sync
    def _(sp):
        sp.dma_start(w1[:, 0], cmp_w1[0]).then_inc(k_loaded, 16)
        sp.dma_start(pe_in[:], cmp_pe).then_inc(k_loaded, 16)
        sp.dma_start(w2[:], cmp_w2).then_inc(k_loaded, 16)
        sp.dma_start(w1[:, 1], cmp_w1[1]).then_inc(v_loaded, 16)
        for s, t in enumerate(ORDER):
            sp.wait_ge(gated, s + 1)
            sp.dma_start(p_cmp_out[t * P:(t + 1) * P, :, 0:NCMP], pg[s % 2][:, :, 0:NCMP]).then_inc(stored[s % 2], 16)

    @block.gpsimd
    def _(pool):
        fills = [(open_bias, 0.0), (open_mask, 1.0), (valid, 1.0), (invalid_score, 0.0), (forced, FORCE), (nsa.onehot, 0.0)]
        for m, value in fills:
            nc.gpsimd.memset(m[:], value).then_inc(mask_filled, 1)
        pool.wait_ge(mask_filled, len(fills))
        ended = dict(base=1 - CMP_LEN, pattern=[[P, NT], [-CMP_STRIDE, 64]], channel_multiplier=1)
        begun = dict(base=0, pattern=[[P, NT], [-SLC_LEN, NSLC]], channel_multiplier=1)
        near = dict(base=2 * SLC_LEN - 1, pattern=[[-P, NT], [SLC_LEN, NSLC]], channel_multiplier=-1)
        for m, fill, where in ((open_bias, NEG, ended), (open_mask, 0.0, dict(ended, pattern=[[-CMP_STRIDE, 64]])), (valid, 0.0, begun),
                               (invalid_score, -FORCE, begun), (forced, 0.0, near)):
            nc.gpsimd.affine_select(out=m[:], in_=m[:], compare_op=ALU.is_ge, fill=fill, **where).then_inc(mask_made, 1)
        nc.gpsimd.affine_select(
            out=nsa.onehot[:].rearrange("r g (j k) -> r g j k", k=SLC_LEN),
            in_=nsa.onehot[:].rearrange("r g (j k) -> r g j k", k=SLC_LEN), compare_op=ALU.not_equal, fill=1.0,
            base=0, pattern=[[-NSLC, GROUPS], [-1, NSLC], [0, SLC_LEN]], channel_multiplier=1).then_inc(mask_made, 1)
        pool.wait_ge(mask_made, 6)
        nc.gpsimd.memset(forced[:, :, 0:1], FORCE).then_inc(mask_made, 1)
        for s, t in enumerate(ORDER):
            view = e[s % RING][:, :, 0:NCMP]
            if t == 0:
                pool.wait_ge(expd, s + 1)
                nc.gpsimd.tensor_tensor(view, view, open_mask[:, :, 0:NCMP].broadcast_to([P, HEADS, NCMP]),
                                        ALU.mult).then_inc(masked, 1)
            pool.wait_ge(inverted, s + 1)
            nc.gpsimd.tensor_tensor(view, view, inv[:, s % RING, :].unsqueeze(2).broadcast_to([P, HEADS, NCMP]),
                                    ALU.mult).then_inc(normed, 1)
            pool.wait_ge(normed, s + 1)
            if s >= 2:
                pool.wait_ge(stored[s % 2], 16 * (s // 2))
            gate = chip.gates[:, t, :].rearrange("p (h c) -> p h c", c=3)[:, :, 0:1]
            nc.gpsimd.tensor_tensor(pg[s % 2][:, :, 0:NCMP], view, gate.broadcast_to([P, HEADS, NCMP]),
                                    ALU.mult).then_inc(gated, 1)

    @block.tensor
    def _(pe):
        for j in range(2):
            if j == 0:
                pe.wait_ge(k_loaded, 48)
            else:
                pe.wait_ge(v_loaded, 16)
            for l in range(PAIRS):
                last_pair = l + CMP_STRIDE // 2 * (NCMP - 1) + 1
                nc.tensor.matmul(banks[0:DH, 2 * j, 0:GROUPS * NCMP].rearrange("p (g n) -> p g n", g=GROUPS), w1[:, j, l, :],
                                 nsa.cmp_in[:, j, :, l:last_pair:CMP_STRIDE // 2], start=(l == 0), stop=(l == PAIRS - 1))
                last = nc.tensor.matmul(banks[0:DH, 2 * j + 1, 0:1], w1[:, j, l, :], pe_in[:, j, l:l + 1],
                                        start=(l == 0), stop=(l == PAIRS - 1))
            last.then_inc(hidden_done, 1)
        pe.wait_ge(hidden, 1)
        nc.tensor.matmul(banks[0:DH, 4, 0:GROUPS * NCMP], w2[:, 0, :], hid[0][:].rearrange("p g n -> p (g n)"),
                         start=True, stop=True).then_inc(compressed, 1)
        pe.wait_ge(hidden, 2)
        for g in range(GROUPS):
            last = nc.tensor.matmul(banks[0:NCMP, 5, g * DH:(g + 1) * DH], hid[1][:, g, :], w2[:, 1, :], start=True, stop=True)
        last.then_inc(compressed, 1)
        pe.wait_ge(kc_ready, 2)

        def scores(s):
            b, t = s % 3, ORDER[s]
            if s == 2:
                pe.wait_ge(vc_ready, 1)
            if s >= 3:
                pe.wait_ge(biased, s - 2)
            for j in range(HEADS // 2):
                last = nc.tensor.matmul(banks[:, 2 * b + j // 4, P * (j % 4):P * (j % 4 + 1)],
                                        nsa.qT[:, j, t * P:(t + 1) * P], kc[:, j // 2].rearrange("p a n -> p (a n)"),
                                        start=True, stop=True)
            last.then_inc(scored, 1)

        def turn_selection(batch):
            pe.wait_ge(chosen, batch + 1)
            for x in range(BATCH):
                if batch > 0:
                    pe.wait_ge(sel_kept, (batch - 1) * BATCH + x + 1)
                nc.tensor.transpose(banks[0:GROUPS * NSLC, 6 + x % 2, 0:P], sel[:, x].rearrange("p g j -> p (g j)"),
                                    chip.ident[:]).then_inc(sel_turned, 1)

        for s in range(NT):
            scores(s)
        for batch in range(BATCHES):
            turn_selection(batch)

    @block.scalar
    def _(act):
        for j in range(2):
            act.wait_ge(hidden_done, j + 1)
            nc.scalar.activation(pe_out[:, j:j + 1], banks[0:DH, 2 * j + 1, 0:1], ACT.Copy).then_inc(pe_kept, 1)
            act.wait_ge(pe_kept, j + 1)
            nc.scalar.activation(hid[j][:].rearrange("p g n -> p (g n)"), banks[0:DH, 2 * j, 0:GROUPS * NCMP],
                                 ACT.Gelu_apprx_tanh, bias=pe_out[:, j:j + 1]).then_inc(hidden, 1)
        act.wait_ge(compressed, 2)
        value = banks[0:NCMP, 5, 0:KVW].rearrange("n (g d) -> n g d", d=DH)
        nc.scalar.activation(nsa.vc[:, :, 0:DH], value, ACT.Copy).then_inc(vc_hi, 1)

        def keep_selection(batch):
            for x in range(BATCH):
                t = FIRST_SEL + batch * BATCH + x
                act.wait_ge(sel_turned, batch * BATCH + x + 1)
                nc.scalar.activation(nsa.selT[:, t * P:(t + 1) * P], banks[0:GROUPS * NSLC, 6 + x % 2, 0:P],
                                     ACT.Copy).then_inc(sel_kept, 1)

        for s in range(NT):
            b = s % RING
            act.wait_ge(topped, s + 1)
            for h in range(HEADS):
                view = e[b][:, h, 0:NCMP]
                last = nc.scalar.activation(view, view, ACT.Exp, bias=negmax[:, b, h:h + 1], accum_out=den[:, b, h:h + 1])
            last.then_inc(expd, 1)
        for batch in range(BATCHES):
            keep_selection(batch)

    @block.vector
    def _(dve):
        steps = [0]

        def then(instruction):
            steps[0] += 1
            instruction.then_inc(step, 1)
            dve.wait_ge(step, steps[0])

        nc.vector.memset(imp[:], 0.0).then_inc(importance_zeroed, 1)
        nc.vector.memset(kc[:], 0.0).then_inc(kc_zeroed, 1)
        dve.wait_ge(kc_zeroed, 1)
        dve.wait_ge(compressed, 1)
        for half in range(2):
            nc.vector.tensor_copy(kc[64 * half:64 * half + 64, :, half, 0:NCMP],
                                  banks[0:DH, 4, 0:GROUPS * NCMP].rearrange("p (g n) -> p g n", n=NCMP)).then_inc(kc_ready, 1)
        dve.wait_ge(vc_hi, 1)
        value = banks[0:NCMP, 5, 0:KVW].rearrange("n (g d) -> n g d", d=DH)
        nc.vector.tensor_tensor(nsa.vc[:, :, DH:P], value, nsa.vc[:, :, 0:DH].bitcast(F32), ALU.subtract).then_inc(vc_ready, 1)
        dve.wait_ge(mask_made, 7)
        dve.wait_ge(importance_zeroed, 1)

        def shift(s):
            b, t = s % RING, ORDER[s]
            dve.wait_ge(scored, s + 1)
            if s >= RING:
                dve.wait_ge(gated, s - RING + 1)
                if s - RING < NT - FIRST_SEL:
                    dve.wait_ge(importance_done, s - RING + 1)
            for a in range(2):
                last = nc.vector.scalar_tensor_tensor(
                    out=e[b][:, a * HEADS // 2:(a + 1) * HEADS // 2, 0:NCMP],
                    in0=banks[:, 2 * (s % 3) + a, :].rearrange("p (h n) -> p h n", n=64)[:, :, 0:NCMP],
                    scalar=SCALE, in1=open_bias[:, t:t + 1, 0:NCMP].broadcast_to([P, HEADS // 2, NCMP]),
                    op0=ALU.mult, op1=ALU.add)
            last.then_inc(biased, 1)
            dve.wait_ge(biased, s + 1)
            nc.vector.tensor_reduce(negmax[:, b, :], e[b][:, :, 0:NCMP], AX.X, ALU.max, negate=True).then_inc(topped, 1)

        def invert(s):
            b = s % RING
            if ORDER[s] == 0:
                dve.wait_ge(masked, 1)
                then(nc.vector.tensor_reduce(den[:, b, :], e[b][:, :, 0:NCMP], AX.X, ALU.add))
            else:
                dve.wait_ge(expd, s + 1)
            then(nc.vector.tensor_scalar(den[:, b, :], den[:, b, :], 1e-30, None, ALU.max))
            nc.vector.reciprocal(inv[:, b, :], den[:, b, :]).then_inc(inverted, 1)

        def weigh(s):
            dve.wait_ge(normed, s + 1)
            nc.vector.tensor_reduce(imp[:, s, :, 0:NCMP], e[s % RING][:, :, 0:NCMP].rearrange("p (g h) n -> p g n h", g=GROUPS),
                                    AX.X, ALU.add).then_inc(importance_done, 1)

        def select(batch):
            mine = slice(batch * BATCH, batch * BATCH + BATCH)
            tiles = slice(FIRST_SEL + batch * BATCH, FIRST_SEL + batch * BATCH + BATCH)
            dve.wait_ge(importance_done, batch * BATCH + BATCH)
            quads = imp[:, mine].rearrange("p t g (j c) -> p (t g) j c", c=4)
            s = score[:].rearrange("p t g j -> p (t g) j")
            then(nc.vector.tensor_tensor(s, quads[:, :, :, 0], quads[:, :, :, 1], ALU.add))
            then(nc.vector.tensor_tensor(s, s, quads[:, :, :, 2], ALU.add))
            then(nc.vector.tensor_scalar(quads[:, :, :, 3], quads[:, :, :, 3], 0.5, None, ALU.mult))
            then(nc.vector.tensor_tensor(s, s, quads[:, :, :, 3], ALU.add))
            then(nc.vector.tensor_tensor(s[:, :, 1:NSLC], s[:, :, 1:NSLC], quads[:, :, 0:NSLC - 1, 3], ALU.add))
            for m, op in ((forced, ALU.add), (valid, ALU.mult), (invalid_score, ALU.add)):
                then(nc.vector.tensor_tensor(score[:], score[:], m[:, tiles, :].unsqueeze(2).broadcast_to([P, BATCH, GROUPS, NSLC]), op))
            for x in range(BATCH):
                for g in range(GROUPS):
                    last = nc.vector.max(best[:, x, g, :], score[:, x, g, :])
            then(last)
            if batch:
                dve.wait_ge(sel_turned, BATCH * batch)
            for x in range(BATCH):
                for g in range(GROUPS):
                    last = nc.vector.match_replace(sel[:, x, g, :], best[:, x, g, :], score[:, x, g, :], 1e30)
            then(last)
            nc.vector.tensor_scalar(sel[:], sel[:], 1e29, NEG, ALU.is_lt, ALU.mult).then_inc(chosen, 1)

        for s in range(NT + 2):
            if s < NT:
                shift(s)
            if 0 <= s - 1 < NT:
                invert(s - 1)
            if 0 <= s - 2 < NT - FIRST_SEL:
                weigh(s - 2)
            if s >= 4 and (s - 3) % BATCH == 0 and (s - 3) // BATCH <= BATCHES:
                select((s - 3) // BATCH - 1)


def attention_plan():
    jobs = [(branch, i) for i in range(NT) for branch in (SLC, WIN)]
    tiles, n = [], 0
    for branch, i in jobs:
        keys = list(range(0, i + 1)) + [None] if branch == SLC else list(range(max(0, i - WINDOW // P), i + 1))
        tiles.append([(n + x, key) for x, key in enumerate(keys)])
        n += len(keys)
    return jobs, tiles, n


def nsa_attention_stage(nc, chip, ctx, nsa, p_cmp_in, oT):
    sem = lambda n: chip.semaphore(f"att_{n}")
    jobs, tiles, TILES = attention_plan()
    JOBS, HEAD_JOBS = len(jobs), len(jobs) * HPG
    PARTS, PART_AT = ((0, 2), (2, 4), (4, NT)), (None, 3, 24)
    need = {2 * first: p for p, (first, _) in enumerate(PARTS)}
    LAG = 2
    q_hi, q_lo, k_hi, k_lo, v_hi, v_lo, group_copied = (
        sem(n) for n in ("q_hi", "q_lo", "k_hi", "k_lo", "v_hi", "v_lo", "group_copied"))
    scored, maxed, expd, inverted, scaled = (sem(n) for n in ("scored", "maxed", "expd", "inverted", "scaled"))
    turned, hi_done, lo_done, multiplied = (sem(n) for n in ("turned", "hi_done", "lo_done", "multiplied"))
    pool_go, pe_go = sem("pool_go"), sem("pe_go")
    pc_loaded, upper_kept, folded = [sem(f"pc_loaded{b}") for b in range(2)], sem("upper_kept"), sem("folded")

    qS = chip.at("att_q", 36, [P, HPG, T], F32R)
    kS_hi = chip.at("att_k_hi", 52, [P, 2, T], F32R)
    kS_lo = chip.at("att_k_lo", 60, [P, 2, T], F32R)
    vS = chip.at("att_v", 100, [P, 2, NT, P], F32R)
    pT_hi = [chip.at(f"att_pT_hi{b}", kb, [P, HALF], F32R) for b, kb in enumerate((108, 110, 205.5))]
    pT_lo = [chip.at(f"att_pT_lo{b}", 112 + 2 * b, [P, HALF], F32R) for b in range(2)]
    vc = chip.at("att_vc", 176, [NCMP, P], F32R)
    gates = chip.at("att_gates", 176.5, [P, NT, HPG, 3])
    prob = [chip.at("att_p_slc", 177, [P, HPG, T]), chip.at("att_p_win", 193, [P, HPG, WINDOW + P])]
    pc = [chip.at(f"att_p_cmp{b}", 203 + b, [P, HPG, 64]) for b in range(2)]
    negmax, den, inv = (chip.at(f"att_{n}", 205 + j / 8, [P, 8]) for j, n in enumerate(("negmax", "den", "inv")))
    upper = chip.at("att_upper", VC_AT, [P, HALF])[64:P]
    banks = chip.banks
    block = ctx.enter_context(nc.Block())

    def key_range(branch, i):
        return (0 if branch == SLC else max(0, i - WINDOW // P)) * P, (i + 1) * P

    NARROW = HPG * len([1 for branch, i in jobs if (i + 1) * P <= HALF])

    def first_bank(m):
        return m % 4 if m < NARROW else 2 * (m % 2)

    def slot(m):
        return banks[:, first_bank(m):first_bank(m) + (1 if m < NARROW else 2), :]

    def slot_user(m):
        if m < NARROW:
            return max(m - 4, -1)
        return m - 2 if m - 2 >= NARROW else NARROW - 3 + 2 * (m - NARROW)

    def beside(J, h):
        if J == 0 or h == 0:
            return []
        n = len(tiles[J - 1])
        return tiles[J - 1][n * (h - 1) // (HPG - 1):n * h // (HPG - 1)]

    def walk(score, soften, tile):
        made = 0
        for m in range(HEAD_JOBS):
            J, h = divmod(m, HPG)
            while made < min(max(m + 2, min(m + 4, NARROW)), HEAD_JOBS):
                score(*divmod(made, HPG))
                made += 1
            soften(J, h)
            for n, key in beside(J, h):
                tile(J - 1, n, key)
        for n, key in tiles[JOBS - 1]:
            tile(JOBS - 1, n, key)

    def folds_before(J, n):
        branch, i = jobs[J]
        return i - 1 if branch == SLC and i >= 1 and n == tiles[J][0][0] + LAG else None

    def nothing(*_):
        pass

    def heads(g, m):
        return g * HEAD_JOBS + (m + 2)

    def keys(g, n):
        return g * TILES + (n + 2)

    def queries(g, i):
        return g * NT + (i + 2)

    @block.sync
    def _(sp):
        for b in range(2):
            sp.wait_ge(nsa.p_cmp_stored[b], 16 * (NT // 2))
        with sp.Fori(0, GROUPS) as g:
            for i in range(NT):
                before = tiles[2 * (i - 2)][-1][0] if i >= 2 else -1
                sp.wait_ge(turned, keys(g, before))
                sp.dma_start(pc[i % 2][:, :, 0:NCMP], p_cmp_in[i * P:(i + 1) * P, bass.ds(g * HPG, HPG), 0:NCMP]
                             ).then_inc(pc_loaded[i % 2], 16)

    @block.scalar
    def _(act):
        for count in (expd, hi_done, upper_kept):
            act.sem_inc(count, 1)
        with act.Fori(0, GROUPS) as g:
            act.wait_ge(scored, heads(g, -1))
            act.wait_ge(multiplied, keys(g, -1))

            def high_parts(p):
                tokens, tiles_of = slice(PARTS[p][0] * P, PARTS[p][1] * P), slice(*PARTS[p])

                def round_q(a):
                    rows = slice(64 * a, 64 * a + 64)
                    nc.scalar.activation(qS[rows, a:HPG:2, tokens], nsa.qT[rows, bass.ds(g * 2, 2), tokens],
                                         ACT.Copy, scale=SCALE).then_inc(q_hi, 1)

                def round_k():
                    nc.scalar.activation(kS_hi[:, :, tokens], nsa.kT[:, :, bass.ds(g, 1), tokens].rearrange("p b g t -> p b (g t)"),
                                         ACT.Copy).then_inc(k_hi, 1)

                def round_v():
                    for b in range(2):
                        last = nc.scalar.activation(vS[:, b, tiles_of, 0:DH], nsa.v[:, tiles_of, bass.ds(g * DH + b * KVW, DH)], ACT.Copy)
                    last.then_inc(v_hi, 1)

                return [lambda: round_q(0), round_k, lambda: round_q(1), round_v]

            for step in high_parts(0):
                step()
            beside_head = {PART_AT[p] + x: step for p in range(1, len(PARTS)) for x, step in enumerate(high_parts(p))}

            def soften(J, h):
                branch, i = jobs[J]
                m = J * HPG + h
                lo, hi = key_range(branch, i)
                act.wait_ge(maxed, heads(g, m))
                if J >= 2:
                    act.wait_ge(turned, keys(g, tiles[J - 2][-1][0]))
                nc.scalar.activation(prob[branch][:, h, 0:hi - lo], pair(slot(m))[:, 0:hi - lo], ACT.Exp,
                                     bias=negmax[:, m % 8:m % 8 + 1], accum_out=den[:, m % 8:m % 8 + 1]).then_inc(expd, 1)
                if m in beside_head:
                    beside_head[m]()

            def tile(J, n, key):
                rows = P if key is not None else NCMP
                act.wait_ge(turned, keys(g, n))
                act.wait_ge(multiplied, keys(g, max(n - 3, -1)))
                nc.scalar.activation(pT_hi[n % 3][0:rows, :], banks[0:rows, 4 + n % 2, :], ACT.Copy).then_inc(hi_done, 1)
                if folds_before(J, n) is not None:
                    keep_upper(folds_before(J, n))

            def keep_upper(i):
                act.wait_ge(multiplied, keys(g, tiles[2 * i + 1][-1][0]))
                act.wait_ge(folded, queries(g, i - 1))
                nc.scalar.activation(upper, banks[64:P, 6 + i % 2, :], ACT.Copy).then_inc(upper_kept, 1)

            walk(nothing, soften, tile)
            keep_upper(NT - 1)

    @block.gpsimd
    def _(pool):
        pool.sem_inc(scaled, 1)
        with pool.Fori(0, GROUPS) as g:
            def low_k(p):
                tokens = slice(PARTS[p][0] * P, PARTS[p][1] * P)
                pool.wait_ge(k_hi, g * len(PARTS) + (p + 1))
                nc.gpsimd.tensor_tensor(kS_lo[:, :, tokens], nsa.kT[:, :, bass.ds(g, 1), tokens].rearrange("p b g t -> p b (g t)"),
                                        kS_hi[:, :, tokens].bitcast(F32), ALU.subtract).then_inc(k_lo, 1)

            low_k(0)
            pool.wait_ge(group_copied, g * 2 + 2)
            for J, (branch, i) in enumerate(jobs):
                lo, hi = key_range(branch, i)
                for h in range(HPG):
                    m = J * HPG + h
                    pool.wait_ge(inverted, heads(g, m))
                    pool.sem_inc(pool_go, 1)
                    at = prob[branch][:, h, 0:hi - lo]
                    nc.gpsimd.tensor_scalar(at, at, inv[:, m % 8:m % 8 + 1], gates[:, i, h, 1 + branch:2 + branch],
                                            ALU.mult, ALU.mult).then_inc(scaled, 1)
                    if m - 1 in PART_AT:
                        low_k(PART_AT.index(m - 1))

    @block.vector
    def _(dve):
        for count in (maxed, inverted, lo_done, folded):
            dve.sem_inc(count, 1)
        with dve.Fori(0, GROUPS) as g:
            dve.wait_ge(scaled, heads(g, -1))
            nc.vector.tensor_copy(gates[:].rearrange("p t h c -> p t (h c)"),
                                  chip.gates[:, :, bass.ds(g * (3 * HPG), 3 * HPG)]).then_inc(group_copied, 1)
            dve.wait_ge(multiplied, keys(g, -1))
            nc.vector.tensor_copy(vc[:], nsa.vc[:, bass.ds(g, 1), :].rearrange("n g d -> n (g d)").bitcast(F32)).then_inc(group_copied, 1)

            def low_parts(p):
                tokens, tiles_of = slice(PARTS[p][0] * P, PARTS[p][1] * P), slice(*PARTS[p])

                def low_q(a):
                    own, other = slice(64 * a, 64 * a + 64), slice(64 - 64 * a, P - 64 * a)
                    dve.wait_ge(q_hi, (g * len(PARTS) + p) * 2 + (a + 1))
                    nc.vector.scalar_tensor_tensor(
                        out=qS[other, a:HPG:2, tokens], in0=nsa.qT[own, bass.ds(g * 2, 2), tokens], scalar=SCALE,
                        in1=qS[own, a:HPG:2, tokens].bitcast(F32), op0=ALU.mult, op1=ALU.subtract).then_inc(q_lo, 1)

                def low_v():
                    dve.wait_ge(v_hi, g * len(PARTS) + (p + 1))
                    for b in range(2):
                        last = nc.vector.tensor_tensor(vS[:, b, tiles_of, DH:P], nsa.v[:, tiles_of, bass.ds(g * DH + b * KVW, DH)],
                                                       vS[:, b, tiles_of, 0:DH].bitcast(F32), ALU.subtract)
                    last.then_inc(v_lo, 1)

                return [lambda: low_q(0), lambda: low_q(1), low_v]

            for step in low_parts(0):
                step()
            beside_head = {PART_AT[p] + 2 + x: step for p in range(1, len(PARTS)) for x, step in enumerate(low_parts(p))}

            def invert(J, h):
                m = J * HPG + h
                dve.wait_ge(expd, heads(g, m))
                if m >= 8:
                    dve.wait_ge(scaled, heads(g, m - 8))
                nc.vector.reciprocal(inv[:, m % 8:m % 8 + 1], den[:, m % 8:m % 8 + 1]).then_inc(inverted, 1)
                if m in beside_head:
                    beside_head[m]()

            def largest(J, h):
                branch, i = jobs[J]
                m = J * HPG + h
                lo, hi = key_range(branch, i)
                dve.wait_ge(scored, heads(g, m))
                nc.vector.tensor_reduce(negmax[:, m % 8:m % 8 + 1], pair(slot(m))[:, 0:hi - lo], AX.X, ALU.max,
                                        negate=True).then_inc(maxed, 1)

            def tile(J, n, key):
                rows = P if key is not None else NCMP
                dve.wait_ge(hi_done, keys(g, n))
                dve.wait_ge(multiplied, keys(g, max(n - 2, -1)))
                nc.vector.tensor_tensor(pT_lo[n % 2][0:rows, :], banks[0:rows, 4 + n % 2, :],
                                        pT_hi[n % 3][0:rows, :].bitcast(F32), ALU.subtract).then_inc(lo_done, 1)
                if folds_before(J, n) is not None:
                    fold(folds_before(J, n))

            def fold(i):
                dve.wait_ge(upper_kept, queries(g, i))
                for a in range(2):
                    pick = lambda ap: ap.rearrange("d (h q) -> d h q", q=P)[:, a:HPG:2, :]
                    last = nc.vector.tensor_tensor(oT[64 * a:64 * a + 64, bass.ds(g * 2, 2), i * P:(i + 1) * P],
                                                   pick(banks[0:64, 6 + i % 2, :]), pick(upper), ALU.add)
                last.then_inc(folded, 1)

            walk(largest, invert, tile)
            fold(NT - 1)

    @block.tensor
    def _(pe):
        for count in (scored, turned, multiplied):
            pe.sem_inc(count, 1)
        with pe.Fori(0, GROUPS) as g:
            pe.wait_ge(group_copied, g * 2 + 2)
            pending = []

            def score(J, h):
                branch, i = jobs[J]
                m = J * HPG + h
                lo, hi = key_range(branch, i)
                pe.wait_ge(expd, heads(g, slot_user(m)))
                choice = branch == SLC and i >= FIRST_SEL
                if J - 1 in need:
                    pe.wait_ge(v_lo, g * len(PARTS) + (need[J - 1] + 1))
                if J in need:
                    part = need[J]
                    pe.wait_ge(q_lo, (g * len(PARTS) + part) * 2 + 2)
                    pe.wait_ge(k_lo, g * len(PARTS) + (part + 1))
                q = qS[:, h, i * P:(i + 1) * P]
                for c, at in enumerate(range(lo, hi, HALF)):
                    end = min(at + HALF, hi)
                    out = banks[:, first_bank(m) + c, 0:end - at]
                    diagonal = end == hi
                    oldest = branch == WIN and c == 0 and i >= WINDOW // P
                    nc.tensor.matmul(out, q, kS_hi[:, branch, at:end], start=True, stop=False)
                    last = nc.tensor.matmul(out, q, kS_lo[:, branch, at:end], start=False,
                                            stop=not (diagonal or oldest or choice))
                    if choice and at < i * P:
                        width = min(end, i * P) - at
                        last = nc.tensor.matmul(out[:, 0:width], nsa.selT[:, i * P:(i + 1) * P],
                                                nsa.onehot[:, bass.ds(g, 1), at:at + width].rearrange("r g k -> r (g k)"),
                                                start=False, stop=not diagonal)
                    if oldest:
                        last = nc.tensor.matmul(out[:, 0:P], chip.ident_bf[:], chip.too_old[:], start=False, stop=not diagonal)
                    if diagonal:
                        last = nc.tensor.matmul(out[:, end - at - P:], chip.ident_bf[:], chip.causal[:], start=False, stop=True)
                last.then_inc(scored, 1)

            def values(J, n, key):
                branch, i = jobs[J]
                rows = P if key is not None else NCMP
                if n == tiles[2 * i][0][0]:
                    pe.wait_ge(folded, queries(g, max(i - 2, -1)))
                pe.wait_ge(hi_done, keys(g, n))
                pe.wait_ge(lo_done, keys(g, n))
                v = vS[:, branch, key, :] if key is not None else vc[:]
                out = banks[:, 6 + i % 2, :]
                nc.tensor.matmul(out, v, pT_hi[n % 3][0:rows, :], start=(n == tiles[2 * i][0][0]), stop=False)
                nc.tensor.matmul(out, v, pT_lo[n % 2][0:rows, :], start=False,
                                 stop=(n == tiles[2 * i + 1][-1][0])).then_inc(multiplied, 1)

            def tile(J, n, key):
                branch, i = jobs[J]
                lo, _ = key_range(branch, i)
                rows = P if key is not None else NCMP
                if key is None:
                    pe.wait_ge(pc_loaded[i % 2], g * (8 * NT) + 16 * (i // 2 + 1))
                elif n == tiles[J][0][0]:
                    pe.wait_ge(scaled, heads(g, (J + 1) * HPG - 1))
                pe.wait_ge(lo_done, keys(g, max(n - 2, -1)))
                if key is None:
                    pe.sem_inc(pe_go, 1)
                for h in range(HPG):
                    source = pc[i % 2][:, h, 0:NCMP] if key is None else prob[branch][:, h, key * P - lo:(key + 1) * P - lo]
                    last = nc.tensor.transpose(banks[0:rows, 4 + n % 2, h * P:(h + 1) * P], source, chip.ident[:])
                last.then_inc(turned, 1)
                pending.append((J, n, key))
                if len(pending) > LAG:
                    values(*pending.pop(0))

            walk(score, nothing, tile)
            for tile_left in pending:
                values(*tile_left)


def nsa_output_stage(nc, chip, ctx, oT, w_out, norm):
    sem = lambda n: chip.semaphore(f"out_{n}")
    loaded = [sem(f"loaded{b}") for b in range(2)]
    w_hi_done, w_ready, o_hi_done, o_ready, done, kept = (
        sem(n) for n in ("w_hi_done", "w_ready", "o_hi_done", "o_ready", "done", "kept"))
    o_hi = chip.at("out_o_hi", 100, [P, KD, T], F32R)
    o_lo = chip.at("out_o_lo", 4, [P, KD, T], F32R)
    w_hi = chip.at("out_w_hi", 36, [P, KD, D], F32R)
    w_lo = chip.at("out_w_lo", 164, [P, KD, D], F32R)
    raw = [chip.at(f"out_raw{b}", 196 + 4 * b, [P, D]) for b in range(2)]
    norm = Norm(nc, chip, y_done=(kept, 0), x_at=132, rest_at=196, lag=NT, coming_after=(done, NT), **norm)
    block = ctx.enter_context(nc.Block())

    @block.sync
    def _(sp):
        for k in range(KD):
            if k >= 2:
                sp.wait_ge(w_ready, k - 1)
            sp.dma_start(raw[k % 2][:], w_out[k * P:(k + 1) * P, :]).then_inc(loaded[k % 2], 16)
        sp.wait_ge(w_ready, KD)
        norm.sync(sp)

    @block.scalar
    def _(act):
        for k in range(KD):
            nc.scalar.activation(o_hi[:, k, :], oT[:, k, :], ACT.Copy).then_inc(o_hi_done, 1)
            act.wait_ge(loaded[k % 2], 16 * (k // 2 + 1))
            nc.scalar.activation(w_hi[:, k, :], raw[k % 2][:], ACT.Copy).then_inc(w_hi_done, 1)

        def keep(t):
            act.wait_ge(done, t + 1)
            b = 2 * (t % 4)
            nc.scalar.activation(chip.y[:, t, :], pair(chip.banks[:, b:b + 2, :]), ACT.Copy).then_inc(kept, 1)

        norm.scalar(act, before=keep)

    @block.gpsimd
    def _(pool):
        for k in range(KD):
            pool.wait_ge(w_hi_done, k + 1)
            nc.gpsimd.tensor_tensor(w_lo[:, k, :], raw[k % 2][:], w_hi[:, k, :].bitcast(F32), ALU.subtract).then_inc(w_ready, 1)
        norm.gpsimd(pool)

    @block.vector
    def _(dve):
        for k in range(KD):
            dve.wait_ge(o_hi_done, k + 1)
            nc.vector.tensor_tensor(o_lo[:, k, :], oT[:, k, :], o_hi[:, k, :].bitcast(F32), ALU.subtract).then_inc(o_ready, 1)
        norm.vector(dve)

    @block.tensor
    def _(pe):
        def product(t, k):
            b = 2 * (t % 4)
            for j, (o, w) in enumerate(((o_hi, w_hi), (o_hi, w_lo), (o_lo, w_hi))):
                for half in range(2):
                    last = nc.tensor.matmul(chip.banks[:, b + half, :], o[:, k, t * P:(t + 1) * P],
                                            w[:, k, half * HALF:(half + 1) * HALF],
                                            start=(k == 0 and j == 0), stop=(k == KD - 1 and j == 2))
            if k == KD - 1:
                last.then_inc(done, 1)

        for k in range(KD):
            pe.wait_ge(w_ready, k + 1)
            pe.wait_ge(o_ready, k + 1)
            for t in range(4):
                product(t, k)
        for t in range(4, NT):
            pe.wait_ge(kept, t - 3)
            for k in range(KD):
                product(t, k)
        pe.wait_ge(kept, NT - 2)
        norm.tensor(pe)


def build(nc, a, out):
    scratch = lambda name, shape: nc.dram_tensor(name, shape, F32, kind="Internal").ap()
    x_mid = [scratch(f"x_mid{j}", (T, D)) for j in range(3)]
    p_cmp = scratch("p_cmp", (T, HEADS, 64))
    v_normed = scratch("v_normed", (T, E))
    gain = lambda layer, j: a["norm_gains"][4 * layer + j:4 * layer + j + 1, :]
    with ExitStack() as whole:
        chip = Chip(nc, whole)
        nsa = NsaState(chip)
        oT = chip.at("oT", 4, [P, KD, T])

        def stage(build_stage, *args, **kwargs):
            with ExitStack() as ctx:
                build_stage(nc, chip, ctx, *args, **kwargs)
            chip.end_stage()

        stage(first_norm_stage, dict(tag="norm0", x_in=a["x"], pre_gain=gain(0, 0)), a["nsa_w_fm"])
        stage(nsa_projection_stage, nsa, a["nsa_w_fm"], a["nsa_w_tok"])
        stage(nsa_compressed_stage, nsa, a["cmp_pe"], a["cmp_w1"], a["cmp_w2"], p_cmp)
        stage(nsa_attention_stage, nsa, p_cmp, oT)
        stage(nsa_output_stage, oT, a["nsa_w_out"],
              norm=dict(tag="norm1", x_in=a["x"], x_out=x_mid[0], post_gain=gain(0, 1), pre_gain=gain(0, 2),
                        coming=ffn_coming(chip, a["ffn_w_up"][0])))
        stage(ffn_stage, "ffn0", a["ffn_w_up"][0], a["ffn_w_down"][0], a["ffn_conv"][0],
              norm=dict(tag="norm2", x_in=x_mid[0], x_out=x_mid[1], post_gain=gain(0, 3), pre_gain=gain(1, 0),
                        coming=gmlp_v_coming(chip, a["sg_w_v"])))
        stage(gmlp_v_stage, a["sg_w_v"], v_normed, a["sg_w_u"], a["sg_w_sp"])
        stage(gmlp_stage, a["sg_w_u"], a["sg_w_out"], v_normed, a["sg_ln_g"], a["sg_ln_b"], a["sg_b_sp"],
              norm=dict(tag="norm3", x_in=x_mid[1], x_out=x_mid[2], post_gain=gain(1, 1), pre_gain=gain(1, 2),
                        coming=ffn_coming(chip, a["ffn_w_up"][1])))
        stage(ffn_stage, "ffn1", a["ffn_w_up"][1], a["ffn_w_down"][1], a["ffn_conv"][1],
              norm=dict(tag="norm4", x_in=x_mid[2], x_out=out, post_gain=gain(1, 3)))


def lay_out(i):
    import numpy as np

    i = {k: np.asarray(v) for k, v in i.items()}
    flat = np.ascontiguousarray
    w_in = i["nsa_w_in"][0]
    q, kc, vc, ks, vs, kw, vw, gl = np.split(w_in, [HEADS * DH + k * KVW for k in range(7)], axis=1)
    piece = lambda w: w.reshape(KD, P, -1).transpose(1, 0, 2).reshape(P, -1)
    columns = lambda w: flat(w.reshape(KD, P, -1, P).transpose(2, 1, 0, 3).reshape(-1, P, KD * P))
    rows2 = lambda w: flat(w.reshape(-1, 2, P, D).transpose(0, 2, 1, 3).reshape(-1, P, 2 * D))
    sg_in = i["sg_w_in"][0]
    layers = i["ffn_w_up"].shape[0]
    conv = np.concatenate([i["ffn_conv_w"], i["ffn_conv_b"][:, None]], axis=1)
    return {
        "x": i["x"][0],
        "norm_gains": i["norm_gains"].reshape(-1, D),
        "nsa_w_fm": columns(np.concatenate([q, kc, vc, ks, kw], axis=1)),
        "nsa_w_tok": flat(np.concatenate([piece(vs), piece(np.concatenate([vw, gl], axis=1))], axis=1)),
        "cmp_pe": flat(i["nsa_cmp_pe"][0].reshape(2, CMP_LEN // 2, P).transpose(2, 0, 1)),
        "cmp_w1": flat(i["nsa_cmp_w1"][0].reshape(2, CMP_LEN // 2, P, DH).transpose(0, 2, 1, 3)),
        "cmp_w2": flat(i["nsa_cmp_w2"][0].transpose(1, 0, 2)),
        "nsa_w_out": i["nsa_w_out"][0],
        "sg_w_v": flat(sg_in[:, E:].reshape(4, 2, P, 4, HALF).transpose(3, 0, 2, 1, 4).reshape(16, P, 2 * HALF)),
        "sg_w_u": columns(sg_in[:, :E]),
        "sg_ln_g": flat(i["sg_ln_g"][0].reshape(KE, P).T),
        "sg_ln_b": i["sg_ln_b"][0].reshape(1, E),
        "sg_w_sp": flat(i["sg_w_sp"][0].transpose(2, 0, 1).reshape(P, KE * P)),
        "sg_b_sp": i["sg_b_sp"][0].reshape(1, KE * P),
        "sg_w_out": rows2(i["sg_w_out"][0]),
        "ffn_w_up": flat(i["ffn_w_up"].reshape(layers, KD, P, 2, KF, P).transpose(0, 4, 2, 3, 1, 5).reshape(layers, KF, P, -1)),
        "ffn_w_down": np.stack([rows2(w) for w in i["ffn_w_down"]]),
        "ffn_conv": flat(conv.reshape(layers, 4, 2, KF, P).transpose(0, 4, 3, 2, 1)),
    }


def kernel(**inputs):
    import numpy as np
    import concourse.bacc as bacc
    from concourse.bass_utils import run_bass_kernel_spmd

    nc = bacc.Bacc("TRN2", target_bir_lowering=False, num_devices=1)
    arrays = {f"in_{name}": np.ascontiguousarray(v) for name, v in lay_out(inputs).items()}
    args = {name[3:]: nc.dram_tensor(name, v.shape, mybir.dt.from_np(v.dtype), kind="ExternalInput").ap()
            for name, v in arrays.items()}
    out = nc.dram_tensor("out", (T, D), F32, kind="ExternalOutput").ap()
    build(nc, args, out)
    result = run_bass_kernel_spmd(nc, [arrays], core_ids=[0])
    return result.results[0]["out"].reshape(1, T, D)
```
